# Optimizing a Trainium2 kernel written in Bass

```python
import jax, jax.numpy as jnp
from jax import lax
import numpy as np

D_MODEL = 1024
BATCH = 1
SEQ = 256
DEPTH = 2
DEC_BATCH = 8
DEC_SEQ = 4
PAST_LEN = 1024
PAGE_SIZE = 128

HEAD_DIM = 64
N_HEADS = D_MODEL // HEAD_DIM
H_SB = N_HEADS // 2
H_MOBA = N_HEADS - H_SB
MOBA_BLOCK = 256
MOBA_TOPK = 3
NSA_HQ = N_HEADS
NSA_HKV = 4
NSA_GROUP = NSA_HQ // NSA_HKV
CMP_BLOCK = 32
CMP_STRIDE = 16
CMP_HIDDEN = 256
SLC_BLOCK = 64
SLC_TOPK = 16
WINDOW = 512
D_FF = ((8 * D_MODEL + 3 * 256 - 1) // (3 * 256)) * 256
ROPE_THETA = 10000.0
NORM_EPS = 1e-6
SB_QBLOCK = 128
GATHER_QBLOCK = 16
N_EVEN = (DEPTH + 1) // 2
N_ODD = DEPTH // 2
EVEN_IN = 3 * N_HEADS * HEAD_DIM
ODD_IN = NSA_HQ * HEAD_DIM + 6 * NSA_HKV * HEAD_DIM + 3 * NSA_HQ
NEG_BIG = -1e30
FORCE_SCORE = 1e9

kernel_name = 'hybrid_stickbreak_moba_nsa_step'

def rms_norm(x, g):
    xf = x.astype(jnp.float32)
    y = xf * lax.rsqrt(jnp.mean(xf * xf, axis=-1, keepdims=True) + NORM_EPS)
    return (y * g.astype(jnp.float32)).astype(x.dtype)

def rope(x, pos):
    half = HEAD_DIM // 2
    inv = jnp.power(ROPE_THETA, -jnp.arange(half, dtype=jnp.float32) / half)
    ang = pos.astype(jnp.float32)[:, None] * inv[None, :]
    cos = jnp.cos(ang)[:, None, :]
    sin = jnp.sin(ang)[:, None, :]
    xf = x.astype(jnp.float32)
    x1, x2 = xf[..., :half], xf[..., half:]
    return jnp.concatenate([x1 * cos - x2 * sin, x2 * cos + x1 * sin], axis=-1).astype(x.dtype)

def masked_softmax(s, mask):
    s = jnp.where(mask, s, NEG_BIG)
    m = jnp.max(s, axis=-1, keepdims=True)
    p = jnp.where(mask, jnp.exp(s - m), 0.0)
    return p / jnp.maximum(jnp.sum(p, axis=-1, keepdims=True), 1e-30)

def swiglu(x, w_gu, w_down):
    g, u = jnp.split(x @ w_gu, 2, axis=-1)
    return (jax.nn.silu(g) * u) @ w_down

def append_rows(past, new, multiple):
    parts = [new] if past is None else [past, new.astype(past.dtype)]
    total = sum(p.shape[1] for p in parts)
    pad = -total % multiple
    if pad:
        parts.append(jnp.zeros((new.shape[0], pad) + new.shape[2:], parts[0].dtype))
    return jnp.concatenate(parts, axis=1) if len(parts) > 1 else parts[0]

def map_query_chunks(fn, xs, block):
    nq = xs[0].shape[1]
    qb = min(block, nq)
    n = -(-nq // qb)
    pad = n * qb - nq

    def prep(a):
        a = jnp.pad(a, [(0, 0), (0, pad)] + [(0, 0)] * (a.ndim - 2))
        a = a.reshape((a.shape[0], n, qb) + a.shape[2:])
        return jnp.moveaxis(a, 1, 0)

    out = lax.map(lambda args: fn(*args), (jnp.arange(n, dtype=jnp.int32),) + tuple(prep(a) for a in xs))
    out = jnp.moveaxis(out, 0, 1)
    out = out.reshape((out.shape[0], n * qb) + out.shape[3:])
    return out[:, :nq]

def stick_breaking_attention(q, k, v, q0):
    kpos = jnp.arange(k.shape[1])
    vf = v.astype(jnp.float32)
    scale = HEAD_DIM ** -0.5

    def block(i, qc):
        qb = qc.shape[1]
        qpos = q0 + i * qb + jnp.arange(qb)
        z = jnp.einsum('bqhd,bkhd->bhqk', qc, k, preferred_element_type=jnp.float32) * scale
        past = (kpos[None, :] < qpos[:, None])[None, None]
        log_keep = jnp.where(past, jax.nn.log_sigmoid(-z), 0.0)
        log_gap = lax.cumsum(log_keep, axis=3, reverse=True) - log_keep
        w = jnp.where(past, jnp.exp(jax.nn.log_sigmoid(z) + log_gap), 0.0)
        return jnp.einsum('bhqk,bkhd->bqhd', w, vf).astype(qc.dtype)

    return map_query_chunks(block, (q,), SB_QBLOCK)

def moba_attention(q, k, v, q0):
    B, Tk, H, D = k.shape
    n_blk = Tk // MOBA_BLOCK
    top = min(MOBA_TOPK, n_blk)
    scale = D ** -0.5
    kb = k.reshape(B, n_blk, MOBA_BLOCK, H, D)
    k_mean = jnp.mean(kb.astype(jnp.float32), axis=2)
    k_blk = jnp.moveaxis(kb, 3, 1)
    v_blk = jnp.moveaxis(v.reshape(B, n_blk, MOBA_BLOCK, H, D), 3, 1)
    b_ix = jnp.arange(B)[:, None, None, None]
    h_ix = jnp.arange(H)[None, None, :, None]
    blk_ids = jnp.arange(n_blk)

    def chunk(i, qc):
        qb = qc.shape[1]
        start = q0 + i * qb
        qpos = start + jnp.arange(qb)
        cur = qpos // MOBA_BLOCK
        gate = jnp.einsum('bqhd,bnhd->bqhn', qc.astype(jnp.float32), k_mean)
        fully_past = (blk_ids[None, :] < cur[:, None])[None, :, None, :]
        gate = jnp.where(fully_past, gate, -jnp.inf)
        _, idx = lax.top_k(gate, top)
        k_sel = k_blk[b_ix, h_ix, idx]
        v_sel = v_blk[b_ix, h_ix, idx]
        ok_sel = jnp.repeat(idx < cur[None, :, None, None], MOBA_BLOCK, axis=-1)
        s_sel = jnp.einsum('bqhd,bqhjsd->bqhjs', qc, k_sel, preferred_element_type=jnp.float32)
        s_sel = s_sel.reshape(B, qb, H, top * MOBA_BLOCK) * scale
        own = start // MOBA_BLOCK
        k_own = lax.dynamic_slice_in_dim(k, own * MOBA_BLOCK, MOBA_BLOCK, axis=1)
        v_own = lax.dynamic_slice_in_dim(v, own * MOBA_BLOCK, MOBA_BLOCK, axis=1)
        own_pos = own * MOBA_BLOCK + jnp.arange(MOBA_BLOCK)
        ok_own = jnp.broadcast_to((own_pos[None, :] <= qpos[:, None])[None, :, None, :], (B, qb, H, MOBA_BLOCK))
        s_own = jnp.einsum('bqhd,bkhd->bqhk', qc, k_own, preferred_element_type=jnp.float32) * scale
        p = masked_softmax(jnp.concatenate([s_sel, s_own], axis=-1), jnp.concatenate([ok_sel, ok_own], axis=-1))
        p_sel = p[..., :top * MOBA_BLOCK].reshape(B, qb, H, top, MOBA_BLOCK)
        p_own = p[..., top * MOBA_BLOCK:]
        o = (jnp.einsum('bqhjs,bqhjsd->bqhd', p_sel, v_sel.astype(jnp.float32))
             + jnp.einsum('bqhk,bkhd->bqhd', p_own, v_own.astype(jnp.float32)))
        return o.astype(qc.dtype)

    return map_query_chunks(chunk, (q,), GATHER_QBLOCK)

def compress_blocks(x, pe, w1, w2):
    B, Tk, H, D = x.shape
    r = CMP_BLOCK // CMP_STRIDE
    c = x.reshape(B, Tk // CMP_STRIDE, CMP_STRIDE, H, D)
    n_cmp = Tk // CMP_STRIDE - r + 1
    blocks = jnp.concatenate([c[:, j:j + n_cmp] for j in range(r)], axis=2)
    blocks = blocks + pe[None, None, :, None, :].astype(x.dtype)
    flat = jnp.moveaxis(blocks, 3, 2).reshape(B, n_cmp, H, CMP_BLOCK * D)
    return jax.nn.silu(flat @ w1) @ w2

def nsa_attention(q, gates, kv, win, q0, cmp_pe, cmp_w1, cmp_w2):
    B, Tk = kv.shape[0], kv.shape[1]
    nq = q.shape[1]
    scale = HEAD_DIM ** -0.5
    k_cmp = compress_blocks(kv[:, :, 0], cmp_pe[0], cmp_w1[0], cmp_w2[0])
    v_cmp = compress_blocks(kv[:, :, 1], cmp_pe[1], cmp_w1[1], cmp_w2[1])
    n_cmp = k_cmp.shape[1]
    cmp_start = jnp.arange(n_cmp) * CMP_STRIDE
    cmp_last = cmp_start + CMP_BLOCK - 1
    n_slc = Tk // SLC_BLOCK
    top = min(SLC_TOPK, n_slc)
    slc_ids = jnp.arange(n_slc)
    slc_start = slc_ids * SLC_BLOCK
    cover = ((cmp_start[:, None] < slc_start[None, :] + SLC_BLOCK)
             & (cmp_last[:, None] >= slc_start[None, :])).astype(jnp.float32)
    k_blk = jnp.moveaxis(kv[:, :, 2].reshape(B, n_slc, SLC_BLOCK, NSA_HKV, HEAD_DIM), 3, 1)
    v_blk = jnp.moveaxis(kv[:, :, 3].reshape(B, n_slc, SLC_BLOCK, NSA_HKV, HEAD_DIM), 3, 1)
    b_ix = jnp.arange(B)[:, None, None, None]
    h_ix = jnp.arange(NSA_HKV)[None, None, :, None]
    qb = min(GATHER_QBLOCK, nq)
    nq_pad = -(-nq // qb) * qb
    win = jnp.pad(win, [(0, 0), (0, nq_pad - nq), (0, 0), (0, 0), (0, 0)])
    k_win, v_win = win[:, :, 0], win[:, :, 1]
    band = WINDOW + qb

    def chunk(i, qc, gc):
        qpos = q0 + i * qb + jnp.arange(qb)
        qg = qc.reshape(B, qb, NSA_HKV, NSA_GROUP, HEAD_DIM)
        s_c = jnp.einsum('bqkgd,bnkd->bqkgn', qg, k_cmp, preferred_element_type=jnp.float32) * scale
        ok_c = (cmp_last[None, :] <= qpos[:, None])[None, :, None, None, :]
        p_c = masked_softmax(s_c, ok_c)
        o_c = jnp.einsum('bqkgn,bnkd->bqkgd', p_c, v_cmp.astype(jnp.float32))
        imp = jnp.einsum('bqkgn,nj->bqkj', p_c, cover)
        cur = qpos // SLC_BLOCK
        forced = (slc_ids[None, :] == 0) | (slc_ids[None, :] == cur[:, None]) | (slc_ids[None, :] == cur[:, None] - 1)
        future = slc_ids[None, :] > cur[:, None]
        score = jnp.where(forced[None, :, None, :], FORCE_SCORE,
                          jnp.where(future[None, :, None, :], -FORCE_SCORE, imp))
        _, idx = lax.top_k(score, top)
        k_sel = k_blk[b_ix, h_ix, idx]
        v_sel = v_blk[b_ix, h_ix, idx]
        pos_sel = idx[..., None] * SLC_BLOCK + jnp.arange(SLC_BLOCK)
        ok_s = (pos_sel <= qpos[None, :, None, None, None]).reshape(B, qb, NSA_HKV, 1, top * SLC_BLOCK)
        s_s = jnp.einsum('bqkgd,bqkjsd->bqkgjs', qg, k_sel, preferred_element_type=jnp.float32)
        s_s = s_s.reshape(B, qb, NSA_HKV, NSA_GROUP, top * SLC_BLOCK) * scale
        p_s = masked_softmax(s_s, ok_s)
        o_s = jnp.einsum('bqkgm,bqkmd->bqkgd', p_s,
                         v_sel.reshape(B, qb, NSA_HKV, top * SLC_BLOCK, HEAD_DIM).astype(jnp.float32))
        k_band = lax.dynamic_slice_in_dim(k_win, i * qb, band, axis=1)
        v_band = lax.dynamic_slice_in_dim(v_win, i * qb, band, axis=1)
        pos_w = q0 - WINDOW + i * qb + jnp.arange(band)
        ok_w = ((pos_w[None, :] >= 0) & (pos_w[None, :] <= qpos[:, None])
                & (qpos[:, None] - pos_w[None, :] < WINDOW))[None, :, None, None, :]
        s_w = jnp.einsum('bqkgd,bskd->bqkgs', qg, k_band, preferred_element_type=jnp.float32) * scale
        p_w = masked_softmax(s_w, ok_w)
        o_w = jnp.einsum('bqkgs,bskd->bqkgd', p_w, v_band.astype(jnp.float32))
        g = gc.reshape(B, qb, NSA_HKV, NSA_GROUP, 3)
        o = g[..., 0:1] * o_c + g[..., 1:2] * o_s + g[..., 2:3] * o_w
        return o.reshape(B, qb, NSA_HQ, HEAD_DIM).astype(qc.dtype)

    return map_query_chunks(chunk, (q, gates), GATHER_QBLOCK)

def even_layer_mixer(xn, q0, past, w_in, g_q, g_k, w_out):
    B, T, _ = xn.shape
    pos = q0 + jnp.arange(T)
    proj = (xn @ w_in).reshape(B, T, 3, N_HEADS, HEAD_DIM)
    q, k, v = proj[:, :, 0], proj[:, :, 1], proj[:, :, 2]
    q_sb = q[:, :, :H_SB]
    q_mb = rope(rms_norm(q[:, :, H_SB:], g_q), pos)
    k_mb = rope(rms_norm(k[:, :, H_SB:], g_k), pos)
    k = jnp.concatenate([k[:, :, :H_SB], k_mb], axis=2)
    new_kv = jnp.stack([k, v], axis=2)
    kv = append_rows(past, new_kv, MOBA_BLOCK)
    o_sb = stick_breaking_attention(q_sb, kv[:, :, 0, :H_SB], kv[:, :, 1, :H_SB], q0)
    o_mb = moba_attention(q_mb, kv[:, :, 0, H_SB:], kv[:, :, 1, H_SB:], q0)
    o = jnp.concatenate([o_sb, o_mb], axis=2).reshape(B, T, N_HEADS * HEAD_DIM)
    return o @ w_out, new_kv

def odd_layer_mixer(xn, q0, past, win_buf, w_in, g_q, g_k, cmp_pe, cmp_w1, cmp_w2, w_out):
    B, T, _ = xn.shape
    pos = q0 + jnp.arange(T)
    proj = xn @ w_in
    n_q = NSA_HQ * HEAD_DIM
    n_kv = 6 * NSA_HKV * HEAD_DIM
    q = rope(rms_norm(proj[..., :n_q].reshape(B, T, NSA_HQ, HEAD_DIM), g_q), pos)
    kvs = proj[..., n_q:n_q + n_kv].reshape(B, T, 6, NSA_HKV, HEAD_DIM)
    gates = jax.nn.sigmoid(proj[..., n_q + n_kv:].astype(jnp.float32)).reshape(B, T, NSA_HQ, 3)
    k_cmp = rope(rms_norm(kvs[:, :, 0], g_k[0]), pos)
    k_slc = rope(rms_norm(kvs[:, :, 2], g_k[1]), pos)
    k_win = rope(rms_norm(kvs[:, :, 4], g_k[2]), pos)
    new_kv = jnp.stack([k_cmp, kvs[:, :, 1], k_slc, kvs[:, :, 3]], axis=2)
    new_win = jnp.stack([k_win, kvs[:, :, 5]], axis=2)
    kv = append_rows(past, new_kv, SLC_BLOCK)
    if win_buf is None:
        win_rows = new_win
        n_keep = min(WINDOW, T)
    else:
        win_rows = jnp.concatenate([win_buf, new_win.astype(win_buf.dtype)], axis=1)
        n_keep = win_buf.shape[1]
    n_before = win_rows.shape[1] - T
    win_arr = jnp.pad(win_rows, [(0, 0), (WINDOW - n_before, 0), (0, 0), (0, 0), (0, 0)])
    new_state = win_rows[:, win_rows.shape[1] - n_keep:]
    o = nsa_attention(q, gates, kv, win_arr, q0, cmp_pe, cmp_w1, cmp_w2)
    return o.reshape(B, T, NSA_HQ * HEAD_DIM) @ w_out, new_kv, new_state

def run_trunk(x, q0, past_kv0, past_kv1, win_bufs,
              g_mix0, w_in0, g_q0, g_k0, w_out0,
              g_mix1, w_in1, g_q1, g_k1, cmp_pe, cmp_w1, cmp_w2, w_out1,
              g_ffn, w_gu, w_down):
    kv0_rows, kv1_rows, win_rows = [], [], []
    h = x
    for layer in range(DEPTH):
        j = layer // 2
        if layer % 2 == 0:
            o, kv_new = even_layer_mixer(rms_norm(h, g_mix0[j]), q0, past_kv0[j],
                                         w_in0[j], g_q0[j], g_k0[j], w_out0[j])
            kv0_rows.append(kv_new)
        else:
            o, kv_new, w_new = odd_layer_mixer(rms_norm(h, g_mix1[j]), q0, past_kv1[j], win_bufs[j],
                                               w_in1[j], g_q1[j], g_k1[j], cmp_pe[j], cmp_w1[j],
                                               cmp_w2[j], w_out1[j])
            kv1_rows.append(kv_new)
            win_rows.append(w_new)
        h = h + o
        h = h + swiglu(rms_norm(h, g_ffn[layer]), w_gu[layer], w_down[layer])
    return h, jnp.stack(kv0_rows), jnp.stack(kv1_rows), jnp.stack(win_rows)

def setup_inputs(seed: int = 0) -> dict:
    key = jax.random.key(seed)
    ks = jax.random.split(key, 24)
    n_pages = PAST_LEN // PAGE_SIZE
    n_pool = (5 * DEC_BATCH * n_pages + 3) // 4
    win_eff = min(WINDOW, PAST_LEN)
    f32 = jnp.float32

    def nrm(k, shape, scale=1.0):
        return jax.random.normal(k, shape, f32) * scale

    def gain(k, shape):
        return 1.0 + 0.02 * jax.random.normal(k, shape, f32)

    page_table = jax.random.permutation(ks[0], n_pool)[:DEC_BATCH * n_pages].reshape(DEC_BATCH, n_pages).astype(jnp.int32)
    return {
        'x_prompt': nrm(ks[1], (BATCH, SEQ, D_MODEL)),
        'x_sample': nrm(ks[2], (DEC_BATCH, DEC_SEQ, D_MODEL)),
        'cache_kv0': nrm(ks[3], (N_EVEN, n_pool, PAGE_SIZE, 2, N_HEADS, HEAD_DIM)),
        'cache_kv1': nrm(ks[4], (N_ODD, n_pool, PAGE_SIZE, 4, NSA_HKV, HEAD_DIM)),
        'state_win': nrm(ks[5], (N_ODD, DEC_BATCH, win_eff, 2, NSA_HKV, HEAD_DIM)),
        'page_table': page_table,
        'g_mix0': gain(ks[6], (N_EVEN, D_MODEL)),
        'w_in0': nrm(ks[7], (N_EVEN, D_MODEL, EVEN_IN), D_MODEL ** -0.5),
        'g_q0': gain(ks[8], (N_EVEN, HEAD_DIM)),
        'g_k0': gain(ks[9], (N_EVEN, HEAD_DIM)),
        'w_out0': nrm(ks[10], (N_EVEN, N_HEADS * HEAD_DIM, D_MODEL), (N_HEADS * HEAD_DIM) ** -0.5),
        'g_mix1': gain(ks[11], (N_ODD, D_MODEL)),
        'w_in1': nrm(ks[12], (N_ODD, D_MODEL, ODD_IN), D_MODEL ** -0.5),
        'g_q1': gain(ks[13], (N_ODD, HEAD_DIM)),
        'g_k1': gain(ks[14], (N_ODD, 3, HEAD_DIM)),
        'cmp_pe': nrm(ks[15], (N_ODD, 2, CMP_BLOCK, HEAD_DIM), 0.1),
        'cmp_w1': nrm(ks[16], (N_ODD, 2, CMP_BLOCK * HEAD_DIM, CMP_HIDDEN), (CMP_BLOCK * HEAD_DIM) ** -0.5),
        'cmp_w2': nrm(ks[17], (N_ODD, 2, CMP_HIDDEN, HEAD_DIM), CMP_HIDDEN ** -0.5),
        'w_out1': nrm(ks[18], (N_ODD, NSA_HQ * HEAD_DIM, D_MODEL), (NSA_HQ * HEAD_DIM) ** -0.5),
        'g_ffn': gain(ks[19], (DEPTH, D_MODEL)),
        'w_gu': nrm(ks[20], (DEPTH, D_MODEL, 2 * D_FF), D_MODEL ** -0.5),
        'w_down': nrm(ks[21], (DEPTH, D_FF, D_MODEL), D_FF ** -0.5),
    }

def reference(x_prompt, x_sample, cache_kv0, cache_kv1, state_win, page_table,
              g_mix0, w_in0, g_q0, g_k0, w_out0,
              g_mix1, w_in1, g_q1, g_k1, cmp_pe, cmp_w1, cmp_w2, w_out1,
              g_ffn, w_gu, w_down):
    y_prompt, kv0_prompt, kv1_prompt, win_prompt = run_trunk(
        x_prompt, 0, [None] * N_EVEN, [None] * N_ODD, [None] * N_ODD,
        g_mix0, w_in0, g_q0, g_k0, w_out0,
        g_mix1, w_in1, g_q1, g_k1, cmp_pe, cmp_w1, cmp_w2, w_out1,
        g_ffn, w_gu, w_down)

    def gather_pages(pool):
        rows = pool[page_table]
        return rows.reshape((rows.shape[0], rows.shape[1] * rows.shape[2]) + rows.shape[3:])

    past0 = [gather_pages(cache_kv0[j]) for j in range(N_EVEN)]
    past1 = [gather_pages(cache_kv1[j]) for j in range(N_ODD)]
    wins = [state_win[j] for j in range(N_ODD)]
    y_sample, kv0_sample, kv1_sample, win_sample = run_trunk(
        x_sample, PAST_LEN, past0, past1, wins,
        g_mix0, w_in0, g_q0, g_k0, w_out0,
        g_mix1, w_in1, g_q1, g_k1, cmp_pe, cmp_w1, cmp_w2, w_out1,
        g_ffn, w_gu, w_down)
    return (y_prompt, y_sample, kv0_prompt, kv0_sample, kv1_prompt, kv1_sample, win_prompt, win_sample)


_drawn_inputs = setup_inputs


def setup_inputs(seed=0):
    import zlib

    import numpy as np

    out = dict(_drawn_inputs(seed))
    spreads = {}
    factors = {'g_mix0': 2.722,
     'g_q0': 8.0,
     'g_k0': 5.224,
     'g_mix1': 2.819,
     'g_q1': 8.0,
     'g_k1': 4.141,
     'g_ffn': 2.985,
     'cmp_pe': 4.449}
    for name, (base, spread) in spreads.items():
        noise = np.random.default_rng([zlib.crc32(name.encode()), seed]).standard_normal(out[name].shape)
        drawn = base * np.exp(spread * noise) if base else spread * noise
        out[name] = __import__('jax').numpy.asarray(drawn.astype(out[name].dtype))
    for name, factor in factors.items():
        out[name] = (out[name] * factor).astype(out[name].dtype)
    return out
```

```python
from contextlib import ExitStack

import concourse.bass as bass
from concourse import mybir
import numpy as np

F32 = mybir.dt.float32
I32 = mybir.dt.int32
ALU = mybir.AluOpType
ACT = mybir.ActivationFunctionType
AX = mybir.AxisListType.X

P = 128
D = 1024
KD = D // P
TP, NB, NQ = 256, 8, 4
TS = NB * NQ
T = TP + TS
PAST, PAGE = 1024, 128
NPG = PAST // PAGE
HD, NH, NKV = 64, 16, 4
DFF = 2816
FT = DFF // P
N0 = 3 * NH * HD
NQ1 = NH * HD
N1 = NQ1 + 6 * NKV * HD + 3 * NH
KVW = NKV * HD
WIN = 512
NWB = WIN // P
NCS = PAST // 16 - 1
NCP = TP // 16 - 1
CH = 256
EPS = 1e-6
SC = HD ** -0.5
NEG = -1e30
WT = (P, P, TS)
SLOTS = 3
SLOTW = 4096
RW = 1060
GATE_ORDER = (1, 2, 0)


def constants():
    c = {}
    c["ident"] = np.eye(P)
    c["mean"] = np.full((P, P), 1.0 / D)
    r = np.arange(P)
    same = (r[:, None] // 16 == r[None, :] // 16) & (r[:, None] % 4 == r[None, :] % 4)
    c["group"] = same * 1.0
    q = r[:, None]
    k = np.arange(P)[None, :]
    diag = np.where(k <= q, 0.0, NEG)
    c["causal"] = np.concatenate([diag, np.zeros((P, P)), diag], 1)
    c["strict"] = (k < q) * 1.0
    c["notpast"] = (k >= q) * 1.0
    half = HD // 2
    inv = np.power(np.float32(10000.0), -np.arange(half, dtype=np.float32) / np.float32(half)).astype(np.float32)
    pos = np.stack([r, P + r, PAST + r % NQ], 1).astype(np.float32)
    ang = (pos[:, :, None] * inv[None, None, :]).astype(np.float32)
    co, si = np.cos(ang).astype(np.float32), np.sin(ang).astype(np.float32)
    c["cos"] = np.concatenate([co, co], 2).reshape(P, -1)
    c["sin"] = np.concatenate([-si, si], 2).reshape(P, -1)
    n = np.arange(NCP)[None, :]
    c["cmpcausal"] = np.concatenate([np.where(16 * n + 31 <= q + P * t, 0.0, NEG) for t in range(2)], 1)
    c["cmpany"] = np.concatenate([(q + P * t >= 31) * 1.0 for t in range(2)], 1)
    tok = np.arange(TS)[None, :]
    for name, per in (("0", 32), ("1", 64)):
        ok, past = [], []
        for g in range(NB * per // P):
            b = g * (P // per) + q // per
            ok.append((tok // NQ == b) & (tok % NQ <= q % NQ))
            past.append((tok // NQ == b) & (tok % NQ < q % NQ))
        c["newneg" + name] = np.where(np.concatenate(ok, 1), 0.0, NEG)
        if name == "0":
            c["newpast"] = np.concatenate(past, 1) * 1.0
            c["newnot"] = 1.0 - c["newpast"]
    c["winneg"] = np.where(np.arange(NQ)[None, :] > q % NQ, 0.0, NEG)
    c["head0"] = (np.arange(8)[None, :] == (q % 32) // 4) * 1.0
    c["head1"] = (np.arange(NKV)[None, :] == (q % 64) // 16) * 1.0
    c["rank"] = np.broadcast_to(np.arange(1, 17)[None, :], (P, 16))
    at, off = 0, {}
    for name, a in c.items():
        off[name] = (at, a.shape[1])
        at += a.shape[1]
    return np.ascontiguousarray(np.concatenate(list(c.values()), 1).astype(np.float32)), off


def trunk(nc, off, x_prompt, x_sample, cache_kv0, cache_kv1, state_win, page_table, w_in0, w_out0, w_in1, w_out1,
          cmp_w1, cmp_w2, w_gu, w_down, consts, gcol, grow, pecol,
          y_prompt, y_sample, kv0_prompt, kv0_sample, kv1_prompt, kv1_sample, win_prompt, win_sample, gate_scratch):
    ctx = ExitStack()
    with ctx:
        def sb(name, cols, dt=F32, rows=P):
            return ctx.enter_context(nc.sbuf_tensor(name, [rows, cols], dt))

        def sem(name):
            return ctx.enter_context(nc.semaphore(name))

        hT = sb("hT", KD * T)[:].rearrange("p (k t) -> p k t", t=T)
        xT = sb("xT", KD * T)[:].rearrange("p (k t) -> p k t", t=T)
        oT = xT
        ring = sb("ring", SLOTS * SLOTW)[:].rearrange("p (s n) -> p s n", s=SLOTS)
        proj_t = sb("proj", 3 * N0)
        proj = proj_t[:].rearrange("p (t n) -> p t n", t=3)
        w1r = proj_t[:, 0:2 * 16 * CH].rearrange("p (k i n) -> p k i n", k=2, i=16)
        qT = sb("qT", KD * T)[:].rearrange("p (k t) -> p k t", t=T)
        kT = sb("kT", KD * T)[:].rearrange("p (k t) -> p k t", t=T)
        big = sb("big", 2 * 8 * 512)
        KT = big[:].rearrange("p (b i n) -> p b i n", b=2, i=8)
        actT = big[:, 0:FT * T].rearrange("p (f t) -> p f t", t=T)
        sqT = big[:, 0:KD * T].rearrange("p (k t) -> p k t", t=T)
        XTp = big[:, 0:8 * P].rearrange("p (i n) -> p i n", i=8)
        PTp = big[:, 2048:4096].rearrange("p (b n) -> p b n", b=2)
        R = sb("rows", 4 * RW)[:].rearrange("p (r n) -> p r n", r=4)
        pq = sb("pq", 2944)
        qb0 = pq[:, 0:2048].rearrange("p (b i c) -> p b i c", b=NB, i=8)
        PT0 = pq[:, 0:2304].rearrange("p (y c n) -> p y c n", y=2, c=9)
        qb1 = pq[:, 0:1024].rearrange("p (b i c) -> p b i c", b=NB, i=2)
        PT1 = pq[:, 1024:2944].rearrange("p (j n) -> p j n", j=15)
        hid = pq[:, 1024:1024 + 4 * 252].rearrange("p (j n) -> p j n", j=4)
        hidp = pq[:, 1024:1024 + 4 * 60].rearrange("p (j n) -> p j n", j=4)
        kc = sb("kc", NB * 2 * NCS)[:].rearrange("p (b i n) -> p b i n", b=NB, i=2)
        vc = sb("vc", NB * KVW)[:].rearrange("p (b n) -> p b n", b=NB)
        kcp = sb("kcp", NKV * NCP)[:].rearrange("p (h n) -> p h n", h=NKV)
        vcp = sb("vcp", KVW)
        w2 = sb("w2", 4 * HD)[:].rearrange("p (k h n) -> p k h n", k=2, h=2)
        ct = sb("ct", sum(n for _, n in off.values()))
        gc = sb("gc", 4 * KD)
        gr = sb("gr", 6 * HD)
        pec = sb("pec", 32)
        cb = sb("cb", 4)
        pages = sb("pages", NB * NPG, I32, 1)
        ss = sb("ss", 3 * 28)[:].rearrange("p (t n) -> p t n", t=3)
        gates = sb("gates", 3 * 48)[:].rearrange("p (t n) -> p t n", t=3)
        gp = sb("gp", NH * 6)[:].rearrange("p (h n) -> p h n", h=NH)
        gs = sb("gs", 12)[:].rearrange("p (g n) -> p g n", g=4)
        st = sb("st", 96)
        osm = sb("osm", 2 * HD)[:].rearrange("p (b n) -> p b n", b=2)
        ps = [ctx.enter_context(nc.psum_tensor(f"ps{i}", [P, 512], F32)) for i in range(8)]

        def C(name, a=0, b=None, rows=P):
            o, n = off[name]
            return ct[0:rows, o + a:o + (n if b is None else b)]

        zero = C("causal", P, P + 1)
        ident = C("ident")

        def rep(ap, axis, n):
            a = ap.unsqueeze(axis)
            shape = list(a.shape)
            shape[axis] = n
            return a.broadcast_to(shape)

        s_page, s_x, s_const, s_kv, s_out, s_w1 = (sem(n) for n in ("s_page", "s_x", "s_const", "s_kv", "s_out", "s_w1"))
        s_slot = [sem(f"s_slot{i}") for i in range(SLOTS)]
        x_t, x_e, y_t, y_e = sem("x_turned"), sem("x_kept"), sem("y_turned"), sem("y_kept")
        n_sq = [sem(f"squares{i}") for i in range(4)]
        n_ps = [sem(f"meansq{i}") for i in range(4)]
        n_rc = [sem(f"recip{i}") for i in range(4)]
        n_rs = [sem(f"rstd{i}") for i in range(4)]
        n_x = [sem(f"normed{i}") for i in range(4)]
        L2 = range(2)
        in_p, in_e = [sem(f"in_done{i}") for i in L2], [sem(f"in_kept{i}") for i in L2]
        q_rc, q_rs, q_d = [sem(f"qk_recip{i}") for i in L2], [sem(f"qk_rstd{i}") for i in L2], [sem(f"roped{i}") for i in L2]
        t_p, t_e = [sem(f"qk_turned{i}") for i in L2], [sem(f"qk_kept{i}") for i in L2]
        a_s, a_g, a_m = [sem(f"pscores{i}") for i in L2], sem("psigmoids"), [sem(f"pmax{i}") for i in L2]
        a_e, a_w, a_t = [sem(f"pexp{i}") for i in L2], [sem(f"pweights{i}") for i in L2], [sem(f"pturned{i}") for i in L2]
        a_te, a_pv, a_oe = [sem(f"pkept{i}") for i in L2], [sem(f"pvdone{i}") for i in L2], [sem(f"pokept{i}") for i in L2]
        qb_z, qb_d = [sem(f"qb_zero{i}") for i in L2], [sem(f"qb_ready{i}") for i in L2]
        k_p, k_a, k_d = ([sem(f"{n}{i}") for i in range(3)] for n in ("k_turned", "k_kept_act", "k_kept_dve"))
        k_s, k_n = [sem(f"dscores{i}") for i in L2], [sem(f"dnew{i}") for i in L2]
        r_sg, r_ps = sem("dsigmoids"), [sem(f"scores_read{i}") for i in L2]
        r_m, r_e = [sem(f"dmax{i}") for i in L2], [sem(f"dexp{i}") for i in L2]
        r_w, r_t, r_te = [sem(f"dweights{i}") for i in L2], [sem(f"dturned{i}") for i in L2], [sem(f"dkept{i}") for i in L2]
        v_c, v_x = [sem(f"pv_chunk{i}") for i in L2], [sem(f"heads_picked{i}") for i in L2]
        v_t, v_e = [sem(f"o_turned{i}") for i in L2], [sem(f"o_kept{i}") for i in L2]
        i_m, i_e, i_w, i_p = sem("cmp_max"), sem("cmp_exp"), sem("cmp_probs"), sem("importance")
        i_r = sem("importance_read")
        c_b, c_be, c_h, c_he, c_w, c_we = (sem(n) for n in ("cmp_bias", "cmp_bias_kept", "cmp_hidden", "cmp_silu", "cmp_out", "cmp_kept"))
        p_h, p_he, p_w, p_we = (sem(n) for n in ("pcmp_hidden", "pcmp_silu", "pcmp_out", "pcmp_kept"))
        g_s, g_d, g_l, g_p = sem("gates_done"), sem("gates_stored"), sem("gates_rows"), sem("gates_prompt")
        o_p, o_e = [sem(f"out_done{i}") for i in L2], [sem(f"out_added{i}") for i in L2]
        u_p, u_a, u_e = [sem(f"gu_done{i}") for i in L2], [sem(f"silu_done{i}") for i in L2], [sem(f"act_kept{i}") for i in L2]
        d_p, d_e = [sem(f"down_done{i}") for i in L2], [sem(f"down_added{i}") for i in L2]
        ch = sem("vector_chain")

        nin = [[min(512, n - c) for c in range(0, n, 512)] for n in (N0, N1)]
        w_in = [w_in0[0].rearrange("(k p) n -> p k n", p=P), w_in1[0].rearrange("(k p) n -> p k n", p=P)]
        w_out = [w_out0[0].rearrange("(k p) n -> p k n", p=P), w_out1[0].rearrange("(k p) n -> p k n", p=P)]
        w1_h = cmp_w1[0].rearrange("k (i p) n -> p k i n", p=P)

        plan = []

        def slot_view(s, a, b, **kw):
            return ring[:, s, a:b]

        for n, w in enumerate(nin[0]):
            plan.append((("in", 0, n), in_p[0], 3 * (n + 1)))
        for cc in range(16):
            plan.append((("k0", cc // 2, cc % 2), k_p[0], 8 * (cc + 1)))
        for cc in range(16):
            plan.append((("v0", cc // 2, cc % 2), v_c[0], cc + 1))

        def ffn_plan(l):
            for n in range(2):
                plan.append((("out", l, n), o_p[l], 4 * (n + 1)))
            for n in range(FT // 2):
                plan.append((("gu", l, n), u_p[l], 2 * (n + 1)))
                if l == 0 and n == 4:
                    plan.append((("w1r",), None, 0))
            for n in range(8):
                plan.append((("down", l, n), d_p[l], n + 1))

        ffn_plan(0)
        for b in range(NB):
            plan.append((("cmp", b), k_p[1], 8 * (b + 1)))
        for n, w in enumerate(nin[1]):
            plan.append((("in", 1, n), in_p[1], 3 * (n + 1)))
        for k in range(2):
            plan.append((("w1", k), p_h, 2 * (k + 1)))
        order = [("k1", 0), ("k1", 1)]
        for g in range(4):
            if g < 3:
                order += [("k1", 2 * g + 2), ("k1", 2 * g + 3)]
            order += [("v1", 2 * g), ("v1", 2 * g + 1)]
        for kind, b in order:
            plan.append(((kind, b),) + ((k_p[2], 6 * (b + 1)) if kind == "k1" else (v_c[1], b + 1)))
        ffn_plan(1)

        place, landed, fill = {}, {}, [0] * SLOTS
        ringed = [e for e in plan if e[0] != ("w1r",)]

        def n_dmas(name):
            return {"k0": 4, "v0": 4, "gu": 2, "cmp": NPG, "k1": NPG + 1, "v1": NPG + 1}.get(name[0], 1)

        for i, e in enumerate(ringed):
            s = i % SLOTS
            fill[s] += 16 * n_dmas(e[0])
            place[e[0]], landed[e[0]] = s, fill[s]

        def take(eng, *name):
            s = place[name]
            eng.wait_ge(s_slot[s], landed[name])
            return ring[:, s, :]

        block = ctx.enter_context(nc.Block())

        @block.sync
        def _(sp):
            sp.dma_start(pages[:], page_table.rearrange("b n -> (b n)").unsqueeze(0)).then_inc(s_page, 16)
            sp.dma_start(ct[:], consts).then_inc(s_const, 16)
            for t in range(2):
                sp.dma_start(proj[:, t, 0:D], x_prompt[0, t * P:(t + 1) * P, :]).then_inc(s_x, 16)
            sp.dma_start(proj[0:TS, 2, 0:D], x_sample.rearrange("b q d -> (b q) d")).then_inc(s_x, 16)
            sp.dma_start(gc[:], gcol).then_inc(s_const, 16)
            sp.dma_start(gr[:], grow).then_inc(s_const, 16)
            sp.dma_start(pec[:], pecol).then_inc(s_const, 16)
            sp.dma_start(w2[:, :, :, :], cmp_w2[0].rearrange("k (h p) n -> p k h n", p=P)).then_inc(s_const, 16)
            sp.wait_ge(s_page, 16)

            def page(b, pg):
                return bass.ds(sp.value_load(pages[0:1, b * NPG + pg:b * NPG + pg + 1], min_val=0,
                                             max_val=cache_kv0.shape[1] - 1), 1)

            i = 0
            for name, _, _ in plan:
                kind = name[0]
                if kind == "w1r":
                    sp.wait_ge(o_p[0], 1)
                    sp.wait_ge(s_kv, 48)
                    sp.dma_start(w1r[:, 0], w1_h[:, 0]).then_inc(s_w1, 16)
                    sp.dma_start(w1r[:, 1], w1_h[:, 1]).then_inc(s_w1, 16)
                    continue
                if i >= SLOTS:
                    _, freed, value = ringed[i - SLOTS]
                    sp.wait_ge(freed, value)
                s = i % SLOTS
                slot = ring[:, s, :]
                i += 1
                if kind == "in":
                    l, n = name[1:]
                    w = nin[l][n]
                    jobs = [(slot[:, 0:8 * w].rearrange("p (k n) -> p k n", k=8), w_in[l][:, :, n * 512:n * 512 + w])]
                elif kind == "out":
                    l, n = name[1:]
                    jobs = [(slot.rearrange("p (k n) -> p k n", k=8), w_out[l][:, :, n * 512:(n + 1) * 512])]
                elif kind == "gu":
                    l, n = name[1:]
                    w = w_gu[l].rearrange("(k p) n -> p k n", p=P)
                    d = slot.rearrange("p (k n) -> p k n", k=8)
                    jobs = [(d[:, :, j * 256:(j + 1) * 256], w[:, :, j * DFF + n * 256:j * DFF + (n + 1) * 256])
                            for j in range(2)]
                elif kind == "down":
                    l, n = name[1:]
                    w = w_down[l].rearrange("(k p) n -> p k n", p=P)
                    jobs = [(slot[:, 0:11 * 256].rearrange("p (k n) -> p k n", k=11),
                             w[:, (n % 2) * 11:(n % 2 + 1) * 11, (n // 2) * 256:(n // 2 + 1) * 256])]
                elif kind in ("k0", "v0"):
                    b, half = name[1:]
                    c = cache_kv0[0].rearrange("g s two h d -> g s two (h d)")
                    jobs = [(slot[:, r * D:(r + 1) * D], (c, b, half * 4 + r, int(kind == "v0"))) for r in range(4)]
                elif kind == "cmp":
                    c = cache_kv1[0].rearrange("g s (two kv) h d -> g s two (kv h d)", two=2)
                    jobs = [(slot[:, r * 512:(r + 1) * 512], (c, name[1], r, 0)) for r in range(NPG)]
                elif kind in ("k1", "v1"):
                    b, v = name[1], int(kind == "v1")
                    c = cache_kv1[0].rearrange("g s kv h d -> g s kv (h d)")
                    jobs = [(slot[:, r * KVW:(r + 1) * KVW], (c, b, r, 2 + v)) for r in range(NPG)]
                    jobs.append((slot[:, NPG * KVW:(NPG + NWB) * KVW].rearrange("p (r n) -> p r n", r=NWB),
                                 state_win[0, b].rearrange("(r p) two h d -> p r two (h d)", p=P)[:, :, v, :]))
                else:
                    jobs = [(slot.rearrange("p (i n) -> p i n", i=16), w1_h[:, name[1]])]
                assert len(jobs) == n_dmas(name)
                for dst, src in jobs:
                    if isinstance(src, tuple):
                        c, b, pg, part = src
                        src = c[page(b, pg), :, part, :].rearrange("g s n -> (g s) n")
                    sp.dma_start(dst, src).then_inc(s_slot[s], 16)

        @block.tensor
        def _(pe):
            mm = nc.tensor.matmul

            def turn(out, in_, rows=P):
                return nc.tensor.transpose(out, in_, C("ident", 0, rows, rows))

            pe.wait_ge(s_x, 48)
            pe.wait_ge(s_const, 80)
            for t in range(3):
                for j in range(2):
                    for i in range(4):
                        last = turn(ps[2 * t + j][:, i * P:i * P + WT[t]],
                                    proj[0:WT[t], t, (4 * j + i) * P:(4 * j + i + 1) * P], WT[t])
                    last.then_inc(x_t, 1)

            def norm(i):
                pe.wait_ge(n_sq[i], 2)
                for k in range(KD):
                    last = mm(ps[7][:, 0:T], C("mean"), sqT[:, k, :], start=k == 0, stop=k == KD - 1)
                last.then_inc(n_ps[i], 1)
                pe.wait_ge(n_x[i], KD)

            def project_in(l):
                for n, w in enumerate(nin[l]):
                    src = take(pe, "in", l, n)[:, 0:8 * w].rearrange("p (k n) -> p k n", k=8)
                    if n >= 2:
                        pe.wait_ge(in_e[l], 3 * (n - 1))
                    for t in range(3):
                        for k in range(KD):
                            last = mm(ps[(n % 2) * 3 + t][0:WT[t], 0:w], xT[:, k, t * P:t * P + WT[t]], src[:, k, :],
                                      start=k == 0, stop=k == KD - 1)
                        last.then_inc(in_p[l], 1)

            def turn_qk(l):
                pe.wait_ge(in_e[l], 3 * len(nin[l]))
                pe.wait_ge(q_d[l], 3)
                if l == 0:
                    groups = [(t, c) for t in range(3) for c in (0, 512, 1024, 1536)]
                else:
                    groups = [(t, c) for t in range(3) for c in (0, 512)] + [(t, None) for t in range(3)] + \
                             [(t, 1024) for t in range(2)]
                for i, (t, c) in enumerate(groups):
                    if i >= 6:
                        pe.wait_ge(t_e[l], i - 5)
                    cols = [c + j * P for j in range(4)] if c is not None else [1536, 1664, 2048, 2176]
                    for j, a in enumerate(cols):
                        last = turn(ps[i % 6][:, j * P:j * P + WT[t]], proj[0:WT[t], t, a:a + P], WT[t])
                    last.then_inc(t_p[l], 1)
                pe.wait_ge(t_e[l], len(groups))

            def prompt0():
                def scores(h):
                    if h >= 2:
                        pe.wait_ge(a_w[0], h - 1)
                    hb = 64 * (h % 2)
                    q, k = qT[hb:hb + 64, h // 2, :], kT[hb:hb + 64, h // 2, :]
                    mm(ps[h % 2][:, 0:P], q[:, 0:P], k[:, 0:P], start=True, stop=True)
                    mm(ps[h % 2][:, P:3 * P], q[:, P:2 * P], k[:, 0:2 * P], start=True, stop=True).then_inc(a_s[0], 1)

                def values(h):
                    pe.wait_ge(a_w[0], h + 1)
                    if h >= 2:
                        pe.wait_ge(a_te[0], h - 1)
                    for j in range(3):
                        last = turn(ps[2 + h % 2][:, j * P:(j + 1) * P], R[:, 3, (h % 2) * 384 + j * P:(h % 2) * 384 + (j + 1) * P])
                    last.then_inc(a_t[0], 1)
                    pe.wait_ge(a_te[0], h + 1)
                    if h >= 4 and h % 2 == 0:
                        pe.wait_ge(a_oe[0], h // 2 - 1)
                    o = ps[4 + (h // 2) % 2][64 * (h % 2):64 * (h % 2) + 64, 0:TP]
                    v = 2 * D + h * HD
                    mm(o, proj[:, 0, v:v + HD], pair_first(PTp[:, h % 2, 0:384]), start=True, stop=False)
                    mm(o[:, P:2 * P], proj[:, 1, v:v + HD], PTp[:, h % 2, 256:384], start=False, stop=True).then_inc(a_pv[0], 1)

                scores(0)
                for h in range(NH):
                    if h + 1 < NH:
                        scores(h + 1)
                    values(h)

            def pair_first(x):
                return x[:, 0:256]

            def decode_k0():
                pe.wait_ge(qb_d[0], 1)
                for cc in range(17):
                    if cc < 16:
                        src = take(pe, "k0", cc // 2, cc % 2)
                    for p in range(8):
                        if cc < 16:
                            i = cc * 8 + p
                            if i >= 2:
                                pe.wait_ge((k_a, k_d)[i % 2][0], i // 2)
                            for r in range(4):
                                last = turn(ps[6 + i % 2][:, r * P:(r + 1) * P], src[:, r * D + p * P:r * D + (p + 1) * P])
                            last.then_inc(k_p[0], 1)
                        if cc >= 1:
                            c = cc - 1
                            b, half = c // 2, c % 2
                            bl = b % 4
                            i = c * 8 + p
                            pe.wait_ge((k_a, k_d)[i % 2][0], i // 2 + 1)
                            if c == 8 and p == 0:
                                pe.wait_ge(r_ps[0], 1)
                                pe.wait_ge(r_sg, 1)
                            mm(ps[(p // 4) * 2 + half][32 * bl:32 * bl + 32, :], qb0[:, b, p, :], KT[:, c % 2, p, :],
                               start=p % 4 == 0, stop=p % 4 == 3).then_inc(k_s[0], 1)
                    if cc >= 1 and (cc - 1) % 2 == 1:
                        b = (cc - 1) // 2
                        bl = b % 4
                        for p in range(8):
                            last = mm(ps[4][32 * bl:32 * bl + 32, (p // 4) * 32:(p // 4) * 32 + 32], qb0[:, b, p, :],
                                      kT[:, p, TP:T], start=p % 4 == 0, stop=p % 4 == 3)
                        last.then_inc(k_n[0], 1)

            def turn_o(l, i):
                pe.wait_ge(v_x[l], i + 1)
                if i >= 1:
                    pe.wait_ge(v_e[l], i)
                if l == 1:
                    pe.wait_ge(i_r, min(i + 3, 4))
                turn(ps[4][0:64, P:2 * P], osm[:, i % 2, :]).then_inc(v_t[l], 1)

            def decode_v0(g):
                pe.wait_ge(r_w[0], 2 * (g + 1))
                for i in range(6):
                    y, c0 = i // 3, 4 * (i % 3)
                    n = g * 6 + i
                    if n >= 2:
                        pe.wait_ge(r_te[0], n - 1)
                    for c in range(c0, min(c0 + 4, 9)):
                        w = P if c < 8 else TS
                        last = turn(ps[6 + i % 2][0:w, (c - c0) * P:(c - c0 + 1) * P], R[:, 3 * y, c * P:c * P + w])
                    last.then_inc(r_t[0], 1)
                pe.wait_ge(r_te[0], 6 * (g + 1))
                for bl in range(4):
                    b = 4 * g + bl
                    n = b // 2
                    if bl % 2 == 0 and n >= 1:
                        pe.wait_ge(v_x[0], n)
                    for half in range(2):
                        src = take(pe, "v0", b, half)
                        for r in range(4):
                            c = half * 4 + r
                            for y in range(2):
                                lo = (bl % 2) * 64 + y * 32
                                last = mm(ps[5][lo:lo + 32, :], PT0[:, y, c, 32 * bl:32 * bl + 32],
                                          src[:, r * D + y * 512:r * D + (y + 1) * 512], start=c == 0, stop=False)
                        if half == 1:
                            for y in range(2):
                                lo = (bl % 2) * 64 + y * 32
                                last = mm(ps[5][lo:lo + 32, :], PT0[0:TS, y, 8, 32 * bl:32 * bl + 32],
                                          proj[0:TS, 2, 2 * D + y * 512:2 * D + (y + 1) * 512], start=False, stop=True)
                        last.then_inc(v_c[0], 1)
                    if bl % 2 == 1 and n >= 1:
                        turn_o(0, n - 1)

            def project_out(l):
                for n in range(2):
                    src = take(pe, "out", l, n).rearrange("p (k n) -> p k n", k=8)
                    for j in range(4):
                        i = n * 4 + j
                        if i >= 4:
                            pe.wait_ge(o_e[l], i - 3)
                        for k in range(KD):
                            last = mm(ps[j][:, 0:T], src[:, k, j * P:(j + 1) * P], oT[:, k, :], start=k == 0, stop=k == KD - 1)
                        last.then_inc(o_p[l], 1)

            def ffn(l):
                for n in range(FT // 2):
                    src = take(pe, "gu", l, n).rearrange("p (k n) -> p k n", k=8)
                    for j in range(2):
                        f = 2 * n + j
                        if f >= 3:
                            pe.wait_ge(u_e[l], f - 2)
                        for y in range(2):
                            for k in range(KD):
                                last = mm(ps[2 * (f % 3) + y][:, 0:T], src[:, k, y * 256 + j * P:y * 256 + (j + 1) * P],
                                          xT[:, k, :], start=k == 0, stop=k == KD - 1)
                        last.then_inc(u_p[l], 1)
                pe.wait_ge(u_e[l], FT)
                for n in range(8):
                    cg, kh = n // 2, n % 2
                    src = take(pe, "down", l, n)[:, 0:11 * 256].rearrange("p (k n) -> p k n", k=11)
                    if cg >= 2 and kh == 0:
                        pe.wait_ge(d_e[l], 2 * (cg - 1))
                    for j in range(2):
                        for k in range(11):
                            last = mm(ps[(cg % 2) * 2 + j][:, 0:T], src[:, k, j * P:(j + 1) * P], actT[:, kh * 11 + k, :],
                                      start=kh == 0 and k == 0, stop=kh == 1 and k == 10)
                    last.then_inc(d_p[l], 1)

            def compress_cache():
                pe.wait_ge(s_w1, 32)
                pe.wait_ge(d_e[0], KD)
                for j in range(4):
                    for i in range(16):
                        last = mm(ps[4][:, j:j + 1], w1r[:, j // 2, i, (j % 2) * P:(j % 2 + 1) * P],
                                  pec[:, (j // 2) * 16 + i:(j // 2) * 16 + i + 1], start=i == 0, stop=i == 15)
                last.then_inc(c_b, 1)

                def second(b):
                    pe.wait_ge(c_he, 4 * (b + 1))
                    if b >= 1:
                        pe.wait_ge(c_we, b)
                    else:
                        pe.wait_ge(c_be, 1)
                    hv = hid.rearrange("p j (h n) -> p j h n", h=NKV)
                    for par in range(2):
                        for kp in range(2):
                            for hf in range(2):
                                mm(ps[5][par * 64:par * 64 + 64, kp * NCS:(kp + 1) * NCS], w2[:, 0, hf, :], hv[:, hf, 2 * kp + par, :],
                                   start=hf == 0, stop=hf == 1)
                    for h in range(NKV):
                        for hf in range(2):
                            last = mm(ps[4][0:NCS, h * HD:(h + 1) * HD], hv[:, 2 + hf, h, :], w2[:, 1, hf, :],
                                      start=hf == 0, stop=hf == 1)
                    last.then_inc(c_w, 1)

                for bb in range(NB + 1):
                    if bb < NB:
                        src = take(pe, "cmp", bb)
                    if bb >= 1:
                        pe.wait_ge(k_a[1], 4 * bb)
                        pe.wait_ge(k_d[1], 4 * bb)
                    for i in range(8):
                        if bb < NB:
                            n = bb * 8 + i
                            if n >= 2:
                                pe.wait_ge((k_a, k_d)[n % 2][1], n // 2)
                            for r in range(4):
                                a = (4 * (i % 2) + r) * 512 + (i // 2) * P
                                last = turn(ps[6 + n % 2][:, r * P:(r + 1) * P], src[:, a:a + P])
                            last.then_inc(k_p[1], 1)
                        if bb >= 1:
                            b, j = bb - 1, i // 2
                            if b >= 1 and i == 1:
                                second(b - 1)
                            if i % 2 == 0 and b >= 1:
                                pe.wait_ge(c_he, 4 * (b - 1) + j + 1)
                            for o in range(8 * (i % 2), 8 * (i % 2) + 8):
                                last = mm(ps[j][:, 0:NKV * NCS], w1r[:, j // 2, o, (j % 2) * P:(j % 2 + 1) * P],
                                          KT[:, b % 2, (j // 2) * 4:(j // 2) * 4 + 4, o:o + 8 * (NCS - 1) + 1:8],
                                          start=o == 0, stop=o == 15)
                            if i % 2 == 1:
                                last.then_inc(c_h, 1)
                second(NB - 1)
                pe.wait_ge(c_we, NB)

            def compress_prompt():
                for k in range(2):
                    src = take(pe, "w1", k).rearrange("p (i n) -> p i n", i=16)
                    for hf in range(2):
                        for o in range(16):
                            last = mm(ps[2 * k + hf][:, 0:NKV * NCP], src[:, o, hf * P:(hf + 1) * P],
                                      XTp[:, k * 4:k * 4 + 4, o:o + 8 * (NCP - 1) + 1:8], start=o == 0, stop=o == 15)
                        last.then_inc(p_h, 1)
                pe.wait_ge(p_he, 4)
                hv = hidp.rearrange("p j (h n) -> p j h n", h=NKV)
                for dh in range(2):
                    for hf in range(2):
                        mm(ps[5][dh * 64:dh * 64 + 64, 0:NKV * NCP], w2[:, 0, hf, :], hidp[:, hf, :], start=hf == 0, stop=hf == 1)
                for h in range(NKV):
                    for hf in range(2):
                        last = mm(ps[4][0:NCP, h * HD:(h + 1) * HD], hv[:, 2 + hf, h, :], w2[:, 1, hf, :],
                                  start=hf == 0, stop=hf == 1)
                last.then_inc(p_w, 1)
                pe.wait_ge(p_we, 1)

            def prompt1():
                def scores(h):
                    if h >= 2:
                        pe.wait_ge(a_m[1], h - 1)
                    hb, kv = 64 * (h % 2), h // 4
                    q = qT[hb:hb + 64, h // 2, :]
                    A, B = ps[2 * (h % 2)], ps[2 * (h % 2) + 1]
                    for br, bank in ((0, A), (1, B)):
                        k = kT[hb:hb + 64, 4 * br + kv, :]
                        mm(bank[:, 0:P], q[:, 0:P], k[:, 0:P], start=True, stop=True)
                        mm(bank[:, P:3 * P], q[:, P:2 * P], k[:, 0:2 * P], start=True, stop=True)
                    for t in range(2):
                        last = mm(A[:, 384 + t * NCP:384 + (t + 1) * NCP], q[:, t * P:(t + 1) * P], kcp[hb:hb + 64, kv, :],
                                  start=True, stop=True)
                    last.then_inc(a_s[1], 1)

                def values(h):
                    pe.wait_ge(a_w[1], h + 1)
                    if h >= 1:
                        pe.wait_ge(a_te[1], h)
                    W = R[:, h % 2, :]
                    for br in range(2):
                        for j in range(3):
                            turn(ps[4 + br][:, j * P:(j + 1) * P], W[:, br * 384 + j * P:br * 384 + (j + 1) * P])
                    for t in range(2):
                        last = turn(ps[6][0:NCP, t * P:(t + 1) * P], W[:, 768 + t * NCP:768 + (t + 1) * NCP])
                    last.then_inc(a_t[1], 1)
                    pe.wait_ge(a_te[1], h + 1)
                    if h >= 2 and h % 2 == 0:
                        pe.wait_ge(a_oe[1], h // 2)
                    kv = h // 4
                    o = ps[7][64 * (h % 2):64 * (h % 2) + 64, 0:TP]
                    X = PTp[:, h % 2, :]
                    mm(o, vcp[0:NCP, kv * HD:(kv + 1) * HD], X[0:NCP, 768:1024], start=True, stop=False)
                    for br in range(2):
                        v = NQ1 + (3 + 2 * br) * KVW + kv * HD
                        mm(o, proj[:, 0, v:v + HD], X[:, br * 384:br * 384 + 256], start=False, stop=False)
                        last = mm(o[:, P:2 * P], proj[:, 1, v:v + HD], X[:, br * 384 + 256:br * 384 + 384], start=False, stop=br == 1)
                    last.then_inc(a_pv[1], 1)

                scores(0)
                for h in range(NH):
                    if h + 1 < NH:
                        scores(h + 1)
                    values(h)

            def decode_k1(g):
                if g >= 1:
                    pe.wait_ge(r_ps[1], g)
                for b2 in range(2):
                    b = 2 * g + b2
                    lo = 64 * b2
                    for kp in range(2):
                        mm(ps[3][lo:lo + 64, 0:NCS], qb1[:, b, kp, :], kc[:, b, kp, :], start=kp == 0, stop=kp == 1)
                    for br in range(2):
                        for kp in range(2):
                            last = mm(ps[3][lo:lo + 64, 64 + 32 * br:96 + 32 * br], qb1[:, b, kp, :],
                                      kT[:, 2 * br + kp, TP:T], start=kp == 0, stop=kp == 1)
                last.then_inc(k_n[1], 1)
                for step in range(3):
                    if step < 2:
                        src = take(pe, "k1", 2 * g + step)
                    for i in range(6):
                        if step < 2:
                            n = (2 * g + step) * 6 + i
                            if n >= 2:
                                pe.wait_ge((k_a, k_d)[n % 2][2], n // 2)
                            for r in range(4):
                                a = ((4 * (i % 2) + r) * KVW + (i // 2) * P) if i < 4 else (NPG + r) * KVW + (i - 4) * P
                                last = turn(ps[6 + n % 2][:, r * P:(r + 1) * P], src[:, a:a + P])
                            last.then_inc(k_p[2], 1)
                        if step >= 1:
                            b2 = step - 1
                            b = 2 * g + b2
                            n = b * 6 + i
                            pe.wait_ge((k_a, k_d)[n % 2][2], n // 2 + 1)
                            kp, bank = (i // 2, i % 2) if i < 4 else (i - 4, 2)
                            mm(ps[bank][64 * b2:64 * b2 + 64, :], qb1[:, b, kp, :], KT[:, b % 2, i, :],
                               start=kp == 0, stop=kp == 1).then_inc(k_s[1], 1)
                pe.wait_ge(i_w, g + 1)
                if g >= 3:
                    pe.wait_ge(v_e[1], g - 2)
                mm(ps[4][:, 0:64], C("group"), R[:, 2, (g % 2) * 256:(g % 2) * 256 + 64], start=True, stop=True).then_inc(i_p, 1)

            def decode_v1(g):
                pe.wait_ge(r_w[1], g + 1)
                for i in range(4):
                    n = 4 * g + i
                    if n >= 2:
                        pe.wait_ge(r_te[1], n - 1)
                    bank = ps[6 + i % 2]
                    if i < 3:
                        for c in range(4):
                            j = 4 * i + c
                            src = R[:, 0, j * P:(j + 1) * P] if j < 8 else R[:, 1, (j - 8) * P:(j - 7) * P]
                            last = turn(bank[:, c * P:(c + 1) * P], src)
                    else:
                        turn(bank[0:TS, 0:P], R[:, 0, PAST:PAST + TS])
                        turn(bank[0:TS, P:2 * P], R[:, 1, WIN:WIN + TS])
                        a = (g % 2) * 256 + 128
                        last = turn(bank[0:NCS, 2 * P:3 * P], R[:, 2, a:a + NCS])
                    last.then_inc(r_t[1], 1)
                pe.wait_ge(r_te[1], 4 * (g + 1))
                for b2 in range(2):
                    b = 2 * g + b2
                    lo = 64 * b2
                    o = ps[5][lo:lo + 64, 0:KVW]
                    if b2 == 0 and g >= 1:
                        pe.wait_ge(v_x[1], g)
                    src = take(pe, "v1", b)
                    for j in range(12):
                        mm(o, PT1[:, j, lo:lo + 64], src[:, j * KVW:(j + 1) * KVW], start=j == 0, stop=False)
                    for br in range(2):
                        v = NQ1 + (3 + 2 * br) * KVW
                        mm(o, PT1[0:TS, 12 + br, lo:lo + 64], proj[0:TS, 2, v:v + KVW], start=False, stop=False)
                    mm(o, PT1[0:NCS, 14, lo:lo + 64], vc[0:NCS, b, :], start=False, stop=True).then_inc(v_c[1], 1)

            norm(0)
            project_in(0)
            turn_qk(0)
            prompt0()
            decode_k0()
            for g in range(2):
                decode_v0(g)
            turn_o(0, 3)
            pe.wait_ge(a_oe[0], 8)
            pe.wait_ge(v_e[0], 4)
            project_out(0)
            norm(1)
            ffn(0)
            compress_cache()
            norm(2)
            project_in(1)
            turn_qk(1)
            compress_prompt()
            prompt1()
            pe.wait_ge(a_oe[1], 8)
            pe.wait_ge(qb_d[1], 1)
            decode_k1(0)
            for g in range(4):
                if g < 3:
                    decode_k1(g + 1)
                if g >= 1:
                    turn_o(1, g - 1)
                decode_v1(g)
            turn_o(1, 3)
            pe.wait_ge(v_e[1], 4)
            project_out(1)
            norm(3)
            ffn(1)
            pe.wait_ge(d_e[1], KD)
            for t in range(3):
                for j in range(2):
                    for i in range(4):
                        last = turn(ps[2 * t + j][0:WT[t], i * P:(i + 1) * P], hT[:, 4 * j + i, t * P:t * P + WT[t]])
                    last.then_inc(y_t, 1)

        @block.scalar
        def _(act):
            f = nc.scalar.activation

            def copy(out, in_):
                return f(out, in_, ACT.Copy)

            for t in range(3):
                for j in range(2):
                    act.wait_ge(x_t, 2 * t + j + 1)
                    v = ps[2 * t + j][:, :].rearrange("p (i n) -> p i n", i=4)
                    copy(hT[:, 4 * j:4 * j + 4, t * P:t * P + WT[t]], v[:, :, 0:WT[t]]).then_inc(x_e, 1)

            def norm(i, ready, value):
                act.wait_ge(ready, value)
                if i == 2:
                    act.wait_ge(c_w, NB)
                for j in range(2):
                    f(sqT[:, 4 * j:4 * j + 4, :], hT[:, 4 * j:4 * j + 4, :], ACT.Square).then_inc(n_sq[i], 1)
                act.wait_ge(n_rc[i], 1)
                f(R[:, 1, 0:T], R[:, 0, 0:T], ACT.Sqrt).then_inc(n_rs[i], 1)

            def project_in(l):
                for n, w in enumerate(nin[l]):
                    for t in range(3):
                        act.wait_ge(in_p[l], 3 * n + t + 1)
                        copy(proj[0:WT[t], t, n * 512:n * 512 + w], ps[(n % 2) * 3 + t][0:WT[t], 0:w]).then_inc(in_e[l], 1)

            def roots(l):
                H = (16, 28)[l]
                for t in range(3):
                    act.wait_ge(q_rc[l], t + 1)
                    f(ss[0:WT[t], t, 0:H], ss[0:WT[t], t, 0:H], ACT.Sqrt).then_inc(q_rs[l], 1)

            def keep_qk(l):
                if l == 0:
                    i = 0
                    for t in range(3):
                        for dst, j in ((qT, 0), (qT, 4), (kT, 0), (kT, 4)):
                            act.wait_ge(t_p[0], i + 1)
                            v = ps[i % 6][:, :].rearrange("p (j n) -> p j n", j=4)
                            copy(dst[:, j:j + 4, t * P:t * P + WT[t]], v[:, :, 0:WT[t]]).then_inc(t_e[0], 1)
                            i += 1
                    return
                for i in range(11):
                    act.wait_ge(t_p[1], i + 1)
                    v = ps[i % 6][:, :].rearrange("p (j n) -> p j n", j=4)
                    if i < 6:
                        t, j = i // 2, 4 * (i % 2)
                        last = copy(qT[:, j:j + 4, t * P:t * P + WT[t]], v[:, :, 0:WT[t]])
                    elif i < 8:
                        t = i - 6
                        kd = kT[:, :, t * P:(t + 1) * P].rearrange("p (j e) n -> p j e n", e=2)
                        for e in range(2):
                            for dh in range(2):
                                last = copy(kd[dh * 64:dh * 64 + 64, :, e, :], v[e * 64:e * 64 + 64, :, :])
                    elif i == 8:
                        last = copy(kT[:, 0:4, TP:T], v[:, :, 0:TS])
                    else:
                        t = i - 9
                        xd = XTp[:, :, t * 64:(t + 1) * 64].rearrange("p (j e) n -> p j e n", e=2)
                        for e in range(2):
                            for par in range(2):
                                last = copy(xd[par * 64:par * 64 + 64, :, e, :], v[e * 64:e * 64 + 64, :, par::2])
                    last.then_inc(t_e[1], 1)

            def prompt0():
                def probs(h):
                    b = h % 2
                    act.wait_ge(a_s[0], h + 1)
                    if h < 8:
                        if h >= 2:
                            act.wait_ge(a_w[0], h - 1)
                        f(R[:, 0, b * 384:b * 384 + 384], ps[b][:, 0:384], ACT.Sigmoid, scale=SC)
                        f(R[:, 1, b * 384:b * 384 + 384], ps[b][:, 0:384], ACT.Sigmoid, scale=-SC).then_inc(a_g, 1)
                    else:
                        act.wait_ge(a_m[0], h - 7)
                        for t, (lo, hi) in enumerate(((0, 128), (128, 384))):
                            last = f(R[:, 1, b * 384 + lo:b * 384 + hi], R[:, 0, b * 384 + lo:b * 384 + hi], ACT.Exp,
                                     scale=SC, bias=st[:, 8 * b + 2 + t:8 * b + 3 + t], accum_out=st[:, 8 * b + 4 + t:8 * b + 5 + t])
                        last.then_inc(a_e[0], 1)

                def keep(h):
                    act.wait_ge(a_t[0], h + 1)
                    if h >= 2:
                        act.wait_ge(a_pv[0], h - 1)
                    copy(PTp[:, h % 2, 0:384], ps[2 + h % 2][:, 0:384]).then_inc(a_te[0], 1)
                    if h % 2 == 1:
                        act.wait_ge(a_pv[0], h + 1)
                        copy(oT[:, h // 2, 0:TP], ps[4 + (h // 2) % 2][:, 0:TP]).then_inc(a_oe[0], 1)

                probs(0)
                for h in range(NH):
                    if h + 1 < NH:
                        probs(h + 1)
                    keep(h)

            def keep_k0(g):
                for cc in range(9 * g, (9, 16)[g]):
                    for p in range(0, 8, 2):
                        i = cc * 8 + p
                        act.wait_ge(k_p[0], i + 1)
                        if cc >= 2:
                            act.wait_ge(k_s[0], 8 * (cc - 2) + p + 1)
                        copy(KT[:, cc % 2, p, :], ps[6][:, :]).then_inc(k_a[0], 1)

            def rows0(g):
                act.wait_ge(k_s[0], 64 * (g + 1))
                act.wait_ge(k_n[0], 4 * (g + 1))
                if g:
                    act.wait_ge(r_t[0], 6 * g)
                for row, s in ((0, SC), (1, -SC)):
                    for j in range(2):
                        f(R[:, row, j * 512:(j + 1) * 512], ps[j][:, :], ACT.Sigmoid, scale=s)
                    last = f(R[:, row, PAST:PAST + TS], ps[4][:, 0:32], ACT.Sigmoid, scale=s)
                last.then_inc(r_sg, 1)
                act.wait_ge(r_m[0], g + 1)
                f(R[:, 3, 0:PAST + TS], R[:, 3, 0:PAST + TS], ACT.Exp, scale=SC, bias=st[:, 40:41],
                  accum_out=st[:, 41:42]).then_inc(r_e[0], 1)

            def keep_o(l, i):
                act.wait_ge(v_t[l], i + 1)
                for b2 in range(2):
                    v = ps[4][0:64, P + 64 * b2:P + 64 * b2 + 64].rearrange("p (i e q) -> p i e q", e=2, q=NQ)
                    c = TP + (2 * i + b2) * NQ
                    for e in range(2):
                        last = copy(oT[e * 64:e * 64 + 64, :, c:c + NQ], v[:, :, e, :])
                last.then_inc(v_e[l], 1)

            def keep_p0(g):
                for i in range(6):
                    y, c0 = i // 3, 4 * (i % 3)
                    act.wait_ge(r_t[0], g * 6 + i + 1)
                    v = ps[6 + i % 2][:, :].rearrange("p (c n) -> p c n", c=4)
                    if i % 3 < 2:
                        last = copy(PT0[:, y, c0:c0 + 4, :], v)
                    else:
                        last = copy(PT0[0:TS, y, 8, :], v[0:TS, 0, :])
                    last.then_inc(r_te[0], 1)

            def ffn(l):
                for j in range(FT):
                    act.wait_ge(u_p[l], j + 1)
                    if j >= 2:
                        act.wait_ge(u_e[l], j - 1)
                    f(R[:, j % 2, 0:T], ps[2 * (j % 3)][:, 0:T], ACT.Silu).then_inc(u_a[l], 1)

            def compress_cache():
                act.wait_ge(c_be, 1)
                for bb in range(NB + 1):
                    for i in range(8):
                        if bb < NB and i % 2 == 0:
                            act.wait_ge(k_p[1], bb * 8 + i + 1)
                            if bb >= 2:
                                act.wait_ge(c_h, 4 * (bb - 1))
                            keep_pairs(f, copy, bb, i, ps[6]).then_inc(k_a[1], 1)
                        if bb >= 1 and i % 2 == 1:
                            b, j = bb - 1, i // 2
                            act.wait_ge(c_h, 4 * b + j + 1)
                            if b >= 1:
                                act.wait_ge(c_w, b)
                            f(hid[:, j, :], ps[j][:, 0:NKV * NCS], ACT.Silu, bias=cb[:, j:j + 1]).then_inc(c_he, 1)

            def keep_pairs(f_, cp, bb, i, bank):
                blk = i // 2
                for e in range(2):
                    for par in range(2):
                        last = cp(KT[par * 64:par * 64 + 64, bb % 2, 2 * blk + e, (i % 2) * 256:(i % 2) * 256 + 256],
                                  bank[e * 64:e * 64 + 64, par::2])
                return last

            def prompt1():
                for t in range(3):
                    last = f(gates[0:WT[t], t, :], proj[0:WT[t], t, N1 - 48:N1], ACT.Sigmoid)
                last.then_inc(g_s, 1)
                for j in range(4):
                    act.wait_ge(p_h, j + 1)
                    f(hidp[:, j, :], ps[j][:, 0:NKV * NCP], ACT.Silu, bias=cb[:, j:j + 1]).then_inc(p_he, 1)

                def probs(h):
                    act.wait_ge(a_m[1], h + 1)
                    W, b = R[:, h % 2, :], 24 * (h % 2)
                    for j, (lo, hi) in enumerate(((0, 128), (128, 384), (384, 512), (512, 768), (768, 783), (783, 798))):
                        last = f(W[:, lo:hi], W[:, lo:hi], ACT.Exp, scale=SC, bias=st[:, b + 6 + j:b + 7 + j],
                                 accum_out=st[:, b + 12 + j:b + 13 + j])
                    last.then_inc(a_e[1], 1)

                def keep(h):
                    act.wait_ge(a_t[1], h + 1)
                    if h >= 2:
                        act.wait_ge(a_pv[1], h - 1)
                    X = PTp[:, h % 2, :]
                    copy(X[:, 0:384], ps[4][:, 0:384])
                    copy(X[:, 384:768], ps[5][:, 0:384])
                    copy(X[0:NCP, 768:1024], ps[6][0:NCP, 0:256]).then_inc(a_te[1], 1)
                    if h % 2 == 1:
                        act.wait_ge(a_pv[1], h + 1)
                        copy(oT[:, h // 2, 0:TP], ps[7][:, 0:TP]).then_inc(a_oe[1], 1)

                probs(0)
                for h in range(NH):
                    if h + 1 < NH:
                        probs(h + 1)
                    keep(h)

            def rows1(g):
                a = (g % 2) * 256
                act.wait_ge(i_m, g + 1)
                f(R[:, 2, a + 1:a + 1 + NCS], ps[3][:, 0:NCS], ACT.Exp, scale=SC, bias=st[:, 52:53],
                  accum_out=st[:, 53:54]).then_inc(i_e, 1)
                act.wait_ge(r_m[1], g + 1)
                f(R[:, 0, 0:PAST + TS], R[:, 0, 0:PAST + TS], ACT.Exp, scale=SC, bias=st[:, 56:57], accum_out=st[:, 58:59])
                f(R[:, 1, 0:WIN + TS], R[:, 1, 0:WIN + TS], ACT.Exp, scale=SC, bias=st[:, 57:58],
                  accum_out=st[:, 59:60]).then_inc(r_e[1], 1)

            def keep_k1(g):
                for b in (2 * g, 2 * g + 1):
                    for i in range(0, 6, 2):
                        n = b * 6 + i
                        act.wait_ge(k_p[2], n + 1)
                        if b >= 2:
                            act.wait_ge(k_s[1], 6 * (b - 2) + i + 1)
                        copy(KT[:, b % 2, i, :], ps[6][:, :]).then_inc(k_a[2], 1)

            def keep_p1(g):
                for i in range(4):
                    act.wait_ge(r_t[1], 4 * g + i + 1)
                    v = ps[6 + i % 2][:, :].rearrange("p (c n) -> p c n", c=4)
                    if i < 3:
                        last = copy(PT1[:, 4 * i:4 * i + 4, :], v)
                    else:
                        copy(PT1[0:TS, 12:14, :], v[0:TS, 0:2, :])
                        last = copy(PT1[0:NCS, 14, :], v[0:NCS, 2, :])
                    last.then_inc(r_te[1], 1)

            act.wait_ge(s_const, 80)
            norm(0, x_e, 6)
            project_in(0)
            roots(0)
            keep_qk(0)
            prompt0()
            keep_k0(0)
            rows0(0)
            keep_k0(1)
            keep_p0(0)
            rows0(1)
            keep_o(0, 0)
            keep_p0(1)
            for i in range(1, 4):
                keep_o(0, i)
            norm(1, o_e[0], KD)
            ffn(0)
            compress_cache()
            norm(2, d_e[0], KD)
            project_in(1)
            roots(1)
            keep_qk(1)
            prompt1()
            keep_k1(0)
            rows1(0)
            for g in range(4):
                if g < 3:
                    keep_k1(g + 1)
                    a = ((g + 1) % 2) * 256
                    act.wait_ge(i_m, g + 2)
                    f(R[:, 2, a + 1:a + 1 + NCS], ps[3][:, 0:NCS], ACT.Exp, scale=SC, bias=st[:, 52:53],
                      accum_out=st[:, 53:54]).then_inc(i_e, 1)
                if g >= 1:
                    keep_o(1, g - 1)
                keep_p1(g)
                if g < 3:
                    act.wait_ge(r_m[1], g + 2)
                    f(R[:, 0, 0:PAST + TS], R[:, 0, 0:PAST + TS], ACT.Exp, scale=SC, bias=st[:, 56:57], accum_out=st[:, 58:59])
                    f(R[:, 1, 0:WIN + TS], R[:, 1, 0:WIN + TS], ACT.Exp, scale=SC, bias=st[:, 57:58],
                      accum_out=st[:, 59:60]).then_inc(r_e[1], 1)
            keep_o(1, 3)
            norm(3, o_e[1], KD)
            ffn(1)
            for t in range(3):
                for j in range(2):
                    act.wait_ge(y_t, 2 * t + j + 1)
                    if t == 0 and j == 0:
                        act.wait_ge(s_kv, 48 + 16 * 5 + 16 * NB)
                    copy(proj[0:WT[t], t, j * 512:(j + 1) * 512], ps[2 * t + j][0:WT[t], :]).then_inc(y_e, 1)

        @block.vector
        def _(dve):
            v = nc.vector
            chained = [0]

            def link(ins):
                chained[0] += 1
                ins.then_inc(ch, 1)
                dve.wait_ge(ch, chained[0])

            tt, ts = v.tensor_tensor, v.tensor_scalar

            def norm(i):
                dve.wait_ge(n_ps[i], 1)
                link(ts(R[:, 2, 0:T], ps[7][:, 0:T], EPS, None, ALU.add))
                v.reciprocal(R[:, 0, 0:T], R[:, 2, 0:T]).then_inc(n_rc[i], 1)
                dve.wait_ge(n_rs[i], 1)
                for k in range(KD):
                    v.scalar_tensor_tensor(xT[:, k, :], hT[:, k, :], gc[:, i * KD + k:i * KD + k + 1], R[:, 1, 0:T],
                                           ALU.mult, ALU.mult).then_inc(n_x[i], 1)

            def norm_rope(l):
                groups = [[(512, 8, 0), (1536, 8, 1)],
                          [(0, 16, 2), (NQ1, 4, 3), (NQ1 + 2 * KVW, 4, 4), (NQ1 + 4 * KVW, 4, 5)]][l]
                dve.wait_ge(in_e[l], 3 * len(nin[l]))
                A, B = R[:, 0, 0:1024], R[:, 1, 0:1024]
                for t in range(3):
                    w, h0 = WT[t], 0
                    for c, H, g in groups:
                        X = proj[0:w, t, c:c + H * HD]
                        link(tt(A[0:w, 0:H * HD], X, X, ALU.mult))
                        link(v.reduce_sum(ss[0:w, t, h0:h0 + H], A[0:w, 0:H * HD].rearrange("p (h d) -> p h d", h=H), AX))
                        h0 += H
                    link(ts(ss[0:w, t, 0:h0], ss[0:w, t, 0:h0], 1.0 / HD, EPS, ALU.mult, ALU.add))
                    v.reciprocal(ss[0:w, t, 0:h0], ss[0:w, t, 0:h0]).then_inc(q_rc[l], 1)
                for t in range(3):
                    w, h0 = WT[t], 0
                    dve.wait_ge(q_rs[l], t + 1)
                    for j, (c, H, g) in enumerate(groups):
                        X = proj[0:w, t, c:c + H * HD].rearrange("p (h d) -> p h d", h=H)
                        a = A[0:w, 0:H * HD].rearrange("p (h d) -> p h d", h=H)
                        b = B[0:w, 0:H * HD].rearrange("p (h d) -> p h d", h=H)
                        co, si = C("cos", t * HD, (t + 1) * HD, w), C("sin", t * HD, (t + 1) * HD, w)
                        link(tt(X, X, rep(ss[0:w, t, h0:h0 + H], 2, HD), ALU.mult))
                        link(tt(X, X, rep(gr[0:w, g * HD:(g + 1) * HD], 1, H), ALU.mult))
                        tt(a, X, rep(co, 1, H), ALU.mult)
                        tt(b[:, :, 0:32], X[:, :, 32:64], rep(si[:, 0:32], 1, H), ALU.mult)
                        link(tt(b[:, :, 32:64], X[:, :, 0:32], rep(si[:, 32:64], 1, H), ALU.mult))
                        last = tt(X, a, b, ALU.add)
                        h0 += H
                        if j == len(groups) - 1:
                            last.then_inc(q_d[l], 1)
                        else:
                            link(last)

            def prompt0():
                for b in range(2):
                    E = R[:, 2, b * 400:b * 400 + 386]
                    v.memset(E[:, 128:129], 1.0)
                    link(v.memset(E[:, 385:386], 1.0))
                for h in range(NH):
                    b = h % 2
                    S, K, W = (R[:, r, b * 384:b * 384 + 384] for r in (0, 1, 3))
                    E = R[:, 2, b * 400:b * 400 + 386]
                    if h < 8:
                        dve.wait_ge(a_g, h + 1)
                        if h >= 2:
                            dve.wait_ge(a_w[0], h - 1)
                        v.tensor_tensor_scan(E[:, 0:128][:, ::-1], K[:, 0:128][:, ::-1], C("notpast")[:, ::-1], 1.0, ALU.mult, ALU.max)
                        link(v.tensor_tensor_scan(E[:, 257:385][:, ::-1], K[:, 256:384][:, ::-1], C("notpast")[:, ::-1], 1.0,
                                                  ALU.mult, ALU.max))
                        v.tensor_tensor_scan(E[:, 129:257][:, ::-1], K[:, 128:256][:, ::-1], zero.broadcast_to([P, 128]),
                                             E[:, 257:258], ALU.mult, ALU.max)
                        tt(S[:, 0:128], S[:, 0:128], C("strict"), ALU.mult)
                        link(tt(S[:, 256:384], S[:, 256:384], C("strict"), ALU.mult))
                        if h >= 2:
                            dve.wait_ge(a_t[0], h - 1)
                        tt(W[:, 0:128], S[:, 0:128], E[:, 1:129], ALU.mult)
                        tt(W[:, 128:384], S[:, 128:384], E[:, 130:386], ALU.mult).then_inc(a_w[0], 1)
                    else:
                        dve.wait_ge(a_s[0], h + 1)
                        mx = st[:, 8 * b:8 * b + 2]
                        link(tt(S, ps[b][:, 0:384], C("causal"), ALU.add))
                        v.reduce_max(mx[:, 0:1], S[:, 0:128], AX)
                        link(v.reduce_max(mx[:, 1:2], S[:, 128:384], AX))
                        ts(st[:, 8 * b + 2:8 * b + 4], mx, -SC, None, ALU.mult).then_inc(a_m[0], 1)
                        dve.wait_ge(a_e[0], h - 7)
                        link(v.reciprocal(st[:, 8 * b + 6:8 * b + 8], st[:, 8 * b + 4:8 * b + 6]))
                        dve.wait_ge(a_t[0], h - 1)
                        ts(W[:, 0:128], K[:, 0:128], st[:, 8 * b + 6:8 * b + 7], None, ALU.mult)
                        ts(W[:, 128:384], K[:, 128:384], st[:, 8 * b + 7:8 * b + 8], None, ALU.mult).then_inc(a_w[0], 1)

            def keep_k0(g):
                for cc in range(9 * g, (9, 16)[g]):
                    for p in range(1, 8, 2):
                        i = cc * 8 + p
                        dve.wait_ge(k_p[0], i + 1)
                        if cc >= 2:
                            dve.wait_ge(k_s[0], 8 * (cc - 2) + p + 1)
                        v.tensor_copy(KT[:, cc % 2, p, :], ps[7][:, :]).then_inc(k_d[0], 1)

            def drop_least(vals, n, neg):
                link(v.tensor_reduce(st[:, 42:43], vals, AX, ALU.min))
                link(v.scalar_tensor_tensor(st[:, 60:60 + n], vals, st[:, 42:43], C("rank", 0, n), ALU.is_le, ALU.mult))
                link(v.reduce_max(st[:, 43:44], st[:, 60:60 + n], AX))
                link(ts(neg, st[:, 60:60 + n], st[:, 43:44], NEG, ALU.is_ge, ALU.mult))

            def rows0(g):
                dve.wait_ge(k_s[0], 64 * (g + 1))
                dve.wait_ge(k_n[0], 4 * (g + 1))
                S, E = R[:, 3, :], R[:, 2, :]
                for j in range(2):
                    last = v.reduce_sum(st[:, 48 + 2 * j:50 + 2 * j], ps[2 + j][:, :].rearrange("p (n k) -> p n k", n=2), AX)
                link(last)
                drop_least(st[:, 48:52], 4, st[:, 76:80])
                if g:
                    dve.wait_ge(r_t[0], 6 * g)
                for j in range(4):
                    ts(S[:, j * 256:(j + 1) * 256], ps[2 + j // 2][:, (j % 2) * 256:(j % 2 + 1) * 256], st[:, 76 + j:77 + j],
                       None, ALU.add)
                dve.wait_ge(r_sg, g + 1)
                tt(S[:, PAST:PAST + TS], ps[4][:, 32:64], C("newneg0", g * TS, (g + 1) * TS), ALU.add).then_inc(r_ps[0], 1)
                dve.wait_ge(r_ps[0], g + 1)
                link(v.reduce_max(st[:, 44:45], S[:, 0:PAST + TS], AX))
                ts(st[:, 40:41], st[:, 44:45], -SC, None, ALU.mult).then_inc(r_m[0], 1)
                G, K = R[:, 0, :], R[:, 1, :]
                n = PAST + TS
                v.memset(E[:, n:n + 1], 1.0)
                link(tt(K[:, PAST:n], K[:, PAST:n], C("newnot", g * TS, (g + 1) * TS), ALU.max))
                v.tensor_tensor_scan(E[:, 0:n][:, ::-1], K[:, 0:n][:, ::-1], zero.broadcast_to([P, n]), 1.0, ALU.mult, ALU.max)
                link(tt(G[:, PAST:n], G[:, PAST:n], C("newpast", g * TS, (g + 1) * TS), ALU.mult))
                tt(G[:, 0:n], G[:, 0:n], E[:, 1:n + 1], ALU.mult).then_inc(r_w[0], 1)
                dve.wait_ge(r_e[0], g + 1)
                link(v.reciprocal(st[:, 45:46], st[:, 41:42]))
                ts(S[:, 0:n], S[:, 0:n], st[:, 45:46], None, ALU.mult).then_inc(r_w[0], 1)

            def pick(l, i):
                H = (8, NKV)[l]
                dve.wait_ge(v_c[l], (4 * (i + 1), 2 * (i + 1))[l])
                if i >= 2:
                    dve.wait_ge(v_t[l], i - 1)
                A = R[:, 2, 512:512 + H * HD]
                link(tt(A.rearrange("p (h d) -> p h d", h=H), ps[5][:, 0:H * HD].rearrange("p (h d) -> p h d", h=H),
                        rep(C(f"head{l}"), 2, HD), ALU.mult))
                v.reduce_sum(osm[:, i % 2, :], A.rearrange("p (h d) -> p d h", h=H), AX).then_inc(v_x[l], 1)

            def project_out(l):
                for i in range(KD):
                    dve.wait_ge(o_p[l], i + 1)
                    tt(hT[:, i, :], hT[:, i, :], ps[i % 4][:, 0:T], ALU.add).then_inc(o_e[l], 1)

            def ffn(l):
                for j in range(FT):
                    dve.wait_ge(u_a[l], j + 1)
                    tt(actT[:, j, :], R[:, j % 2, 0:T], ps[2 * (j % 3) + 1][:, 0:T], ALU.mult).then_inc(u_e[l], 1)
                for i in range(KD):
                    cg, j = i // 2, i % 2
                    dve.wait_ge(d_p[l], 2 * (cg + 1))
                    tt(hT[:, i, :], hT[:, i, :], ps[(cg % 2) * 2 + j][:, 0:T], ALU.add).then_inc(d_e[l], 1)

            def compress_cache():
                dve.wait_ge(c_b, 1)
                v.tensor_copy(cb[:, :], ps[4][:, 0:4]).then_inc(c_be, 1)

                def keep_second(b):
                    dve.wait_ge(c_w, b + 1)
                    v.tensor_copy(kc[:, b, :, :], ps[5][:, 0:2 * NCS].rearrange("p (i n) -> p i n", i=2))
                    v.tensor_copy(vc[0:NCS, b, :], ps[4][0:NCS, 0:KVW]).then_inc(c_we, 1)

                for bb in range(NB + 1):
                    for i in range(1, 8, 2):
                        if bb < NB:
                            dve.wait_ge(k_p[1], bb * 8 + i + 1)
                            if bb >= 2:
                                dve.wait_ge(c_h, 4 * (bb - 1))
                            blk = i // 2
                            for e in range(2):
                                for par in range(2):
                                    last = v.tensor_copy(KT[par * 64:par * 64 + 64, bb % 2, 2 * blk + e, 256:512],
                                                         ps[7][e * 64:e * 64 + 64, par::2])
                            last.then_inc(k_d[1], 1)
                        if bb >= 2 and i == 1:
                            keep_second(bb - 2)
                keep_second(NB - 1)

            def prompt1():
                dve.wait_ge(p_w, 1)
                v.tensor_copy(kcp[:, :, :], ps[5][:, 0:NKV * NCP].rearrange("p (h n) -> p h n", h=NKV))
                v.tensor_copy(vcp[0:NCP, :], ps[4][0:NCP, 0:KVW]).then_inc(p_we, 1)
                dve.wait_ge(g_s, 1)
                for t in range(2):
                    gv = gates[:, t, :].rearrange("p (h r) -> p h r", r=3)
                    for j, br in enumerate(GATE_ORDER):
                        if br:
                            last = v.tensor_copy(gp[:, :, 2 * j + t], gv[:, :, br])
                        else:
                            last = ts(gp[:, :, 2 * j + t], gv[:, :, br], C("cmpany", t, t + 1), None, ALU.mult)
                link(last)
                for h in range(NH):
                    W, b = R[:, h % 2, :], 24 * (h % 2)
                    A, B = ps[2 * (h % 2)], ps[2 * (h % 2) + 1]
                    dve.wait_ge(a_s[1], h + 1)
                    if h >= 2:
                        dve.wait_ge(a_t[1], h - 1)
                    tt(W[:, 0:384], A[:, 0:384], C("causal"), ALU.add)
                    tt(W[:, 384:768], B[:, 0:384], C("causal"), ALU.add)
                    link(tt(W[:, 768:798], A[:, 384:414], C("cmpcausal"), ALU.add))
                    two = W[:, 0:768].rearrange("p (r n) -> p r n", r=2)
                    cm = W[:, 768:798].rearrange("p (t n) -> p t n", t=2)
                    parts = ((two[:, :, 0:128], 0, 4, 2), (two[:, :, 128:384], 1, 4, 2), (cm, 4, 6, 1))
                    for x, lo, hi, step in parts:
                        last = v.reduce_max(st[:, b + lo:b + hi:step], x, AX)
                    link(last)
                    ts(st[:, b + 6:b + 12], st[:, b:b + 6], -SC, None, ALU.mult).then_inc(a_m[1], 1)
                    dve.wait_ge(a_e[1], h + 1)
                    link(v.reciprocal(st[:, b + 18:b + 24], st[:, b + 12:b + 18]))
                    link(tt(st[:, b + 18:b + 24], st[:, b + 18:b + 24], gp[:, h, :], ALU.mult))
                    for x, lo, hi, step in parts:
                        last = tt(x, x, rep(st[:, b + 18 + lo:b + 18 + hi:step], 2, x.shape[2]), ALU.mult)
                    last.then_inc(a_w[1], 1)

            def keep_k1(g):
                for b in (2 * g, 2 * g + 1):
                    for i in range(1, 6, 2):
                        n = b * 6 + i
                        dve.wait_ge(k_p[2], n + 1)
                        if b >= 2:
                            dve.wait_ge(k_s[1], 6 * (b - 2) + i + 1)
                        v.tensor_copy(KT[:, b % 2, i, :], ps[7][:, :]).then_inc(k_d[2], 1)

            def cmp_rows(g):
                a = (g % 2) * 256
                pc, pg = R[:, 2, a:a + 64], R[:, 2, a + 128:a + 128 + NCS]
                dve.wait_ge(k_n[1], g + 1)
                if g >= 2:
                    dve.wait_ge(r_t[1], 4 * (g - 1))
                v.memset(pc[:, 0:1], 0.0)
                link(v.reduce_max(st[:, 48:49], ps[3][:, 0:NCS], AX))
                ts(st[:, 52:53], st[:, 48:49], -SC, None, ALU.mult).then_inc(i_m, 1)
                dve.wait_ge(i_e, g + 1)
                link(v.reciprocal(st[:, 54:55], st[:, 53:54]))
                ts(pc[:, 1:64], pc[:, 1:64], st[:, 54:55], None, ALU.mult).then_inc(i_w, 1)
                dve.wait_ge(i_w, g + 1)
                link(ts(pg, pc[:, 1:64], gs[:, g, 0:1], None, ALU.mult))

            def rows1(g):
                dve.wait_ge(i_p, g + 1)
                link(v.reduce_sum(st[:, 0:16], ps[4][:, 0:64].rearrange("p (j c) -> p j c", c=4), AX))
                link(tt(st[:, 16:30], st[:, 1:15], ps[4][:, 8:61:4], ALU.add))
                v.memset(st[:, 76:77], 0.0)
                v.memset(st[:, 91:92], 0.0).then_inc(i_r, 1)
                drop_least(st[:, 16:30], 14, st[:, 77:91])
                dve.wait_ge(k_s[1], 12 * (g + 1))
                if g:
                    dve.wait_ge(r_t[1], 4 * g)
                S, W = R[:, 0, :], R[:, 1, :]
                for j in range(2):
                    tt(S[:, j * 512:(j + 1) * 512].rearrange("p (n k) -> p n k", n=8),
                       ps[j][:, :].rearrange("p (n k) -> p n k", n=8), rep(st[:, 76 + 8 * j:84 + 8 * j], 2, HD), ALU.add)
                new = C("newneg1", g * TS, (g + 1) * TS)
                tt(S[:, PAST:PAST + TS], ps[3][:, 64:96], new, ALU.add)
                tt(W[:, 0:NQ], ps[2][:, 0:NQ], C("winneg"), ALU.add)
                v.tensor_copy(W[:, NQ:WIN], ps[2][:, NQ:WIN])
                tt(W[:, WIN:WIN + TS], ps[3][:, 96:128], new, ALU.add).then_inc(r_ps[1], 1)
                dve.wait_ge(r_ps[1], g + 1)
                v.reduce_max(st[:, 48:49], S[:, 0:PAST + TS], AX)
                link(v.reduce_max(st[:, 49:50], W[:, 0:WIN + TS], AX))
                ts(st[:, 56:58], st[:, 48:50], -SC, None, ALU.mult).then_inc(r_m[1], 1)
                dve.wait_ge(r_e[1], g + 1)
                link(v.reciprocal(st[:, 48:50], st[:, 58:60]))
                link(tt(st[:, 48:50], st[:, 48:50], gs[:, g, 1:3], ALU.mult))
                ts(S[:, 0:PAST + TS], S[:, 0:PAST + TS], st[:, 48:49], None, ALU.mult)
                ts(W[:, 0:WIN + TS], W[:, 0:WIN + TS], st[:, 49:50], None, ALU.mult).then_inc(r_w[1], 1)

            dve.wait_ge(s_const, 80)
            norm(0)
            norm_rope(0)
            prompt0()
            keep_k0(0)
            rows0(0)
            keep_k0(1)
            rows0(1)
            for i in range(4):
                pick(0, i)
            project_out(0)
            norm(1)
            ffn(0)
            compress_cache()
            norm(2)
            norm_rope(1)
            prompt1()
            dve.wait_ge(g_l, 64)
            keep_k1(0)
            cmp_rows(0)
            rows1(0)
            for g in range(4):
                if g < 3:
                    keep_k1(g + 1)
                    cmp_rows(g + 1)
                    rows1(g + 1)
                pick(1, g)
            project_out(1)
            norm(3)
            ffn(1)

        @block.gpsimd
        def _(pool):
            flat_state = state_win[0].rearrange("b w two h d -> b w (two h d)")
            flat_win = win_sample[0].rearrange("b w two h d -> b w (two h d)")
            pool.memset(pq[:], 0.0).then_inc(qb_z[0], 1)
            for b in range(NB):
                pool.dma_start(flat_win[b, 0:WIN - NQ, :], flat_state[b, NQ:WIN, :]).then_inc(s_out, 16)
            pool.wait_ge(q_d[0], 3)
            pool.wait_ge(in_e[0], 3 * len(nin[0]))
            kv = kv0_prompt[0, 0].rearrange("(t p) two h d -> t p (two h d)", p=P)
            for t in range(2):
                pool.dma_start(kv[t], proj[:, t, D:N0]).then_inc(s_kv, 16)
            pool.dma_start(kv0_sample[0].rearrange("b q two h d -> (b q) (two h d)"), proj[0:TS, 2, D:N0]).then_inc(s_kv, 16)
            pool.wait_ge(t_e[0], 12)
            pool.wait_ge(qb_z[0], 1)
            for p in range(8):
                for e in range(2):
                    h = 2 * (p % 4) + e
                    last = nc.gpsimd.tensor_copy(qb0[e * 64:e * 64 + 64, :, p, h * NQ:(h + 1) * NQ],
                                                 qT[e * 64:e * 64 + 64, p, TP:T].rearrange("p (b q) -> p b q", q=NQ))
            last.then_inc(qb_d[0], 1)
            pool.wait_ge(o_e[0], 1)
            nc.gpsimd.memset(pq[:, 0:1024], 0.0).then_inc(qb_z[1], 1)
            pool.wait_ge(q_d[1], 3)
            pool.wait_ge(in_e[1], 3 * len(nin[1]))
            for t in range(2):
                rows = slice(t * P, (t + 1) * P)
                pool.dma_start(kv1_prompt[0, 0, rows].rearrange("p k h d -> p (k h d)"), proj[:, t, NQ1:NQ1 + 4 * KVW]).then_inc(s_kv, 16)
                pool.dma_start(win_prompt[0, 0, rows].rearrange("p k h d -> p (k h d)"), proj[:, t, NQ1 + 4 * KVW:NQ1 + 6 * KVW]).then_inc(s_kv, 16)
            pool.dma_start(kv1_sample[0].rearrange("b q k h d -> (b q) (k h d)"), proj[0:TS, 2, NQ1:NQ1 + 4 * KVW]).then_inc(s_kv, 16)
            for b in range(NB):
                pool.dma_start(flat_win[b, WIN - NQ:WIN, :], proj[b * NQ:(b + 1) * NQ, 2, NQ1 + 4 * KVW:NQ1 + 6 * KVW]).then_inc(s_kv, 16)
            pool.wait_ge(g_s, 1)
            for b in range(NB):
                pool.dma_start(gate_scratch[b].rearrange("h q r -> q h r"),
                               gates[b * NQ:(b + 1) * NQ, 2, :].rearrange("q (h r) -> q h r", r=3)).then_inc(g_d, 16)
            pool.wait_ge(g_d, 16 * NB)
            rows = gate_scratch.rearrange("b h q r -> (b h q) r")
            for g in range(4):
                pool.dma_start(gs[:, g, :], rows[g * P:(g + 1) * P, :]).then_inc(g_l, 16)
            pool.wait_ge(t_e[1], 11)
            pool.wait_ge(qb_z[1], 1)
            for h in range(NH):
                kvh = h // 4
                kp, e, s = kvh // 2, kvh % 2, h % 2
                last = nc.gpsimd.tensor_copy(qb1[e * 64:e * 64 + 64, :, kp, h * NQ:(h + 1) * NQ],
                                             qT[s * 64:s * 64 + 64, h // 2, TP:T].rearrange("p (b q) -> p b q", q=NQ))
            last.then_inc(qb_d[1], 1)
            yp = y_prompt[0].rearrange("(t p) d -> t p d", p=P)
            for t in range(2):
                pool.wait_ge(y_e, 2 * t + 2)
                pool.dma_start(yp[t], proj[:, t, 0:D]).then_inc(s_out, 16)
            pool.wait_ge(y_e, 6)
            pool.dma_start(y_sample.rearrange("b q d -> (b q) d"), proj[0:TS, 2, 0:D]).then_inc(s_out, 16)
            pool.wait_ge(s_out, 16 * (NB + 3))
            pool.wait_ge(s_kv, 48 + 16 * 5 + 16 * NB)


_OUTS = [(1, TP, D), (NB, NQ, D), (1, 1, TP, 2, NH, HD), (1, NB, NQ, 2, NH, HD), (1, 1, TP, 4, NKV, HD),
         (1, NB, NQ, 4, NKV, HD), (1, 1, TP, 2, NKV, HD), (1, NB, WIN, 2, NKV, HD)]
_INS = ["x_prompt", "x_sample", "cache_kv0", "cache_kv1", "state_win", "page_table", "w_in0", "w_out0", "w_in1",
        "w_out1", "cmp_w1", "cmp_w2", "w_gu", "w_down"]


def kernel(**inputs):
    import concourse.bacc as _bacc
    from concourse.bass_utils import run_bass_kernel_spmd as _run

    nc = _bacc.Bacc("TRN2", target_bir_lowering=False, num_devices=1)
    table, off = constants()
    arrays = {n: np.ascontiguousarray(inputs[n]) for n in _INS}
    arrays["consts"] = table
    g = [inputs["g_mix0"][0], inputs["g_ffn"][0], inputs["g_mix1"][0], inputs["g_ffn"][1]]
    arrays["gcol"] = np.ascontiguousarray(np.concatenate([np.asarray(a).reshape(KD, P).T for a in g], 1))
    r = [inputs["g_q0"][0], inputs["g_k0"][0], inputs["g_q1"][0]] + [inputs["g_k1"][0, i] for i in range(3)]
    arrays["grow"] = np.ascontiguousarray(np.broadcast_to(np.concatenate([np.asarray(a) for a in r])[None, :], (P, 6 * HD)))
    pe = np.asarray(inputs["cmp_pe"])[0].reshape(2, 16, P)
    arrays["pecol"] = np.ascontiguousarray(pe.transpose(2, 0, 1).reshape(P, 32))
    args = [nc.dram_tensor("in_" + n, a.shape, mybir.dt.from_np(a.dtype), kind="ExternalInput").ap() for n, a in arrays.items()]
    args += [nc.dram_tensor(f"out_{i}", s, F32, kind="ExternalOutput").ap() for i, s in enumerate(_OUTS)]
    args.append(nc.dram_tensor("gate_scratch", (NB, NH, NQ, 3), F32, kind="Internal").ap())
    trunk(nc, off, *args)
    res = _run(nc, [{"in_" + n: a for n, a in arrays.items()}], core_ids=[0])
    return tuple(res.results[0][f"out_{i}"] for i in range(len(_OUTS)))
```

```python
from contextlib import ExitStack

import concourse.bass as bass
from concourse import mybir
import numpy as np

F32 = mybir.dt.float32
I32 = mybir.dt.int32
ALU = mybir.AluOpType
ACT = mybir.ActivationFunctionType
AX = mybir.AxisListType.X

P = 128
D = 1024
KD = D // P
TP, NB, NQ = 256, 8, 4
TS = NB * NQ
T = TP + TS
PAST, PAGE = 1024, 128
NPG = PAST // PAGE
HD, NH, NKV = 64, 16, 4
DFF = 2816
FT = DFF // P
N0 = 3 * NH * HD
NQ1 = NH * HD
N1 = NQ1 + 6 * NKV * HD + 3 * NH
KVW = NKV * HD
WIN = 512
NWB = WIN // P
NCS = PAST // 16 - 1
NCP = TP // 16 - 1
CH = 256
EPS = 1e-6
SC = HD ** -0.5
NEG = -1e30
WT = (P, P, TS)
SLOTS = 3
SLOTW = 4096
RW = 1060
GATE_ORDER = (1, 2, 0)


def constants():
    c = {}
    c["ident"] = np.eye(P)
    c["mean"] = np.full((P, P), 1.0 / D)
    r = np.arange(P)
    same = (r[:, None] // 16 == r[None, :] // 16) & (r[:, None] % 4 == r[None, :] % 4)
    c["group"] = same * 1.0
    q = r[:, None]
    k = np.arange(P)[None, :]
    diag = np.where(k <= q, 0.0, NEG)
    c["causal"] = np.concatenate([diag, np.zeros((P, P)), diag], 1)
    c["strict"] = (k < q) * 1.0
    c["notpast"] = (k >= q) * 1.0
    half = HD // 2
    inv = np.power(np.float32(10000.0), -np.arange(half, dtype=np.float32) / np.float32(half)).astype(np.float32)
    pos = np.stack([r, P + r, PAST + r % NQ], 1).astype(np.float32)
    ang = (pos[:, :, None] * inv[None, None, :]).astype(np.float32)
    co, si = np.cos(ang).astype(np.float32), np.sin(ang).astype(np.float32)
    c["cos"] = np.concatenate([co, co], 2).reshape(P, -1)
    c["sin"] = np.concatenate([-si, si], 2).reshape(P, -1)
    n = np.arange(NCP)[None, :]
    c["cmpcausal"] = np.concatenate([np.where(16 * n + 31 <= q + P * t, 0.0, NEG) for t in range(2)], 1)
    c["cmpany"] = np.concatenate([(q + P * t >= 31) * 1.0 for t in range(2)], 1)
    tok = np.arange(TS)[None, :]
    for name, per in (("0", 32), ("1", 64)):
        ok, past = [], []
        for g in range(NB * per // P):
            b = g * (P // per) + q // per
            ok.append((tok // NQ == b) & (tok % NQ <= q % NQ))
            past.append((tok // NQ == b) & (tok % NQ < q % NQ))
        c["newneg" + name] = np.where(np.concatenate(ok, 1), 0.0, NEG)
        if name == "0":
            c["newpast"] = np.concatenate(past, 1) * 1.0
            c["newnot"] = 1.0 - c["newpast"]
    c["winneg"] = np.where(np.arange(NQ)[None, :] > q % NQ, 0.0, NEG)
    c["head0"] = (np.arange(8)[None, :] == (q % 32) // 4) * 1.0
    c["head1"] = (np.arange(NKV)[None, :] == (q % 64) // 16) * 1.0
    c["rank"] = np.broadcast_to(np.arange(1, 17)[None, :], (P, 16))
    at, off = 0, {}
    for name, a in c.items():
        off[name] = (at, a.shape[1])
        at += a.shape[1]
    return np.ascontiguousarray(np.concatenate(list(c.values()), 1).astype(np.float32)), off


def trunk(nc, off, x_prompt, x_sample, cache_kv0, cache_kv1, state_win, page_table, w_in0, w_out0, w_in1, w_out1,
          cmp_w1, cmp_w2, w_gu, w_down, consts, gcol, grow, pecol,
          y_prompt, y_sample, kv0_prompt, kv0_sample, kv1_prompt, kv1_sample, win_prompt, win_sample, gate_scratch):
    ctx = ExitStack()
    with ctx:
        def sb(name, cols, dt=F32, rows=P):
            return ctx.enter_context(nc.sbuf_tensor(name, [rows, cols], dt))

        def sem(name):
            return ctx.enter_context(nc.semaphore(name))

        hT = sb("hT", KD * T)[:].rearrange("p (k t) -> p k t", t=T)
        xT = sb("xT", KD * T)[:].rearrange("p (k t) -> p k t", t=T)
        oT = xT
        ring = sb("ring", SLOTS * SLOTW)[:].rearrange("p (s n) -> p s n", s=SLOTS)
        proj_t = sb("proj", 3 * N0)
        proj = proj_t[:].rearrange("p (t n) -> p t n", t=3)
        w1r = proj_t[:, 0:2 * 16 * CH].rearrange("p (k i n) -> p k i n", k=2, i=16)
        qT = sb("qT", KD * T)[:].rearrange("p (k t) -> p k t", t=T)
        kT = sb("kT", KD * T)[:].rearrange("p (k t) -> p k t", t=T)
        x2T, sqT = qT, kT
        big = sb("big", 2 * 8 * 512)
        KT = big[:].rearrange("p (b i n) -> p b i n", b=2, i=8)
        actT = big[:, 0:FT * T].rearrange("p (f t) -> p f t", t=T)
        XTp = big[:, 0:8 * P].rearrange("p (i n) -> p i n", i=8)
        PTp = big[:, 2048:4096].rearrange("p (b n) -> p b n", b=2)
        R = sb("rows", 4 * RW)[:].rearrange("p (r n) -> p r n", r=4)
        pq = sb("pq", 2944)
        qb0 = pq[:, 0:2048].rearrange("p (b i c) -> p b i c", b=NB, i=8)
        PT0 = pq[:, 0:2304].rearrange("p (y c n) -> p y c n", y=2, c=9)
        qb1 = pq[:, 0:1024].rearrange("p (b i c) -> p b i c", b=NB, i=2)
        PT1 = pq[:, 1024:2944].rearrange("p (j n) -> p j n", j=15)
        hid = pq[:, 1024:1024 + 4 * 252].rearrange("p (j n) -> p j n", j=4)
        hidp = pq[:, 1024:1024 + 4 * 60].rearrange("p (j n) -> p j n", j=4)
        kc = sb("kc", NB * 2 * NCS)[:].rearrange("p (b i n) -> p b i n", b=NB, i=2)
        vc = sb("vc", NB * KVW)[:].rearrange("p (b n) -> p b n", b=NB)
        kcp = sb("kcp", NKV * NCP)[:].rearrange("p (h n) -> p h n", h=NKV)
        vcp = sb("vcp", KVW)
        w2 = sb("w2", 4 * HD)[:].rearrange("p (k h n) -> p k h n", k=2, h=2)
        ct = sb("ct", sum(n for _, n in off.values()))
        gc = sb("gc", 4 * KD)
        gr = sb("gr", 6 * HD)
        pec = sb("pec", 32)
        cb = sb("cb", 4)
        rt = sb("rt", 3)
        rst = R[:, 3, 0:T]
        smp = sb("smp", 2 * P)[:].rearrange("p (b n) -> p b n", b=2)
        pages = sb("pages", NB * NPG, I32, 1)
        ss = sb("ss", 3 * 28)[:].rearrange("p (t n) -> p t n", t=3)
        gates = sb("gates", 3 * 48)[:].rearrange("p (t n) -> p t n", t=3)
        gp = sb("gp", NH * 6)[:].rearrange("p (h n) -> p h n", h=NH)
        gs = sb("gs", 12)[:].rearrange("p (g n) -> p g n", g=4)
        st = sb("st", 96)
        osm = sb("osm", 2 * HD)[:].rearrange("p (b n) -> p b n", b=2)
        ps = [ctx.enter_context(nc.psum_tensor(f"ps{i}", [P, 512], F32)) for i in range(8)]

        def C(name, a=0, b=None, rows=P):
            o, n = off[name]
            return ct[0:rows, o + a:o + (n if b is None else b)]

        zero = C("causal", P, P + 1)
        ident = C("ident")

        def rep(ap, axis, n):
            a = ap.unsqueeze(axis)
            shape = list(a.shape)
            shape[axis] = n
            return a.broadcast_to(shape)

        s_page, s_x, s_const, s_kv, s_out, s_w1 = (sem(n) for n in ("s_page", "s_x", "s_const", "s_kv", "s_out", "s_w1"))
        s_slot = [sem(f"s_slot{i}") for i in range(SLOTS)]
        x_t, x_e, y_t, y_e = sem("x_turned"), sem("x_kept"), sem("y_turned"), sem("y_kept")
        n_sq = [sem(f"squares{i}") for i in range(4)]
        n_ps = [sem(f"meansq{i}") for i in range(4)]
        n_rc = [sem(f"recip{i}") for i in range(4)]
        n_rs = [sem(f"rstd{i}") for i in range(4)]
        n_x = [sem(f"normed{i}") for i in range(4)]
        L2 = range(2)
        in_p, in_e, in_q = ([sem(f"{n}{i}") for i in L2] for n in ("in_done", "in_kept", "in_sample_kept"))
        q_rc, q_rs, q_d = [sem(f"qk_recip{i}") for i in L2], [sem(f"qk_rstd{i}") for i in L2], [sem(f"roped{i}") for i in L2]
        t_p, t_e = [sem(f"qk_turned{i}") for i in L2], [sem(f"qk_kept{i}") for i in L2]
        a_s, a_g, a_m = [sem(f"pscores{i}") for i in L2], sem("psigmoids"), [sem(f"pmax{i}") for i in L2]
        a_e, a_w, a_t = [sem(f"pexp{i}") for i in L2], [sem(f"pweights{i}") for i in L2], [sem(f"pturned{i}") for i in L2]
        a_te, a_pv, a_oe = [sem(f"pkept{i}") for i in L2], [sem(f"pvdone{i}") for i in L2], [sem(f"pokept{i}") for i in L2]
        qb_z, qb_d = [sem(f"qb_zero{i}") for i in L2], [sem(f"qb_ready{i}") for i in L2]
        k_p, k_a, k_d = ([sem(f"{n}{i}") for i in range(3)] for n in ("k_turned", "k_kept_act", "k_kept_dve"))
        k_s, k_n = [sem(f"dscores{i}") for i in L2], [sem(f"dnew{i}") for i in L2]
        r_sg, r_ps = sem("dsigmoids"), [sem(f"scores_read{i}") for i in L2]
        r_m, r_e = [sem(f"dmax{i}") for i in L2], [sem(f"dexp{i}") for i in L2]
        r_w, r_t, r_te = [sem(f"dweights{i}") for i in L2], [sem(f"dturned{i}") for i in L2], [sem(f"dkept{i}") for i in L2]
        v_c, v_x = [sem(f"pv_chunk{i}") for i in L2], [sem(f"heads_picked{i}") for i in L2]
        v_t, v_e = [sem(f"o_turned{i}") for i in L2], [sem(f"o_kept{i}") for i in L2]
        i_m, i_e, i_w, i_p = sem("cmp_max"), sem("cmp_exp"), sem("cmp_probs"), sem("importance")
        i_r = sem("importance_read")
        c_b, c_be, c_h, c_he, c_w, c_we = (sem(n) for n in ("cmp_bias", "cmp_bias_kept", "cmp_hidden", "cmp_silu", "cmp_out", "cmp_kept"))
        p_h, p_he, p_w, p_we = (sem(n) for n in ("pcmp_hidden", "pcmp_silu", "pcmp_out", "pcmp_kept"))
        g_s, g_d, g_l, g_p = sem("gates_done"), sem("gates_stored"), sem("gates_rows"), sem("gates_prompt")
        o_p, o_e = [sem(f"out_done{i}") for i in L2], [sem(f"out_added{i}") for i in L2]
        u_p, u_g, u_u, u_a, u_e = ([sem(f"{n}{i}") for i in L2] for n in ("gu_done", "g_scaled", "u_scaled", "silu_done", "act_kept"))
        c_a = sem("pe_times_w1")
        d_p, d_e = [sem(f"down_done{i}") for i in L2], [sem(f"down_added{i}") for i in L2]
        ch = sem("vector_chain")

        nin = [[min(512, n - c) for c in range(0, n, 512)] for n in (N0, N1)]
        IN_ORDER = ([1, 3, 0, 2, 4, 5], [0, 1, 2, 3, 5, 4])
        ROPED = ([(1, 512, 8, 0), (3, 1536, 8, 1)],
                 [(0, 0, 8, 2), (1, 512, 8, 2), (2, NQ1, 4, 3), (3, NQ1 + 2 * KVW, 4, 4), (4, NQ1 + 4 * KVW, 4, 5)])

        def full_chunks(l, pos):
            return sum(nin[l][n] == 512 for n in IN_ORDER[l][:pos + 1])

        w_in = [w_in0[0].rearrange("(k p) n -> p k n", p=P), w_in1[0].rearrange("(k p) n -> p k n", p=P)]
        w_out = [w_out0[0].rearrange("(k p) n -> p k n", p=P), w_out1[0].rearrange("(k p) n -> p k n", p=P)]
        w1_h = cmp_w1[0].rearrange("k (i p) n -> p k i n", p=P)

        plan = []

        def slot_view(s, a, b, **kw):
            return ring[:, s, a:b]

        for i, n in enumerate(IN_ORDER[0]):
            plan.append((("in", 0, n), in_p[0], 3 * (i + 1)))
        for cc in range(16):
            plan.append((("k0", cc // 2, cc % 2), k_p[0], 8 * (cc + 1)))
        for cc in range(16):
            plan.append((("v0", cc // 2, cc % 2), v_c[0], cc + 1))

        def ffn_plan(l):
            for n in range(2):
                plan.append((("out", l, n), o_p[l], 4 * (n + 1)))
            for n in range(FT // 2):
                plan.append((("gu", l, n), u_p[l], 2 * (n + 1)))
                if l == 0 and n == 4:
                    plan.append((("w1r",), None, 0))
            for n in range(8):
                plan.append((("down", l, n), d_p[l], n + 1))

        ffn_plan(0)
        for b in range(NB):
            plan.append((("cmp", b), k_p[1], 8 * (b + 1)))
        for i, n in enumerate(IN_ORDER[1]):
            plan.append((("in", 1, n), in_p[1], 3 * (i + 1)))
        for k in range(2):
            plan.append((("w1", k), p_h, 2 * (k + 1)))
        order = [("k1", 0), ("k1", 1)]
        for g in range(4):
            if g < 3:
                order += [("k1", 2 * g + 2), ("k1", 2 * g + 3)]
            order += [("v1", 2 * g), ("v1", 2 * g + 1)]
        for kind, b in order:
            plan.append(((kind, b),) + ((k_p[2], 6 * (b + 1)) if kind == "k1" else (v_c[1], b + 1)))
        ffn_plan(1)

        place, landed, fill = {}, {}, [0] * SLOTS
        ringed = [e for e in plan if e[0] != ("w1r",)]

        def n_dmas(name):
            return {"k0": 4, "v0": 4, "gu": 2, "cmp": NPG, "k1": NPG + 1, "v1": NPG + 1}.get(name[0], 1)

        for i, e in enumerate(ringed):
            s = i % SLOTS
            fill[s] += 16 * n_dmas(e[0])
            place[e[0]], landed[e[0]] = s, fill[s]

        def take(eng, *name):
            s = place[name]
            eng.wait_ge(s_slot[s], landed[name])
            return ring[:, s, :]

        block = ctx.enter_context(nc.Block())

        @block.sync
        def _(sp):
            sp.dma_start(pages[:], page_table.rearrange("b n -> (b n)").unsqueeze(0)).then_inc(s_page, 16)
            sp.dma_start(ct[:], consts).then_inc(s_const, 16)
            for t in range(2):
                sp.dma_start(proj[:, t, 0:D], x_prompt[0, t * P:(t + 1) * P, :]).then_inc(s_x, 16)
            sp.dma_start(proj[0:TS, 2, 0:D], x_sample.rearrange("b q d -> (b q) d")).then_inc(s_x, 16)
            sp.dma_start(gc[:], gcol).then_inc(s_const, 16)
            sp.dma_start(gr[:], grow).then_inc(s_const, 16)
            sp.dma_start(pec[:], pecol).then_inc(s_const, 16)
            sp.dma_start(w2[:, :, :, :], cmp_w2[0].rearrange("k (h p) n -> p k h n", p=P)).then_inc(s_const, 16)
            sp.wait_ge(s_page, 16)

            def page(b, pg):
                return bass.ds(sp.value_load(pages[0:1, b * NPG + pg:b * NPG + pg + 1], min_val=0,
                                             max_val=cache_kv0.shape[1] - 1), 1)

            i = 0
            for name, _, _ in plan:
                kind = name[0]
                if kind == "w1r":
                    sp.wait_ge(o_p[0], 1)
                    sp.wait_ge(s_kv, 48)
                    sp.dma_start(w1r[:, 0], w1_h[:, 0]).then_inc(s_w1, 16)
                    sp.dma_start(w1r[:, 1], w1_h[:, 1]).then_inc(s_w1, 16)
                    continue
                if i >= SLOTS:
                    _, freed, value = ringed[i - SLOTS]
                    sp.wait_ge(freed, value)
                s = i % SLOTS
                slot = ring[:, s, :]
                i += 1
                if kind == "in":
                    l, n = name[1:]
                    w = nin[l][n]
                    jobs = [(slot[:, 0:8 * w].rearrange("p (k n) -> p k n", k=8), w_in[l][:, :, n * 512:n * 512 + w])]
                elif kind == "out":
                    l, n = name[1:]
                    jobs = [(slot.rearrange("p (k n) -> p k n", k=8), w_out[l][:, :, n * 512:(n + 1) * 512])]
                elif kind == "gu":
                    l, n = name[1:]
                    w = w_gu[l].rearrange("(k p) n -> p k n", p=P)
                    d = slot.rearrange("p (k n) -> p k n", k=8)
                    jobs = [(d[:, :, j * 256:(j + 1) * 256], w[:, :, j * DFF + n * 256:j * DFF + (n + 1) * 256])
                            for j in range(2)]
                elif kind == "down":
                    l, n = name[1:]
                    w = w_down[l].rearrange("(k p) n -> p k n", p=P)
                    jobs = [(slot[:, 0:11 * 256].rearrange("p (k n) -> p k n", k=11),
                             w[:, (n % 2) * 11:(n % 2 + 1) * 11, (n // 2) * 256:(n // 2 + 1) * 256])]
                elif kind in ("k0", "v0"):
                    b, half = name[1:]
                    c = cache_kv0[0].rearrange("g s two h d -> g s two (h d)")
                    jobs = [(slot[:, r * D:(r + 1) * D], (c, b, half * 4 + r, int(kind == "v0"))) for r in range(4)]
                elif kind == "cmp":
                    c = cache_kv1[0].rearrange("g s (two kv) h d -> g s two (kv h d)", two=2)
                    jobs = [(slot[:, r * 512:(r + 1) * 512], (c, name[1], r, 0)) for r in range(NPG)]
                elif kind in ("k1", "v1"):
                    b, v = name[1], int(kind == "v1")
                    c = cache_kv1[0].rearrange("g s kv h d -> g s kv (h d)")
                    jobs = [(slot[:, r * KVW:(r + 1) * KVW], (c, b, r, 2 + v)) for r in range(NPG)]
                    jobs.append((slot[:, NPG * KVW:(NPG + NWB) * KVW].rearrange("p (r n) -> p r n", r=NWB),
                                 state_win[0, b].rearrange("(r p) two h d -> p r two (h d)", p=P)[:, :, v, :]))
                else:
                    jobs = [(slot.rearrange("p (i n) -> p i n", i=16), w1_h[:, name[1]])]
                assert len(jobs) == n_dmas(name)
                for dst, src in jobs:
                    if isinstance(src, tuple):
                        c, b, pg, part = src
                        src = c[page(b, pg), :, part, :].rearrange("g s n -> (g s) n")
                    sp.dma_start(dst, src).then_inc(s_slot[s], 16)

        @block.tensor
        def _(pe):
            mm = nc.tensor.matmul

            def turn(out, in_, rows=P):
                return nc.tensor.transpose(out, in_, C("ident", 0, rows, rows))

            pe.wait_ge(s_x, 48)
            pe.wait_ge(s_const, 80)
            for t in range(3):
                for j in range(2):
                    for i in range(4):
                        last = turn(ps[2 * t + j][:, i * P:i * P + WT[t]],
                                    proj[0:WT[t], t, (4 * j + i) * P:(4 * j + i + 1) * P], WT[t])
                    last.then_inc(x_t, 1)

            def mean_rows(i):
                pe.wait_ge(n_sq[i], KD)
                for t in range(2):
                    for k in range(KD):
                        mm(ps[7][:, t:t + 1], sqT[:, k, t * P:(t + 1) * P], C("mean", 0, 1), start=k == 0, stop=k == KD - 1)
                for j in range(4):
                    for k in range(KD):
                        last = mm(ps[7][32 * j:32 * j + 32, 2:3], sqT[:, k, TP:T], C("mean", 0, 1), start=k == 0, stop=k == KD - 1)
                last.then_inc(n_ps[i], 1)

            def mean_cols(i):
                pe.wait_ge(n_sq[i], KD)
                for k in range(KD):
                    last = mm(ps[7][:, 0:T], C("mean"), sqT[:, k, :], start=k == 0, stop=k == KD - 1)
                last.then_inc(n_ps[i], 1)

            def project_in(l):
                for i, n in enumerate(IN_ORDER[l]):
                    w = nin[l][n]
                    src = take(pe, "in", l, n)[:, 0:8 * w].rearrange("p (k n) -> p k n", k=8)
                    if i >= 2:
                        pe.wait_ge(in_e[l], 3 * (i - 1))
                    b = (i % 2) * 3
                    for t in range(2):
                        for k in range(KD):
                            if i == 0 and t == 0:
                                pe.wait_ge(n_x[2 * l], k + 1)
                            last = mm(ps[b + t][:, 0:w], xT[:, k, t * P:(t + 1) * P], src[:, k, :], start=k == 0, stop=k == KD - 1)
                        last.then_inc(in_p[l], 1)
                    if w == 512:
                        for k in range(KD):
                            for j in range(4):
                                last = mm(ps[b + 2][32 * j:32 * j + 32, 0:P], xT[:, k, TP:T], src[:, k, j * P:(j + 1) * P],
                                          start=k == 0, stop=k == KD - 1)
                    else:
                        for k in range(KD):
                            last = mm(ps[b + 2][0:TS, 0:w], xT[:, k, TP:T], src[:, k, :], start=k == 0, stop=k == KD - 1)
                    last.then_inc(in_p[l], 1)
                    if i == 0:
                        mean_rows(2 * l)

            def turn_qk(l, lo, hi):
                if l == 0:
                    groups = [(t, c) for t in range(3) for c in (0, 512, 1024, 1536)]
                else:
                    groups = [(t, c) for t in range(3) for c in (0, 512)] + [(t, 1024) for t in range(2)] + \
                             [(t, None) for t in range(3)]
                for i in range(lo, hi):
                    t, c = groups[i]
                    if i >= 6:
                        pe.wait_ge(t_e[l], i - 5)
                    cols = [c + j * P for j in range(4)] if c is not None else [1536, 1664, 2048, 2176]
                    for j, a in enumerate(cols):
                        last = turn(ps[i % 6][:, j * P:j * P + WT[t]], proj[0:WT[t], t, a:a + P], WT[t])
                    last.then_inc(t_p[l], 1)
                pe.wait_ge(t_e[l], hi)

            def prompt0():
                def scores(h):
                    if h >= 2:
                        pe.wait_ge(a_w[0], h - 1)
                    hb = 64 * (h % 2)
                    q, k = qT[hb:hb + 64, h // 2, :], kT[hb:hb + 64, h // 2, :]
                    mm(ps[h % 2][:, 0:P], q[:, 0:P], k[:, 0:P], start=True, stop=True)
                    mm(ps[h % 2][:, P:3 * P], q[:, P:2 * P], k[:, 0:2 * P], start=True, stop=True).then_inc(a_s[0], 1)

                def turn_w(h):
                    pe.wait_ge(a_w[0], h + 1)
                    if h >= 2:
                        pe.wait_ge(a_te[0], h - 1)
                    for j in range(3):
                        last = turn(ps[2 + h % 2][:, j * P:(j + 1) * P], R[:, 3, (h % 2) * 384 + j * P:(h % 2) * 384 + (j + 1) * P])
                    last.then_inc(a_t[0], 1)

                def values(h):
                    pe.wait_ge(a_te[0], h + 1)
                    if h >= 4 and h % 2 == 0:
                        pe.wait_ge(a_oe[0], h // 2 - 1)
                    o = ps[4 + (h // 2) % 2][64 * (h % 2):64 * (h % 2) + 64, 0:TP]
                    v = 2 * D + h * HD
                    mm(o, proj[:, 0, v:v + HD], pair_first(PTp[:, h % 2, 0:384]), start=True, stop=False)
                    mm(o[:, P:2 * P], proj[:, 1, v:v + HD], PTp[:, h % 2, 256:384], start=False, stop=True).then_inc(a_pv[0], 1)

                scores(0)
                scores(1)
                for h in range(NH + 1):
                    if h < NH:
                        turn_w(h)
                    if h + 2 < NH:
                        scores(h + 2)
                    if h >= 1:
                        values(h - 1)

            def pair_first(x):
                return x[:, 0:256]

            def decode_k0():
                pe.wait_ge(qb_d[0], 1)
                for cc in range(17):
                    if cc < 16:
                        src = take(pe, "k0", cc // 2, cc % 2)
                    for p in range(8):
                        if cc < 16:
                            i = cc * 8 + p
                            if i >= 2:
                                pe.wait_ge((k_a, k_d)[i % 2][0], i // 2)
                            for r in range(4):
                                last = turn(ps[6 + i % 2][:, r * P:(r + 1) * P], src[:, r * D + p * P:r * D + (p + 1) * P])
                            last.then_inc(k_p[0], 1)
                        if cc >= 1:
                            c = cc - 1
                            b, half = c // 2, c % 2
                            bl = b % 4
                            i = c * 8 + p
                            pe.wait_ge((k_a, k_d)[i % 2][0], i // 2 + 1)
                            if c == 8 and p == 0:
                                pe.wait_ge(r_ps[0], 1)
                                pe.wait_ge(r_sg, 1)
                            mm(ps[(p // 4) * 2 + half][32 * bl:32 * bl + 32, :], qb0[:, b, p, :], KT[:, c % 2, p, :],
                               start=p % 4 == 0, stop=p % 4 == 3).then_inc(k_s[0], 1)
                    if cc >= 1 and (cc - 1) % 2 == 1:
                        b = (cc - 1) // 2
                        bl = b % 4
                        for p in range(8):
                            last = mm(ps[4][32 * bl:32 * bl + 32, (p // 4) * 32:(p // 4) * 32 + 32], qb0[:, b, p, :],
                                      kT[:, p, TP:T], start=p % 4 == 0, stop=p % 4 == 3)
                        last.then_inc(k_n[0], 1)

            def turn_o(l, i):
                pe.wait_ge(v_x[l], i + 1)
                if i >= 1:
                    pe.wait_ge(v_e[l], i)
                if l == 1:
                    pe.wait_ge(i_r, min(i + 3, 4))
                turn(ps[4][0:64, P:2 * P], osm[:, i % 2, :]).then_inc(v_t[l], 1)

            def decode_v0(g):
                pe.wait_ge(r_w[0], 2 * (g + 1))
                for i in range(6):
                    y, c0 = i // 3, 4 * (i % 3)
                    n = g * 6 + i
                    if n >= 2:
                        pe.wait_ge(r_te[0], n - 1)
                    for c in range(c0, min(c0 + 4, 9)):
                        w = P if c < 8 else TS
                        last = turn(ps[6 + i % 2][0:w, (c - c0) * P:(c - c0 + 1) * P], R[:, 3 * y, c * P:c * P + w])
                    last.then_inc(r_t[0], 1)
                pe.wait_ge(r_te[0], 6 * (g + 1))
                for bl in range(4):
                    b = 4 * g + bl
                    n = b // 2
                    if bl % 2 == 0 and n >= 1:
                        pe.wait_ge(v_x[0], n)
                    for half in range(2):
                        src = take(pe, "v0", b, half)
                        for r in range(4):
                            c = half * 4 + r
                            for y in range(2):
                                lo = (bl % 2) * 64 + y * 32
                                last = mm(ps[5][lo:lo + 32, :], PT0[:, y, c, 32 * bl:32 * bl + 32],
                                          src[:, r * D + y * 512:r * D + (y + 1) * 512], start=c == 0, stop=False)
                        if half == 1:
                            for y in range(2):
                                lo = (bl % 2) * 64 + y * 32
                                last = mm(ps[5][lo:lo + 32, :], PT0[0:TS, y, 8, 32 * bl:32 * bl + 32],
                                          proj[0:TS, 2, 2 * D + y * 512:2 * D + (y + 1) * 512], start=False, stop=True)
                        last.then_inc(v_c[0], 1)
                    if bl % 2 == 1 and n >= 1:
                        turn_o(0, n - 1)

            def project_out(l):
                for n in range(2):
                    src = take(pe, "out", l, n).rearrange("p (k n) -> p k n", k=8)
                    for j in range(4):
                        i = n * 4 + j
                        if i >= 4:
                            pe.wait_ge(o_e[l], i - 3)
                        for k in range(KD):
                            last = mm(ps[4 + j][:, 0:T], src[:, k, j * P:(j + 1) * P], oT[:, k, :], start=k == 0, stop=k == KD - 1)
                        last.then_inc(o_p[l], 1)

            def ffn(l):
                for n in range(FT // 2):
                    src = take(pe, "gu", l, n).rearrange("p (k n) -> p k n", k=8)
                    for j in range(2):
                        f = 2 * n + j
                        if f >= 3:
                            pe.wait_ge(u_u[l], f - 2)
                        for y in range(2):
                            for k in range(KD):
                                if f == 0 and y == 0:
                                    pe.wait_ge(n_x[2 * l + 1], k + 1)
                                last = mm(ps[2 * (f % 3) + y][:, 0:T], src[:, k, y * 256 + j * P:y * 256 + (j + 1) * P],
                                          x2T[:, k, :], start=k == 0, stop=k == KD - 1)
                        last.then_inc(u_p[l], 1)
                        if f == 0:
                            mean_cols(2 * l + 1)
                pe.wait_ge(u_e[l], FT)
                for n in range(8):
                    cg, kh = n // 2, n % 2
                    src = take(pe, "down", l, n)[:, 0:11 * 256].rearrange("p (k n) -> p k n", k=11)
                    if cg >= 2 and kh == 0:
                        pe.wait_ge(d_e[l], 2 * (cg - 1))
                    for j in range(2):
                        for k in range(11):
                            last = mm(ps[(cg % 2) * 2 + j][:, 0:T], src[:, k, j * P:(j + 1) * P], actT[:, kh * 11 + k, :],
                                      start=kh == 0 and k == 0, stop=kh == 1 and k == 10)
                    last.then_inc(d_p[l], 1)

            def compress_cache():
                pe.wait_ge(s_w1, 32)
                pe.wait_ge(d_e[0], KD)
                pe.wait_ge(c_a, 1)
                for j in range(4):
                    last = mm(ps[4][:, j:j + 1], R[:, 0, j * P:(j + 1) * P], C("mean", 0, 1), start=True, stop=True)
                last.then_inc(c_b, 1)

                def second(b):
                    pe.wait_ge(c_he, 4 * (b + 1))
                    if b >= 1:
                        pe.wait_ge(c_we, b)
                    else:
                        pe.wait_ge(c_be, 1)
                    hv = hid.rearrange("p j (h n) -> p j h n", h=NKV)
                    for par in range(2):
                        for kp in range(2):
                            for hf in range(2):
                                mm(ps[5][par * 64:par * 64 + 64, kp * NCS:(kp + 1) * NCS], w2[:, 0, hf, :], hv[:, hf, 2 * kp + par, :],
                                   start=hf == 0, stop=hf == 1)
                    for h in range(NKV):
                        for hf in range(2):
                            last = mm(ps[4][0:NCS, h * HD:(h + 1) * HD], hv[:, 2 + hf, h, :], w2[:, 1, hf, :],
                                      start=hf == 0, stop=hf == 1)
                    last.then_inc(c_w, 1)

                for bb in range(NB + 1):
                    if bb < NB:
                        src = take(pe, "cmp", bb)
                    if bb >= 1:
                        pe.wait_ge(k_a[1], 4 * bb)
                        pe.wait_ge(k_d[1], 4 * bb)
                    for i in range(8):
                        if bb < NB:
                            n = bb * 8 + i
                            if n >= 2:
                                pe.wait_ge((k_a, k_d)[n % 2][1], n // 2)
                            for r in range(4):
                                a = (4 * (i % 2) + r) * 512 + (i // 2) * P
                                last = turn(ps[6 + n % 2][:, r * P:(r + 1) * P], src[:, a:a + P])
                            last.then_inc(k_p[1], 1)
                        if bb >= 1:
                            b, j = bb - 1, i // 2
                            if b >= 1 and i == 1:
                                second(b - 1)
                            if i % 2 == 0 and b >= 1:
                                pe.wait_ge(c_he, 4 * (b - 1) + j + 1)
                            for o in range(8 * (i % 2), 8 * (i % 2) + 8):
                                last = mm(ps[j][:, 0:NKV * NCS], w1r[:, j // 2, o, (j % 2) * P:(j % 2 + 1) * P],
                                          KT[:, b % 2, (j // 2) * 4:(j // 2) * 4 + 4, o:o + 8 * (NCS - 1) + 1:8],
                                          start=o == 0, stop=o == 15)
                            if i % 2 == 1:
                                last.then_inc(c_h, 1)
                second(NB - 1)
                pe.wait_ge(c_we, NB)

            def compress_prompt():
                for k in range(2):
                    src = take(pe, "w1", k).rearrange("p (i n) -> p i n", i=16)
                    for hf in range(2):
                        for o in range(16):
                            last = mm(ps[2 * k + hf][:, 0:NKV * NCP], src[:, o, hf * P:(hf + 1) * P],
                                      XTp[:, k * 4:k * 4 + 4, o:o + 8 * (NCP - 1) + 1:8], start=o == 0, stop=o == 15)
                        last.then_inc(p_h, 1)
                pe.wait_ge(p_he, 4)
                hv = hidp.rearrange("p j (h n) -> p j h n", h=NKV)
                for dh in range(2):
                    for hf in range(2):
                        mm(ps[5][dh * 64:dh * 64 + 64, 0:NKV * NCP], w2[:, 0, hf, :], hidp[:, hf, :], start=hf == 0, stop=hf == 1)
                for h in range(NKV):
                    for hf in range(2):
                        last = mm(ps[4][0:NCP, h * HD:(h + 1) * HD], hv[:, 2 + hf, h, :], w2[:, 1, hf, :],
                                  start=hf == 0, stop=hf == 1)
                last.then_inc(p_w, 1)
                pe.wait_ge(p_we, 1)

            def prompt1():
                def scores(h):
                    if h >= 2:
                        pe.wait_ge(a_m[1], h - 1)
                    hb, kv = 64 * (h % 2), h // 4
                    q = qT[hb:hb + 64, h // 2, :]
                    A, B = ps[2 * (h % 2)], ps[2 * (h % 2) + 1]
                    for br, bank in ((0, A), (1, B)):
                        k = kT[hb:hb + 64, 4 * br + kv, :]
                        mm(bank[:, 0:P], q[:, 0:P], k[:, 0:P], start=True, stop=True)
                        mm(bank[:, P:3 * P], q[:, P:2 * P], k[:, 0:2 * P], start=True, stop=True)
                    for t in range(2):
                        last = mm(A[:, 384 + t * NCP:384 + (t + 1) * NCP], q[:, t * P:(t + 1) * P], kcp[hb:hb + 64, kv, :],
                                  start=True, stop=True)
                    last.then_inc(a_s[1], 1)

                def turn_w(h):
                    pe.wait_ge(a_w[1], h + 1)
                    if h >= 1:
                        pe.wait_ge(a_te[1], h)
                    W = R[:, h % 3, :]
                    for br in range(2):
                        for j in range(3):
                            turn(ps[4 + br][:, j * P:(j + 1) * P], W[:, br * 384 + j * P:br * 384 + (j + 1) * P])
                    for t in range(2):
                        last = turn(ps[6][0:NCP, t * P:(t + 1) * P], W[:, 768 + t * NCP:768 + (t + 1) * NCP])
                    last.then_inc(a_t[1], 1)

                def values(h):
                    pe.wait_ge(a_te[1], h + 1)
                    if h >= 2 and h % 2 == 0:
                        pe.wait_ge(a_oe[1], h // 2)
                    kv = h // 4
                    o = ps[7][64 * (h % 2):64 * (h % 2) + 64, 0:TP]
                    X = PTp[:, h % 2, :]
                    mm(o, vcp[0:NCP, kv * HD:(kv + 1) * HD], X[0:NCP, 768:1024], start=True, stop=False)
                    for br in range(2):
                        v = NQ1 + (3 + 2 * br) * KVW + kv * HD
                        mm(o, proj[:, 0, v:v + HD], X[:, br * 384:br * 384 + 256], start=False, stop=False)
                        last = mm(o[:, P:2 * P], proj[:, 1, v:v + HD], X[:, br * 384 + 256:br * 384 + 384], start=False, stop=br == 1)
                    last.then_inc(a_pv[1], 1)

                scores(0)
                scores(1)
                for h in range(NH + 1):
                    if h < NH:
                        turn_w(h)
                    if h + 2 < NH:
                        scores(h + 2)
                    if h >= 1:
                        values(h - 1)

            def decode_k1(g):
                if g >= 1:
                    pe.wait_ge(r_ps[1], g)
                for b2 in range(2):
                    b = 2 * g + b2
                    lo = 64 * b2
                    for kp in range(2):
                        mm(ps[3][lo:lo + 64, 0:NCS], qb1[:, b, kp, :], kc[:, b, kp, :], start=kp == 0, stop=kp == 1)
                    for br in range(2):
                        for kp in range(2):
                            last = mm(ps[3][lo:lo + 64, 64 + 32 * br:96 + 32 * br], qb1[:, b, kp, :],
                                      kT[:, 2 * br + kp, TP:T], start=kp == 0, stop=kp == 1)
                last.then_inc(k_n[1], 1)
                for step in range(3):
                    if step < 2:
                        src = take(pe, "k1", 2 * g + step)
                    for i in range(6):
                        if step < 2:
                            n = (2 * g + step) * 6 + i
                            if n >= 2:
                                pe.wait_ge((k_a, k_d)[n % 2][2], n // 2)
                            for r in range(4):
                                a = ((4 * (i % 2) + r) * KVW + (i // 2) * P) if i < 4 else (NPG + r) * KVW + (i - 4) * P
                                last = turn(ps[6 + n % 2][:, r * P:(r + 1) * P], src[:, a:a + P])
                            last.then_inc(k_p[2], 1)
                        if step >= 1:
                            b2 = step - 1
                            b = 2 * g + b2
                            n = b * 6 + i
                            pe.wait_ge((k_a, k_d)[n % 2][2], n // 2 + 1)
                            kp, bank = (i // 2, i % 2) if i < 4 else (i - 4, 2)
                            mm(ps[bank][64 * b2:64 * b2 + 64, :], qb1[:, b, kp, :], KT[:, b % 2, i, :],
                               start=kp == 0, stop=kp == 1).then_inc(k_s[1], 1)
                pe.wait_ge(i_w, g + 1)
                if g >= 3:
                    pe.wait_ge(v_e[1], g - 2)
                mm(ps[4][:, 0:64], C("group"), R[:, 2, (g % 2) * 256:(g % 2) * 256 + 64], start=True, stop=True).then_inc(i_p, 1)

            def decode_v1(g):
                pe.wait_ge(r_w[1], g + 1)
                for i in range(4):
                    n = 4 * g + i
                    if n >= 2:
                        pe.wait_ge(r_te[1], n - 1)
                    bank = ps[6 + i % 2]
                    if i < 3:
                        for c in range(4):
                            j = 4 * i + c
                            src = R[:, 0, j * P:(j + 1) * P] if j < 8 else R[:, 1, (j - 8) * P:(j - 7) * P]
                            last = turn(bank[:, c * P:(c + 1) * P], src)
                    else:
                        turn(bank[0:TS, 0:P], R[:, 0, PAST:PAST + TS])
                        turn(bank[0:TS, P:2 * P], R[:, 1, WIN:WIN + TS])
                        a = (g % 2) * 256 + 128
                        last = turn(bank[0:NCS, 2 * P:3 * P], R[:, 2, a:a + NCS])
                    last.then_inc(r_t[1], 1)
                pe.wait_ge(r_te[1], 4 * (g + 1))
                for b2 in range(2):
                    b = 2 * g + b2
                    lo = 64 * b2
                    o = ps[5][lo:lo + 64, 0:KVW]
                    if b2 == 0 and g >= 1:
                        pe.wait_ge(v_x[1], g)
                    src = take(pe, "v1", b)
                    for j in range(12):
                        mm(o, PT1[:, j, lo:lo + 64], src[:, j * KVW:(j + 1) * KVW], start=j == 0, stop=False)
                    for br in range(2):
                        v = NQ1 + (3 + 2 * br) * KVW
                        mm(o, PT1[0:TS, 12 + br, lo:lo + 64], proj[0:TS, 2, v:v + KVW], start=False, stop=False)
                    mm(o, PT1[0:NCS, 14, lo:lo + 64], vc[0:NCS, b, :], start=False, stop=True).then_inc(v_c[1], 1)

            project_in(0)
            pe.wait_ge(in_e[0], 3 * len(nin[0]))
            pe.wait_ge(in_q[0], full_chunks(0, 5))
            pe.wait_ge(q_d[0], 6)
            turn_qk(0, 0, 12)
            prompt0()
            decode_k0()
            for g in range(2):
                decode_v0(g)
            turn_o(0, 3)
            pe.wait_ge(a_oe[0], 8)
            pe.wait_ge(v_e[0], 4)
            project_out(0)
            ffn(0)
            compress_cache()
            project_in(1)
            pe.wait_ge(in_e[1], 3 * len(nin[1]))
            pe.wait_ge(q_d[1], 6)
            turn_qk(1, 0, 6)
            pe.wait_ge(q_d[1], 9)
            turn_qk(1, 6, 8)
            compress_prompt()
            pe.wait_ge(q_d[1], 15)
            turn_qk(1, 8, 11)
            prompt1()
            pe.wait_ge(a_oe[1], 8)
            pe.wait_ge(qb_d[1], 1)
            decode_k1(0)
            for g in range(4):
                if g < 3:
                    decode_k1(g + 1)
                if g >= 1:
                    turn_o(1, g - 1)
                decode_v1(g)
            turn_o(1, 3)
            pe.wait_ge(v_e[1], 4)
            project_out(1)
            ffn(1)
            pe.wait_ge(d_e[1], KD)
            for t in range(3):
                for j in range(2):
                    for i in range(4):
                        last = turn(ps[2 * t + j][0:WT[t], i * P:(i + 1) * P], hT[:, 4 * j + i, t * P:t * P + WT[t]])
                    last.then_inc(y_t, 1)

        @block.scalar
        def _(act):
            f = nc.scalar.activation

            def copy(out, in_):
                return f(out, in_, ACT.Copy)

            for t in range(3):
                for j in range(2):
                    act.wait_ge(x_t, 2 * t + j + 1)
                    v = ps[2 * t + j][:, :].rearrange("p (i n) -> p i n", i=4)
                    copy(hT[:, 4 * j:4 * j + 4, t * P:t * P + WT[t]], v[:, :, 0:WT[t]]).then_inc(x_e, 1)

            def squares(i, ready):
                for k in range(KD):
                    act.wait_ge(ready, k + 1 if i else 6)
                    f(sqT[:, k, :], hT[:, k, :], ACT.Square).then_inc(n_sq[i], 1)

            def project_in(l):
                def roots(pos):
                    h0 = 0
                    for gi, (n, _, H, _) in enumerate(ROPED[l]):
                        if IN_ORDER[l].index(n) == pos:
                            act.wait_ge(q_rc[l], gi + 1)
                            f(ss[:, 0:2, h0:h0 + H], ss[:, 0:2, h0:h0 + H], ACT.Sqrt)
                            f(ss[0:TS, 2, h0:h0 + H], ss[0:TS, 2, h0:h0 + H], ACT.Sqrt).then_inc(q_rs[l], 1)
                        h0 += H

                act.wait_ge(n_rc[2 * l], 1)
                f(rt[:, :], rt[:, :], ACT.Sqrt).then_inc(n_rs[2 * l], 1)
                act.wait_ge(n_rs[2 * l], 1)
                for i, n in enumerate(IN_ORDER[l]):
                    w = nin[l][n]
                    b = (i % 2) * 3
                    for t in range(2):
                        act.wait_ge(in_p[l], 3 * i + t + 1)
                        f(proj[:, t, n * 512:n * 512 + w], ps[b + t][:, 0:w], ACT.Copy, scale=rt[:, t:t + 1]).then_inc(in_e[l], 1)
                    act.wait_ge(in_p[l], 3 * i + 3)
                    if w == 512:
                        full = full_chunks(l, i)
                        if full > 2:
                            act.wait_ge(in_q[l], full - 2)
                        f(smp[:, full % 2, :], ps[b + 2][:, 0:P], ACT.Copy, scale=rt[:, 2:3]).then_inc(in_e[l], 1)
                    else:
                        f(proj[0:TS, 2, n * 512:n * 512 + w], ps[b + 2][0:TS, 0:w], ACT.Copy, scale=rt[0:TS, 2:3]).then_inc(in_e[l], 1)
                    if i >= 1:
                        roots(i - 1)
                roots(len(nin[l]) - 1)

            def keep_qk(l, lo, hi):
                if l == 0:
                    i = 0
                    for t in range(3):
                        for dst, j in ((qT, 0), (qT, 4), (kT, 0), (kT, 4)):
                            act.wait_ge(t_p[0], i + 1)
                            v = ps[i % 6][:, :].rearrange("p (j n) -> p j n", j=4)
                            copy(dst[:, j:j + 4, t * P:t * P + WT[t]], v[:, :, 0:WT[t]]).then_inc(t_e[0], 1)
                            i += 1
                    return
                for i in range(lo, hi):
                    act.wait_ge(t_p[1], i + 1)
                    v = ps[i % 6][:, :].rearrange("p (j n) -> p j n", j=4)
                    if i < 6:
                        t, j = i // 2, 4 * (i % 2)
                        last = copy(qT[:, j:j + 4, t * P:t * P + WT[t]], v[:, :, 0:WT[t]])
                    elif i < 8:
                        t = i - 6
                        xd = XTp[:, :, t * 64:(t + 1) * 64].rearrange("p (j e) n -> p j e n", e=2)
                        for e in range(2):
                            for par in range(2):
                                last = copy(xd[par * 64:par * 64 + 64, :, e, :], v[e * 64:e * 64 + 64, :, par::2])
                    elif i < 10:
                        t = i - 8
                        kd = kT[:, :, t * P:(t + 1) * P].rearrange("p (j e) n -> p j e n", e=2)
                        for e in range(2):
                            for dh in range(2):
                                last = copy(kd[dh * 64:dh * 64 + 64, :, e, :], v[e * 64:e * 64 + 64, :, :])
                    else:
                        last = copy(kT[:, 0:4, TP:T], v[:, :, 0:TS])
                    last.then_inc(t_e[1], 1)

            def prompt0():
                def probs(h):
                    b = h % 2
                    act.wait_ge(a_s[0], h + 1)
                    if h < 8:
                        if h >= 2:
                            act.wait_ge(a_w[0], h - 1)
                        f(R[:, 0, b * 384:b * 384 + 384], ps[b][:, 0:384], ACT.Sigmoid, scale=SC)
                        f(R[:, 1, b * 384:b * 384 + 384], ps[b][:, 0:384], ACT.Sigmoid, scale=-SC).then_inc(a_g, 1)
                    else:
                        act.wait_ge(a_m[0], h - 7)
                        for t, (lo, hi) in enumerate(((0, 128), (128, 384))):
                            last = f(R[:, 1, b * 384 + lo:b * 384 + hi], R[:, 0, b * 384 + lo:b * 384 + hi], ACT.Exp,
                                     scale=SC, bias=st[:, 8 * b + 2 + t:8 * b + 3 + t], accum_out=st[:, 8 * b + 4 + t:8 * b + 5 + t])
                        last.then_inc(a_e[0], 1)

                def keep(h):
                    act.wait_ge(a_t[0], h + 1)
                    if h >= 2:
                        act.wait_ge(a_pv[0], h - 1)
                    copy(PTp[:, h % 2, 0:384], ps[2 + h % 2][:, 0:384]).then_inc(a_te[0], 1)

                def keep_out(h):
                    if h % 2 == 1:
                        act.wait_ge(a_pv[0], h + 1)
                        copy(oT[:, h // 2, 0:TP], ps[4 + (h // 2) % 2][:, 0:TP]).then_inc(a_oe[0], 1)

                probs(0)
                for h in range(NH):
                    if h + 1 < NH:
                        probs(h + 1)
                    if h >= 1:
                        keep_out(h - 1)
                    keep(h)
                keep_out(NH - 1)

            def keep_k0(g):
                for cc in range(9 * g, (9, 16)[g]):
                    for p in range(0, 8, 2):
                        i = cc * 8 + p
                        act.wait_ge(k_p[0], i + 1)
                        if cc >= 2:
                            act.wait_ge(k_s[0], 8 * (cc - 2) + p + 1)
                        copy(KT[:, cc % 2, p, :], ps[6][:, :]).then_inc(k_a[0], 1)

            def rows0(g):
                act.wait_ge(k_s[0], 64 * (g + 1))
                act.wait_ge(k_n[0], 4 * (g + 1))
                if g:
                    act.wait_ge(r_t[0], 6 * g)
                for row, s in ((0, SC), (1, -SC)):
                    for j in range(2):
                        f(R[:, row, j * 512:(j + 1) * 512], ps[j][:, :], ACT.Sigmoid, scale=s)
                    last = f(R[:, row, PAST:PAST + TS], ps[4][:, 0:32], ACT.Sigmoid, scale=s)
                last.then_inc(r_sg, 1)
                act.wait_ge(r_m[0], g + 1)
                f(R[:, 3, 0:PAST + TS], R[:, 3, 0:PAST + TS], ACT.Exp, scale=SC, bias=st[:, 40:41],
                  accum_out=st[:, 41:42]).then_inc(r_e[0], 1)

            def keep_o(l, i):
                act.wait_ge(v_t[l], i + 1)
                for b2 in range(2):
                    v = ps[4][0:64, P + 64 * b2:P + 64 * b2 + 64].rearrange("p (i e q) -> p i e q", e=2, q=NQ)
                    c = TP + (2 * i + b2) * NQ
                    for e in range(2):
                        last = copy(oT[e * 64:e * 64 + 64, :, c:c + NQ], v[:, :, e, :])
                last.then_inc(v_e[l], 1)

            def keep_p0(g):
                for i in range(6):
                    y, c0 = i // 3, 4 * (i % 3)
                    act.wait_ge(r_t[0], g * 6 + i + 1)
                    v = ps[6 + i % 2][:, :].rearrange("p (c n) -> p c n", c=4)
                    if i % 3 < 2:
                        last = copy(PT0[:, y, c0:c0 + 4, :], v)
                    else:
                        last = copy(PT0[0:TS, y, 8, :], v[0:TS, 0, :])
                    last.then_inc(r_te[0], 1)

            def ffn(l):
                act.wait_ge(n_rc[2 * l + 1], 1)
                f(rst, R[:, 3, T:2 * T], ACT.Sqrt).then_inc(n_rs[2 * l + 1], 1)
                for j in range(FT):
                    a = (j % 2) * T
                    act.wait_ge(u_g[l], j + 1)
                    if j >= 2:
                        act.wait_ge(u_e[l], j - 1)
                    f(R[:, 1, a:a + T], R[:, 0, a:a + T], ACT.Silu).then_inc(u_a[l], 1)

            def compress_cache():
                act.wait_ge(c_be, 1)
                for bb in range(NB + 1):
                    for i in range(8):
                        if bb < NB and i % 2 == 0:
                            act.wait_ge(k_p[1], bb * 8 + i + 1)
                            if bb >= 2:
                                act.wait_ge(c_h, 4 * (bb - 1))
                            keep_pairs(f, copy, bb, i, ps[6]).then_inc(k_a[1], 1)
                        if bb >= 1 and i % 2 == 1:
                            b, j = bb - 1, i // 2
                            act.wait_ge(c_h, 4 * b + j + 1)
                            if b >= 1:
                                act.wait_ge(c_w, b)
                            f(hid[:, j, :], ps[j][:, 0:NKV * NCS], ACT.Silu, bias=cb[:, j:j + 1]).then_inc(c_he, 1)

            def keep_pairs(f_, cp, bb, i, bank):
                blk = i // 2
                for e in range(2):
                    for par in range(2):
                        last = cp(KT[par * 64:par * 64 + 64, bb % 2, 2 * blk + e, (i % 2) * 256:(i % 2) * 256 + 256],
                                  bank[e * 64:e * 64 + 64, par::2])
                return last

            def prompt1():
                def probs(h):
                    act.wait_ge(a_m[1], h + 1)
                    W, b = R[:, h % 3, :], 24 * (h % 3)
                    for j, (lo, hi) in enumerate(((0, 128), (128, 384), (384, 512), (512, 768), (768, 783), (783, 798))):
                        last = f(W[:, lo:hi], W[:, lo:hi], ACT.Exp, scale=SC, bias=st[:, b + 6 + j:b + 7 + j],
                                 accum_out=st[:, b + 12 + j:b + 13 + j])
                    last.then_inc(a_e[1], 1)

                def keep(h):
                    act.wait_ge(a_t[1], h + 1)
                    if h >= 2:
                        act.wait_ge(a_pv[1], h - 1)
                    X = PTp[:, h % 2, :]
                    copy(X[:, 0:384], ps[4][:, 0:384])
                    copy(X[:, 384:768], ps[5][:, 0:384])
                    copy(X[0:NCP, 768:1024], ps[6][0:NCP, 0:256]).then_inc(a_te[1], 1)

                def keep_out(h):
                    if h % 2 == 1:
                        act.wait_ge(a_pv[1], h + 1)
                        copy(oT[:, h // 2, 0:TP], ps[7][:, 0:TP]).then_inc(a_oe[1], 1)

                probs(0)
                for h in range(NH):
                    if h + 1 < NH:
                        probs(h + 1)
                    if h >= 1:
                        keep_out(h - 1)
                    keep(h)
                keep_out(NH - 1)

            def rows1(g):
                a = (g % 2) * 256
                act.wait_ge(i_m, g + 1)
                f(R[:, 2, a + 1:a + 1 + NCS], ps[3][:, 0:NCS], ACT.Exp, scale=SC, bias=st[:, 52:53],
                  accum_out=st[:, 53:54]).then_inc(i_e, 1)
                act.wait_ge(r_m[1], g + 1)
                f(R[:, 0, 0:PAST + TS], R[:, 0, 0:PAST + TS], ACT.Exp, scale=SC, bias=st[:, 56:57], accum_out=st[:, 58:59])
                f(R[:, 1, 0:WIN + TS], R[:, 1, 0:WIN + TS], ACT.Exp, scale=SC, bias=st[:, 57:58],
                  accum_out=st[:, 59:60]).then_inc(r_e[1], 1)

            def keep_k1(g):
                for b in (2 * g, 2 * g + 1):
                    for i in range(0, 6, 2):
                        n = b * 6 + i
                        act.wait_ge(k_p[2], n + 1)
                        if b >= 2:
                            act.wait_ge(k_s[1], 6 * (b - 2) + i + 1)
                        copy(KT[:, b % 2, i, :], ps[6][:, :]).then_inc(k_a[2], 1)

            def keep_p1(g):
                for i in range(4):
                    act.wait_ge(r_t[1], 4 * g + i + 1)
                    v = ps[6 + i % 2][:, :].rearrange("p (c n) -> p c n", c=4)
                    if i < 3:
                        last = copy(PT1[:, 4 * i:4 * i + 4, :], v)
                    else:
                        copy(PT1[0:TS, 12:14, :], v[0:TS, 0:2, :])
                        last = copy(PT1[0:NCS, 14, :], v[0:NCS, 2, :])
                    last.then_inc(r_te[1], 1)

            act.wait_ge(s_const, 80)
            squares(0, x_e)
            project_in(0)
            keep_qk(0, 0, 12)
            prompt0()
            keep_k0(0)
            rows0(0)
            keep_k0(1)
            keep_p0(0)
            rows0(1)
            keep_o(0, 0)
            keep_p0(1)
            for i in range(1, 4):
                keep_o(0, i)
            squares(1, o_e[0])
            ffn(0)
            squares(2, d_e[0])
            compress_cache()
            project_in(1)
            keep_qk(1, 0, 8)
            for t in range(3):
                last = f(gates[0:WT[t], t, :], proj[0:WT[t], t, N1 - 48:N1], ACT.Sigmoid)
            last.then_inc(g_s, 1)
            for j in range(4):
                act.wait_ge(p_h, j + 1)
                f(hidp[:, j, :], ps[j][:, 0:NKV * NCP], ACT.Silu, bias=cb[:, j:j + 1]).then_inc(p_he, 1)
            keep_qk(1, 8, 11)
            prompt1()
            keep_k1(0)
            rows1(0)
            for g in range(4):
                if g < 3:
                    keep_k1(g + 1)
                    a = ((g + 1) % 2) * 256
                    act.wait_ge(i_m, g + 2)
                    f(R[:, 2, a + 1:a + 1 + NCS], ps[3][:, 0:NCS], ACT.Exp, scale=SC, bias=st[:, 52:53],
                      accum_out=st[:, 53:54]).then_inc(i_e, 1)
                if g >= 1:
                    keep_o(1, g - 1)
                keep_p1(g)
                if g < 3:
                    act.wait_ge(r_m[1], g + 2)
                    f(R[:, 0, 0:PAST + TS], R[:, 0, 0:PAST + TS], ACT.Exp, scale=SC, bias=st[:, 56:57], accum_out=st[:, 58:59])
                    f(R[:, 1, 0:WIN + TS], R[:, 1, 0:WIN + TS], ACT.Exp, scale=SC, bias=st[:, 57:58],
                      accum_out=st[:, 59:60]).then_inc(r_e[1], 1)
            keep_o(1, 3)
            squares(3, o_e[1])
            ffn(1)
            for t in range(3):
                for j in range(2):
                    act.wait_ge(y_t, 2 * t + j + 1)
                    if t == 0 and j == 0:
                        act.wait_ge(s_kv, 48 + 16 * 5 + 16 * NB)
                    copy(proj[0:WT[t], t, j * 512:(j + 1) * 512], ps[2 * t + j][0:WT[t], :]).then_inc(y_e, 1)

        @block.vector
        def _(dve):
            v = nc.vector
            chained = [0]

            def link(ins):
                chained[0] += 1
                ins.then_inc(ch, 1)
                dve.wait_ge(ch, chained[0])

            tt, ts = v.tensor_tensor, v.tensor_scalar

            def norm_rows(i):
                dve.wait_ge(n_ps[i], 1)
                link(ts(rt[:, :], ps[7][:, 0:3], EPS, None, ALU.add))
                v.reciprocal(rt[:, :], rt[:, :]).then_inc(n_rc[i], 1)

            def norm_cols(i):
                dve.wait_ge(n_ps[i], 1)
                link(ts(R[:, 3, T:2 * T], ps[7][:, 0:T], EPS, None, ALU.add))
                v.reciprocal(R[:, 3, T:2 * T], R[:, 3, T:2 * T]).then_inc(n_rc[i], 1)
                dve.wait_ge(n_rs[i], 1)

            def norm_rope(l):
                A, B = R[:, 0, 0:512], R[:, 1, 0:512]
                h0 = 0
                for gi, (n, c, H, g) in enumerate(ROPED[l]):
                    pos = IN_ORDER[l].index(n)
                    dve.wait_ge(in_e[l], 3 * (pos + 1))
                    dve.wait_ge(in_q[l], full_chunks(l, pos))
                    for t in range(3):
                        w = WT[t]
                        X = proj[0:w, t, c:c + H * HD]
                        link(tt(A[0:w, 0:H * HD], X, X, ALU.mult))
                        link(v.reduce_sum(ss[0:w, t, h0:h0 + H], A[0:w, 0:H * HD].rearrange("p (h d) -> p h d", h=H), AX))
                    two = ((ss[:, 0:2, h0:h0 + H]), (ss[0:TS, 2, h0:h0 + H]))
                    for x in two:
                        last = ts(x, x, 1.0 / HD, EPS, ALU.mult, ALU.add)
                    link(last)
                    for x in two:
                        last = v.reciprocal(x, x)
                    last.then_inc(q_rc[l], 1)
                    dve.wait_ge(q_rs[l], gi + 1)
                    for t in range(3):
                        w = WT[t]
                        X = proj[0:w, t, c:c + H * HD].rearrange("p (h d) -> p h d", h=H)
                        a = A[0:w, 0:H * HD].rearrange("p (h d) -> p h d", h=H)
                        b = B[0:w, 0:H * HD].rearrange("p (h d) -> p h d", h=H)
                        co, si = C("cos", t * HD, (t + 1) * HD, w), C("sin", t * HD, (t + 1) * HD, w)
                        link(tt(X, X, rep(ss[0:w, t, h0:h0 + H], 2, HD), ALU.mult))
                        link(tt(X, X, rep(gr[0:w, g * HD:(g + 1) * HD], 1, H), ALU.mult))
                        tt(a, X, rep(co, 1, H), ALU.mult)
                        tt(b[:, :, 0:32], X[:, :, 32:64], rep(si[:, 0:32], 1, H), ALU.mult)
                        link(tt(b[:, :, 32:64], X[:, :, 0:32], rep(si[:, 32:64], 1, H), ALU.mult))
                        tt(X, a, b, ALU.add).then_inc(q_d[l], 1)
                        dve.wait_ge(q_d[l], 3 * gi + t + 1)
                    h0 += H

            def prompt0():
                for b in range(2):
                    E = R[:, 2, b * 400:b * 400 + 386]
                    v.memset(E[:, 128:129], 1.0)
                    link(v.memset(E[:, 385:386], 1.0))

                def views(h):
                    b = h % 2
                    return (b,) + tuple(R[:, r, b * 384:b * 384 + 384] for r in (0, 1, 3)) + (R[:, 2, b * 400:b * 400 + 386],)

                def first(h):
                    b, S, K, W, E = views(h)
                    dve.wait_ge(a_s[0], h + 1)
                    dve.wait_ge(a_w[0], h - 1)
                    mx = st[:, 8 * b:8 * b + 2]
                    link(tt(S, ps[b][:, 0:384], C("causal"), ALU.add))
                    v.reduce_max(mx[:, 0:1], S[:, 0:128], AX)
                    link(v.reduce_max(mx[:, 1:2], S[:, 128:384], AX))
                    ts(st[:, 8 * b + 2:8 * b + 4], mx, -SC, None, ALU.mult).then_inc(a_m[0], 1)

                def second(h):
                    b, S, K, W, E = views(h)
                    if h < 8:
                        dve.wait_ge(a_g, h + 1)
                        if h >= 2:
                            dve.wait_ge(a_w[0], h - 1)
                        v.tensor_tensor_scan(E[:, 0:128][:, ::-1], K[:, 0:128][:, ::-1], C("notpast")[:, ::-1], 1.0, ALU.mult, ALU.max)
                        link(v.tensor_tensor_scan(E[:, 257:385][:, ::-1], K[:, 256:384][:, ::-1], C("notpast")[:, ::-1], 1.0,
                                                  ALU.mult, ALU.max))
                        v.tensor_tensor_scan(E[:, 129:257][:, ::-1], K[:, 128:256][:, ::-1], zero.broadcast_to([P, 128]),
                                             E[:, 257:258], ALU.mult, ALU.max)
                        tt(S[:, 0:128], S[:, 0:128], C("strict"), ALU.mult)
                        link(tt(S[:, 256:384], S[:, 256:384], C("strict"), ALU.mult))
                        if h >= 2:
                            dve.wait_ge(a_t[0], h - 1)
                        tt(W[:, 0:128], S[:, 0:128], E[:, 1:129], ALU.mult)
                        tt(W[:, 128:384], S[:, 128:384], E[:, 130:386], ALU.mult).then_inc(a_w[0], 1)
                    else:
                        dve.wait_ge(a_e[0], h - 7)
                        link(v.reciprocal(st[:, 8 * b + 6:8 * b + 8], st[:, 8 * b + 4:8 * b + 6]))
                        dve.wait_ge(a_t[0], h - 1)
                        ts(W[:, 0:128], K[:, 0:128], st[:, 8 * b + 6:8 * b + 7], None, ALU.mult)
                        ts(W[:, 128:384], K[:, 128:384], st[:, 8 * b + 7:8 * b + 8], None, ALU.mult).then_inc(a_w[0], 1)

                for h in range(NH):
                    if 8 <= h + 1 < NH:
                        first(h + 1)
                    second(h)

            def keep_k0(g):
                for cc in range(9 * g, (9, 16)[g]):
                    for p in range(1, 8, 2):
                        i = cc * 8 + p
                        dve.wait_ge(k_p[0], i + 1)
                        if cc >= 2:
                            dve.wait_ge(k_s[0], 8 * (cc - 2) + p + 1)
                        v.tensor_copy(KT[:, cc % 2, p, :], ps[7][:, :]).then_inc(k_d[0], 1)

            def drop_least(vals, n, neg):
                link(v.tensor_reduce(st[:, 42:43], vals, AX, ALU.min))
                link(v.scalar_tensor_tensor(st[:, 60:60 + n], vals, st[:, 42:43], C("rank", 0, n), ALU.is_le, ALU.mult))
                link(v.reduce_max(st[:, 43:44], st[:, 60:60 + n], AX))
                link(ts(neg, st[:, 60:60 + n], st[:, 43:44], NEG, ALU.is_ge, ALU.mult))

            def rows0(g):
                dve.wait_ge(k_s[0], 64 * (g + 1))
                dve.wait_ge(k_n[0], 4 * (g + 1))
                S, E = R[:, 3, :], R[:, 2, :]
                for j in range(2):
                    last = v.reduce_sum(st[:, 48 + 2 * j:50 + 2 * j], ps[2 + j][:, :].rearrange("p (n k) -> p n k", n=2), AX)
                link(last)
                drop_least(st[:, 48:52], 4, st[:, 76:80])
                if g:
                    dve.wait_ge(r_t[0], 6 * g)
                for j in range(4):
                    ts(S[:, j * 256:(j + 1) * 256], ps[2 + j // 2][:, (j % 2) * 256:(j % 2 + 1) * 256], st[:, 76 + j:77 + j],
                       None, ALU.add)
                dve.wait_ge(r_sg, g + 1)
                tt(S[:, PAST:PAST + TS], ps[4][:, 32:64], C("newneg0", g * TS, (g + 1) * TS), ALU.add).then_inc(r_ps[0], 1)
                dve.wait_ge(r_ps[0], g + 1)
                link(v.reduce_max(st[:, 44:45], S[:, 0:PAST + TS], AX))
                ts(st[:, 40:41], st[:, 44:45], -SC, None, ALU.mult).then_inc(r_m[0], 1)
                G, K = R[:, 0, :], R[:, 1, :]
                n = PAST + TS
                v.memset(E[:, n:n + 1], 1.0)
                link(tt(K[:, PAST:n], K[:, PAST:n], C("newnot", g * TS, (g + 1) * TS), ALU.max))
                v.tensor_tensor_scan(E[:, 0:n][:, ::-1], K[:, 0:n][:, ::-1], zero.broadcast_to([P, n]), 1.0, ALU.mult, ALU.max)
                link(tt(G[:, PAST:n], G[:, PAST:n], C("newpast", g * TS, (g + 1) * TS), ALU.mult))
                tt(G[:, 0:n], G[:, 0:n], E[:, 1:n + 1], ALU.mult).then_inc(r_w[0], 1)
                dve.wait_ge(r_e[0], g + 1)
                link(v.reciprocal(st[:, 45:46], st[:, 41:42]))
                ts(S[:, 0:n], S[:, 0:n], st[:, 45:46], None, ALU.mult).then_inc(r_w[0], 1)

            def pick(l, i):
                H = (8, NKV)[l]
                dve.wait_ge(v_c[l], (4 * (i + 1), 2 * (i + 1))[l])
                if i >= 2:
                    dve.wait_ge(v_t[l], i - 1)
                A = R[:, 2, 512:512 + H * HD]
                link(tt(A.rearrange("p (h d) -> p h d", h=H), ps[5][:, 0:H * HD].rearrange("p (h d) -> p h d", h=H),
                        rep(C(f"head{l}"), 2, HD), ALU.mult))
                v.reduce_sum(osm[:, i % 2, :], A.rearrange("p (h d) -> p d h", h=H), AX).then_inc(v_x[l], 1)

            def project_out(l):
                for i in range(KD):
                    dve.wait_ge(o_p[l], i + 1)
                    tt(hT[:, i, :], hT[:, i, :], ps[4 + i % 4][:, 0:T], ALU.add).then_inc(o_e[l], 1)

            def ffn(l):
                norm_cols(2 * l + 1)
                for j in range(FT):
                    a = (j % 2) * T
                    dve.wait_ge(u_p[l], j + 1)
                    if j >= 2:
                        dve.wait_ge(u_a[l], j - 1)
                        dve.wait_ge(u_e[l], j - 1)
                    tt(R[:, 0, a:a + T], ps[2 * (j % 3)][:, 0:T], rst, ALU.mult).then_inc(u_g[l], 1)
                    tt(R[:, 2, a:a + T], ps[2 * (j % 3) + 1][:, 0:T], rst, ALU.mult).then_inc(u_u[l], 1)
                if l == 0:
                    dve.wait_ge(u_a[l], FT)
                    dve.wait_ge(s_w1, 32)
                    for i in range(16):
                        for k in range(2):
                            acc, w, s_ = R[:, 0, k * CH:(k + 1) * CH], w1r[:, k, i, :], pec[:, k * 16 + i:k * 16 + i + 1]
                            if i == 0:
                                last = ts(acc, w, s_, None, ALU.mult)
                            else:
                                last = v.scalar_tensor_tensor(acc, w, s_, acc, ALU.mult, ALU.add)
                        if i < 15:
                            link(last)
                    last.then_inc(c_a, 1)
                for i in range(KD):
                    cg, j = i // 2, i % 2
                    dve.wait_ge(d_p[l], 2 * (cg + 1))
                    tt(hT[:, i, :], hT[:, i, :], ps[(cg % 2) * 2 + j][:, 0:T], ALU.add).then_inc(d_e[l], 1)

            def compress_cache():
                dve.wait_ge(c_b, 1)
                ts(cb[:, :], ps[4][:, 0:4], float(D), None, ALU.mult).then_inc(c_be, 1)

                def keep_second(b):
                    dve.wait_ge(c_w, b + 1)
                    v.tensor_copy(kc[:, b, :, :], ps[5][:, 0:2 * NCS].rearrange("p (i n) -> p i n", i=2))
                    v.tensor_copy(vc[0:NCS, b, :], ps[4][0:NCS, 0:KVW]).then_inc(c_we, 1)

                for bb in range(NB + 1):
                    for i in range(1, 8, 2):
                        if bb < NB:
                            dve.wait_ge(k_p[1], bb * 8 + i + 1)
                            if bb >= 2:
                                dve.wait_ge(c_h, 4 * (bb - 1))
                            blk = i // 2
                            for e in range(2):
                                for par in range(2):
                                    last = v.tensor_copy(KT[par * 64:par * 64 + 64, bb % 2, 2 * blk + e, 256:512],
                                                         ps[7][e * 64:e * 64 + 64, par::2])
                            last.then_inc(k_d[1], 1)
                        if bb >= 2 and i == 1:
                            keep_second(bb - 2)
                keep_second(NB - 1)

            def prompt1():
                dve.wait_ge(p_w, 1)
                v.tensor_copy(kcp[:, :, :], ps[5][:, 0:NKV * NCP].rearrange("p (h n) -> p h n", h=NKV))
                v.tensor_copy(vcp[0:NCP, :], ps[4][0:NCP, 0:KVW]).then_inc(p_we, 1)
                dve.wait_ge(g_s, 1)
                for t in range(2):
                    gv = gates[:, t, :].rearrange("p (h r) -> p h r", r=3)
                    for j, br in enumerate(GATE_ORDER):
                        if br:
                            last = v.tensor_copy(gp[:, :, 2 * j + t], gv[:, :, br])
                        else:
                            last = ts(gp[:, :, 2 * j + t], gv[:, :, br], C("cmpany", t, t + 1), None, ALU.mult)
                link(last)

                def views(h):
                    W, b = R[:, h % 3, :], 24 * (h % 3)
                    two = W[:, 0:768].rearrange("p (r n) -> p r n", r=2)
                    cm = W[:, 768:798].rearrange("p (t n) -> p t n", t=2)
                    return W, b, ((two[:, :, 0:128], 0, 4, 2), (two[:, :, 128:384], 1, 4, 2), (cm, 4, 6, 1))

                def first(h):
                    W, b, parts = views(h)
                    A, B = ps[2 * (h % 2)], ps[2 * (h % 2) + 1]
                    dve.wait_ge(a_s[1], h + 1)
                    if h >= 3:
                        dve.wait_ge(a_t[1], h - 2)
                    tt(W[:, 0:384], A[:, 0:384], C("causal"), ALU.add)
                    tt(W[:, 384:768], B[:, 0:384], C("causal"), ALU.add)
                    link(tt(W[:, 768:798], A[:, 384:414], C("cmpcausal"), ALU.add))
                    for x, lo, hi, step in parts:
                        last = v.reduce_max(st[:, b + lo:b + hi:step], x, AX)
                    link(last)
                    ts(st[:, b + 6:b + 12], st[:, b:b + 6], -SC, None, ALU.mult).then_inc(a_m[1], 1)

                def second(h):
                    W, b, parts = views(h)
                    dve.wait_ge(a_e[1], h + 1)
                    link(v.reciprocal(st[:, b + 18:b + 24], st[:, b + 12:b + 18]))
                    link(tt(st[:, b + 18:b + 24], st[:, b + 18:b + 24], gp[:, h, :], ALU.mult))
                    for x, lo, hi, step in parts:
                        last = tt(x, x, rep(st[:, b + 18 + lo:b + 18 + hi:step], 2, x.shape[2]), ALU.mult)
                    last.then_inc(a_w[1], 1)

                first(0)
                for h in range(NH):
                    if h + 1 < NH:
                        first(h + 1)
                    second(h)

            def keep_k1(g):
                for b in (2 * g, 2 * g + 1):
                    for i in range(1, 6, 2):
                        n = b * 6 + i
                        dve.wait_ge(k_p[2], n + 1)
                        if b >= 2:
                            dve.wait_ge(k_s[1], 6 * (b - 2) + i + 1)
                        v.tensor_copy(KT[:, b % 2, i, :], ps[7][:, :]).then_inc(k_d[2], 1)

            def cmp_rows(g):
                a = (g % 2) * 256
                pc, pg = R[:, 2, a:a + 64], R[:, 2, a + 128:a + 128 + NCS]
                dve.wait_ge(k_n[1], g + 1)
                if g >= 2:
                    dve.wait_ge(r_t[1], 4 * (g - 1))
                v.memset(pc[:, 0:1], 0.0)
                link(v.reduce_max(st[:, 48:49], ps[3][:, 0:NCS], AX))
                ts(st[:, 52:53], st[:, 48:49], -SC, None, ALU.mult).then_inc(i_m, 1)
                dve.wait_ge(i_e, g + 1)
                link(v.reciprocal(st[:, 54:55], st[:, 53:54]))
                ts(pc[:, 1:64], pc[:, 1:64], st[:, 54:55], None, ALU.mult).then_inc(i_w, 1)
                dve.wait_ge(i_w, g + 1)
                link(ts(pg, pc[:, 1:64], gs[:, g, 0:1], None, ALU.mult))

            def rows1(g):
                dve.wait_ge(i_p, g + 1)
                link(v.reduce_sum(st[:, 0:16], ps[4][:, 0:64].rearrange("p (j c) -> p j c", c=4), AX))
                link(tt(st[:, 16:30], st[:, 1:15], ps[4][:, 8:61:4], ALU.add))
                v.memset(st[:, 76:77], 0.0)
                v.memset(st[:, 91:92], 0.0).then_inc(i_r, 1)
                drop_least(st[:, 16:30], 14, st[:, 77:91])
                dve.wait_ge(k_s[1], 12 * (g + 1))
                if g:
                    dve.wait_ge(r_t[1], 4 * g)
                S, W = R[:, 0, :], R[:, 1, :]
                for j in range(2):
                    tt(S[:, j * 512:(j + 1) * 512].rearrange("p (n k) -> p n k", n=8),
                       ps[j][:, :].rearrange("p (n k) -> p n k", n=8), rep(st[:, 76 + 8 * j:84 + 8 * j], 2, HD), ALU.add)
                new = C("newneg1", g * TS, (g + 1) * TS)
                tt(S[:, PAST:PAST + TS], ps[3][:, 64:96], new, ALU.add)
                tt(W[:, 0:NQ], ps[2][:, 0:NQ], C("winneg"), ALU.add)
                v.tensor_copy(W[:, NQ:WIN], ps[2][:, NQ:WIN])
                tt(W[:, WIN:WIN + TS], ps[3][:, 96:128], new, ALU.add).then_inc(r_ps[1], 1)
                dve.wait_ge(r_ps[1], g + 1)
                v.reduce_max(st[:, 48:49], S[:, 0:PAST + TS], AX)
                link(v.reduce_max(st[:, 49:50], W[:, 0:WIN + TS], AX))
                ts(st[:, 56:58], st[:, 48:50], -SC, None, ALU.mult).then_inc(r_m[1], 1)
                dve.wait_ge(r_e[1], g + 1)
                link(v.reciprocal(st[:, 48:50], st[:, 58:60]))
                link(tt(st[:, 48:50], st[:, 48:50], gs[:, g, 1:3], ALU.mult))
                ts(S[:, 0:PAST + TS], S[:, 0:PAST + TS], st[:, 48:49], None, ALU.mult)
                ts(W[:, 0:WIN + TS], W[:, 0:WIN + TS], st[:, 49:50], None, ALU.mult).then_inc(r_w[1], 1)

            dve.wait_ge(s_const, 80)
            dve.wait_ge(x_e, 6)
            for k in range(KD):
                ts(xT[:, k, :], hT[:, k, :], gc[:, k:k + 1], None, ALU.mult).then_inc(n_x[0], 1)
            norm_rows(0)
            norm_rope(0)
            prompt0()
            keep_k0(0)
            rows0(0)
            keep_k0(1)
            rows0(1)
            for i in range(4):
                pick(0, i)
            project_out(0)
            ffn(0)
            compress_cache()
            norm_rows(2)
            norm_rope(1)
            prompt1()
            dve.wait_ge(g_l, 64)
            keep_k1(0)
            cmp_rows(0)
            rows1(0)
            for g in range(4):
                if g < 3:
                    keep_k1(g + 1)
                    cmp_rows(g + 1)
                    rows1(g + 1)
                pick(1, g)
            project_out(1)
            ffn(1)

        @block.gpsimd
        def _(pool):
            flat_state = state_win[0].rearrange("b w two h d -> b w (two h d)")
            flat_win = win_sample[0].rearrange("b w two h d -> b w (two h d)")
            pool.memset(pq[:], 0.0).then_inc(qb_z[0], 1)
            for b in range(NB):
                pool.dma_start(flat_win[b, 0:WIN - NQ, :], flat_state[b, NQ:WIN, :]).then_inc(s_out, 16)


            def spread(l):
                for i, n in enumerate(IN_ORDER[l]):
                    if nin[l][n] == 512:
                        full = full_chunks(l, i)
                        pool.wait_ge(in_e[l], 3 * (i + 1))
                        for j in range(4):
                            last = nc.gpsimd.tensor_copy(proj[0:TS, 2, n * 512 + j * P:n * 512 + (j + 1) * P],
                                                         smp[32 * j:32 * j + 32, full % 2, :])
                        last.then_inc(in_q[l], 1)

            def scale_by_gain(i, dst, ready):
                for k in range(KD):
                    pool.wait_ge(ready, k + 1)
                    nc.gpsimd.tensor_scalar(dst[:, k, :], hT[:, k, :], gc[:, i * KD + k:i * KD + k + 1], None,
                                            ALU.mult).then_inc(n_x[i], 1)

            def gate_up(l):
                for j in range(FT):
                    a = (j % 2) * T
                    pool.wait_ge(u_a[l], j + 1)
                    pool.wait_ge(u_u[l], j + 1)
                    nc.gpsimd.tensor_tensor(actT[:, j, :], R[:, 1, a:a + T], R[:, 2, a:a + T], ALU.mult).then_inc(u_e[l], 1)

            spread(0)
            pool.wait_ge(q_d[0], 6)
            pool.wait_ge(in_e[0], 3 * len(nin[0]))
            pool.wait_ge(in_q[0], full_chunks(0, 5))
            kv = kv0_prompt[0, 0].rearrange("(t p) two h d -> t p (two h d)", p=P)
            for t in range(2):
                pool.dma_start(kv[t], proj[:, t, D:N0]).then_inc(s_kv, 16)
            pool.dma_start(kv0_sample[0].rearrange("b q two h d -> (b q) (two h d)"), proj[0:TS, 2, D:N0]).then_inc(s_kv, 16)
            pool.wait_ge(t_e[0], 12)
            pool.wait_ge(qb_z[0], 1)
            for p in range(8):
                for e in range(2):
                    h = 2 * (p % 4) + e
                    last = nc.gpsimd.tensor_copy(qb0[e * 64:e * 64 + 64, :, p, h * NQ:(h + 1) * NQ],
                                                 qT[e * 64:e * 64 + 64, p, TP:T].rearrange("p (b q) -> p b q", q=NQ))
            last.then_inc(qb_d[0], 1)
            scale_by_gain(1, x2T, o_e[0])
            gate_up(0)
            scale_by_gain(2, xT, d_e[0])
            nc.gpsimd.memset(pq[:, 0:1024], 0.0).then_inc(qb_z[1], 1)
            spread(1)
            pool.wait_ge(q_d[1], 15)
            pool.wait_ge(in_e[1], 3 * len(nin[1]))
            pool.wait_ge(in_q[1], full_chunks(1, 5))
            for t in range(2):
                rows = slice(t * P, (t + 1) * P)
                pool.dma_start(kv1_prompt[0, 0, rows].rearrange("p k h d -> p (k h d)"), proj[:, t, NQ1:NQ1 + 4 * KVW]).then_inc(s_kv, 16)
                pool.dma_start(win_prompt[0, 0, rows].rearrange("p k h d -> p (k h d)"), proj[:, t, NQ1 + 4 * KVW:NQ1 + 6 * KVW]).then_inc(s_kv, 16)
            pool.dma_start(kv1_sample[0].rearrange("b q k h d -> (b q) (k h d)"), proj[0:TS, 2, NQ1:NQ1 + 4 * KVW]).then_inc(s_kv, 16)
            for b in range(NB):
                pool.dma_start(flat_win[b, WIN - NQ:WIN, :], proj[b * NQ:(b + 1) * NQ, 2, NQ1 + 4 * KVW:NQ1 + 6 * KVW]).then_inc(s_kv, 16)
            pool.wait_ge(g_s, 1)
            for b in range(NB):
                pool.dma_start(gate_scratch[b].rearrange("h q r -> q h r"),
                               gates[b * NQ:(b + 1) * NQ, 2, :].rearrange("q (h r) -> q h r", r=3)).then_inc(g_d, 16)
            pool.wait_ge(g_d, 16 * NB)
            rows = gate_scratch.rearrange("b h q r -> (b h q) r")
            for g in range(4):
                pool.dma_start(gs[:, g, :], rows[g * P:(g + 1) * P, :]).then_inc(g_l, 16)
            pool.wait_ge(t_e[1], 11)
            pool.wait_ge(qb_z[1], 1)
            for h in range(NH):
                kvh = h // 4
                kp, e, s = kvh // 2, kvh % 2, h % 2
                last = nc.gpsimd.tensor_copy(qb1[e * 64:e * 64 + 64, :, kp, h * NQ:(h + 1) * NQ],
                                             qT[s * 64:s * 64 + 64, h // 2, TP:T].rearrange("p (b q) -> p b q", q=NQ))
            last.then_inc(qb_d[1], 1)
            scale_by_gain(3, x2T, o_e[1])
            gate_up(1)
            yp = y_prompt[0].rearrange("(t p) d -> t p d", p=P)
            for t in range(2):
                pool.wait_ge(y_e, 2 * t + 2)
                pool.dma_start(yp[t], proj[:, t, 0:D]).then_inc(s_out, 16)
            pool.wait_ge(y_e, 6)
            pool.dma_start(y_sample.rearrange("b q d -> (b q) d"), proj[0:TS, 2, 0:D]).then_inc(s_out, 16)
            pool.wait_ge(s_out, 16 * (NB + 3))
            pool.wait_ge(s_kv, 48 + 16 * 5 + 16 * NB)


_OUTS = [(1, TP, D), (NB, NQ, D), (1, 1, TP, 2, NH, HD), (1, NB, NQ, 2, NH, HD), (1, 1, TP, 4, NKV, HD),
         (1, NB, NQ, 4, NKV, HD), (1, 1, TP, 2, NKV, HD), (1, NB, WIN, 2, NKV, HD)]
_INS = ["x_prompt", "x_sample", "cache_kv0", "cache_kv1", "state_win", "page_table", "w_in0", "w_out0", "w_in1",
        "w_out1", "cmp_w1", "cmp_w2", "w_gu", "w_down"]


def kernel(**inputs):
    import concourse.bacc as _bacc
    from concourse.bass_utils import run_bass_kernel_spmd as _run

    nc = _bacc.Bacc("TRN2", target_bir_lowering=False, num_devices=1)
    table, off = constants()
    arrays = {n: np.ascontiguousarray(inputs[n]) for n in _INS}
    arrays["consts"] = table
    g = [inputs["g_mix0"][0], inputs["g_ffn"][0], inputs["g_mix1"][0], inputs["g_ffn"][1]]
    arrays["gcol"] = np.ascontiguousarray(np.concatenate([np.asarray(a).reshape(KD, P).T for a in g], 1))
    r = [inputs["g_q0"][0], inputs["g_k0"][0], inputs["g_q1"][0]] + [inputs["g_k1"][0, i] for i in range(3)]
    arrays["grow"] = np.ascontiguousarray(np.broadcast_to(np.concatenate([np.asarray(a) for a in r])[None, :], (P, 6 * HD)))
    pe = np.asarray(inputs["cmp_pe"])[0].reshape(2, 16, P)
    arrays["pecol"] = np.ascontiguousarray(pe.transpose(2, 0, 1).reshape(P, 32))
    args = [nc.dram_tensor("in_" + n, a.shape, mybir.dt.from_np(a.dtype), kind="ExternalInput").ap() for n, a in arrays.items()]
    args += [nc.dram_tensor(f"out_{i}", s, F32, kind="ExternalOutput").ap() for i, s in enumerate(_OUTS)]
    args.append(nc.dram_tensor("gate_scratch", (NB, NH, NQ, 3), F32, kind="Internal").ap())
    trunk(nc, off, *args)
    res = _run(nc, [{"in_" + n: a for n, a in arrays.items()}], core_ids=[0])
    return tuple(res.results[0][f"out_{i}"] for i in range(len(_OUTS)))
```

```python
from contextlib import ExitStack

import concourse.bass as bass
from concourse import mybir
import numpy as np

F32 = mybir.dt.float32
I32 = mybir.dt.int32
ALU = mybir.AluOpType
ACT = mybir.ActivationFunctionType
AX = mybir.AxisListType.X

P = 128
D = 1024
KD = D // P
TP, NB, NQ = 256, 8, 4
TS = NB * NQ
T = TP + TS
PAST, PAGE = 1024, 128
NPG = PAST // PAGE
HD, NH, NKV = 64, 16, 4
DFF = 2816
FT = DFF // P
N0 = 3 * NH * HD
NQ1 = NH * HD
N1 = NQ1 + 6 * NKV * HD + 3 * NH
KVW = NKV * HD
WIN = 512
NWB = WIN // P
NCS = PAST // 16 - 1
NCP = TP // 16 - 1
CH = 256
EPS = 1e-6
SC = HD ** -0.5
NEG = -1e30
WT = (P, P, TS)
SLOTS = 3
SLOTW = 4096
PCMP_BANKS = (0, 1, 6, 7)
GU_FIRST, GU_BODY = 2, SLOTS
SP_ITS = (FT // 2 - SLOTS) // SLOTS
GU_ITS = (FT // 2 - GU_FIRST) // GU_BODY
RW = 1060
GATE_ORDER = (1, 2, 0)


def constants():
    c = {}
    c["ident"] = np.eye(P)
    c["mean"] = np.full((P, P), 1.0 / D)
    r = np.arange(P)
    same = (r[:, None] // 16 == r[None, :] // 16) & (r[:, None] % 4 == r[None, :] % 4)
    c["group"] = same * 1.0
    q = r[:, None]
    k = np.arange(P)[None, :]
    diag = np.where(k <= q, 0.0, NEG)
    c["causal"] = np.concatenate([diag, np.zeros((P, P)), diag], 1)
    c["strict"] = (k < q) * 1.0
    c["notpast"] = (k >= q) * 1.0
    half = HD // 2
    inv = np.power(np.float32(10000.0), -np.arange(half, dtype=np.float32) / np.float32(half)).astype(np.float32)
    pos = np.stack([r, P + r, PAST + r % NQ], 1).astype(np.float32)
    ang = (pos[:, :, None] * inv[None, None, :]).astype(np.float32)
    co, si = np.cos(ang).astype(np.float32), np.sin(ang).astype(np.float32)
    c["cos"] = np.concatenate([co, co], 2).reshape(P, -1)
    c["sin"] = np.concatenate([-si, si], 2).reshape(P, -1)
    n = np.arange(NCP)[None, :]
    c["cmpcausal"] = np.concatenate([np.where(16 * n + 31 <= q + P * t, 0.0, NEG) for t in range(2)], 1)
    c["cmpany"] = np.concatenate([(q + P * t >= 31) * 1.0 for t in range(2)], 1)
    tok = np.arange(TS)[None, :]
    for name, per in (("0", 32), ("1", 64)):
        ok, past = [], []
        for g in range(NB * per // P):
            b = g * (P // per) + q // per
            ok.append((tok // NQ == b) & (tok % NQ <= q % NQ))
            past.append((tok // NQ == b) & (tok % NQ < q % NQ))
        c["newneg" + name] = np.where(np.concatenate(ok, 1), 0.0, NEG)
        if name == "0":
            c["newpast"] = np.concatenate(past, 1) * 1.0
            c["newnot"] = 1.0 - c["newpast"]
    c["winneg"] = np.where(np.arange(NQ)[None, :] > q % NQ, 0.0, NEG)
    c["head0"] = (np.arange(8)[None, :] == (q % 32) // 4) * 1.0
    c["head1"] = (np.arange(NKV)[None, :] == (q % 64) // 16) * 1.0
    c["rank"] = np.broadcast_to(np.arange(1, 17)[None, :], (P, 16))
    at, off = 0, {}
    for name, a in c.items():
        off[name] = (at, a.shape[1])
        at += a.shape[1]
    return np.ascontiguousarray(np.concatenate(list(c.values()), 1).astype(np.float32)), off


def trunk(nc, off, x_prompt, x_sample, cache_kv0, cache_kv1, state_win, page_table, w_in0, w_out0, w_in1, w_out1,
          cmp_w1, cmp_w2, w_gu, w_down, consts, gcol, grow, pecol,
          y_prompt, y_sample, kv0_prompt, kv0_sample, kv1_prompt, kv1_sample, win_prompt, win_sample, gate_scratch):
    ctx = ExitStack()
    with ctx:
        def sb(name, cols, dt=F32, rows=P):
            return ctx.enter_context(nc.sbuf_tensor(name, [rows, cols], dt))

        def sem(name):
            return ctx.enter_context(nc.semaphore(name))

        hT = sb("hT", KD * T)[:].rearrange("p (k t) -> p k t", t=T)
        xT = sb("xT", KD * T)[:].rearrange("p (k t) -> p k t", t=T)
        oT = xT
        ring = sb("ring", SLOTS * SLOTW)[:].rearrange("p (s n) -> p s n", s=SLOTS)
        proj_t = sb("proj", 3 * N0)
        proj = proj_t[:].rearrange("p (t n) -> p t n", t=3)

        def w1r(k, i):
            m = 16 * k + i
            t, c = (m // 8, m % 8) if m < 24 else ((m - 24) // 4, 8 + m % 4)
            return proj[:, t, c * CH:(c + 1) * CH]

        qT = sb("qT", KD * T)[:].rearrange("p (k t) -> p k t", t=T)
        kT = sb("kT", KD * T)[:].rearrange("p (k t) -> p k t", t=T)
        x2T, sqT = qT, kT
        big = sb("big", 2 * 8 * 512)
        KT = big[:].rearrange("p (b i n) -> p b i n", b=2, i=8)
        actT = big[:, 0:FT * T].rearrange("p (f t) -> p f t", t=T)
        XTp = big[:, 0:8 * P].rearrange("p (i n) -> p i n", i=8)
        PTp = big[:, 2048:4096].rearrange("p (b n) -> p b n", b=2)
        R = sb("rows", 4 * RW)[:].rearrange("p (r n) -> p r n", r=4)
        pq = sb("pq", 2944)
        qb0 = pq[:, 0:2048].rearrange("p (b i c) -> p b i c", b=NB, i=8)
        PT0 = pq[:, 0:2304].rearrange("p (y c n) -> p y c n", y=2, c=9)
        qb1 = pq[:, 0:1024].rearrange("p (b i c) -> p b i c", b=NB, i=2)
        PT1 = pq[:, 1024:2944].rearrange("p (j n) -> p j n", j=15)
        pew = pq[:, 2304:2304 + 2 * CH]
        hid = pq[:, 2304:2304 + 2 * 252].rearrange("p (j n) -> p j n", j=2)
        hidp = pq[:, 2304:2304 + 4 * 60].rearrange("p (j n) -> p j n", j=4)
        kc = sb("kc", NB * 2 * NCS)[:].rearrange("p (b i n) -> p b i n", b=NB, i=2)
        vc = sb("vc", NB * KVW)[:].rearrange("p (b n) -> p b n", b=NB)
        kcp = sb("kcp", NKV * NCP)[:].rearrange("p (h n) -> p h n", h=NKV)
        vcp = sb("vcp", KVW)
        w2 = sb("w2", 4 * HD)[:].rearrange("p (k h n) -> p k h n", k=2, h=2)
        ct = sb("ct", sum(n for _, n in off.values()))
        gc = sb("gc", 4 * KD)
        gr = sb("gr", 6 * HD)
        pec = sb("pec", 32)
        cb = sb("cb", 4)
        rt = sb("rt", 3)
        rst = R[:, 3, 0:T]
        smp_t = sb("smp", 2 * P)
        smp = smp_t[:].rearrange("p (b n) -> p b n", b=2)
        pages = sb("pages", NB * NPG, I32, 1)
        ss = sb("ss", 3 * 28)[:].rearrange("p (t n) -> p t n", t=3)
        gates = sb("gates", 3 * 48)[:].rearrange("p (t n) -> p t n", t=3)
        gp = sb("gp", NH * 6)[:].rearrange("p (h n) -> p h n", h=NH)
        gs = sb("gs", 12)[:].rearrange("p (g n) -> p g n", g=4)
        st = sb("st", 96)
        osm = sb("osm", 2 * HD)[:].rearrange("p (b n) -> p b n", b=2)
        ps = [ctx.enter_context(nc.psum_tensor(f"ps{i}", [P, 512], F32)) for i in range(8)]

        def C(name, a=0, b=None, rows=P):
            o, n = off[name]
            return ct[0:rows, o + a:o + (n if b is None else b)]

        zero = C("causal", P, P + 1)
        ident = C("ident")

        def rep(ap, axis, n):
            a = ap.unsqueeze(axis)
            shape = list(a.shape)
            shape[axis] = n
            return a.broadcast_to(shape)

        s_page, s_x, s_first, s_const, s_kv, s_out, s_w1 = (sem(n) for n in ("s_page", "s_x", "s_first", "s_const", "s_kv", "s_out", "s_w1"))
        s_slot = [sem(f"s_slot{i}") for i in range(SLOTS)]
        s_half = [sem(f"s_half{i}") for i in range(SLOTS)]
        x_t, x_e, y_t, y_e = sem("x_turned"), sem("x_kept"), sem("y_turned"), sem("y_kept")
        n_sq = [sem(f"squares{i}") for i in range(4)]
        n_ps = [sem(f"meansq{i}") for i in range(4)]
        n_rc = [sem(f"recip{i}") for i in range(4)]
        n_rs = [sem(f"rstd{i}") for i in range(4)]
        n_x = [sem(f"normed{i}") for i in range(4)]
        L2 = range(2)
        in_p, in_e, in_q = ([sem(f"{n}{i}") for i in L2] for n in ("in_done", "in_kept", "in_sample_kept"))
        q_rc, q_rs, q_d = [sem(f"qk_recip{i}") for i in L2], [sem(f"qk_rstd{i}") for i in L2], [sem(f"roped{i}") for i in L2]
        t_p, t_e = [sem(f"qk_turned{i}") for i in L2], [sem(f"qk_kept{i}") for i in L2]
        a_s, a_g, a_m = [sem(f"pscores{i}") for i in L2], sem("psigmoids"), [sem(f"pmax{i}") for i in L2]
        a_e, a_w, a_t = [sem(f"pexp{i}") for i in L2], [sem(f"pweights{i}") for i in L2], [sem(f"pturned{i}") for i in L2]
        a_te, a_pv, a_oe = [sem(f"pkept{i}") for i in L2], [sem(f"pvdone{i}") for i in L2], [sem(f"pokept{i}") for i in L2]
        qb_z, qb_d = [sem(f"qb_zero{i}") for i in L2], [sem(f"qb_ready{i}") for i in L2]
        k_p, k_a, k_d = ([sem(f"{n}{i}") for i in range(3)] for n in ("k_turned", "k_kept_act", "k_kept_dve"))
        k_s, k_n = [sem(f"dscores{i}") for i in L2], [sem(f"dnew{i}") for i in L2]
        r_sg, r_ps = sem("dsigmoids"), [sem(f"scores_read{i}") for i in L2]
        r_m, r_e = [sem(f"dmax{i}") for i in L2], [sem(f"dexp{i}") for i in L2]
        r_w, r_t, r_te = [sem(f"dweights{i}") for i in L2], [sem(f"dturned{i}") for i in L2], [sem(f"dkept{i}") for i in L2]
        v_c, v_x = [sem(f"pv_chunk{i}") for i in L2], [sem(f"heads_picked{i}") for i in L2]
        v_t, v_e = [sem(f"o_turned{i}") for i in L2], [sem(f"o_kept{i}") for i in L2]
        i_m, i_e, i_w, i_p = sem("cmp_max"), sem("cmp_exp"), sem("cmp_probs"), sem("importance")
        i_r = sem("importance_read")
        c_b, c_be, c_h, c_he, c_w, c_we = (sem(n) for n in ("cmp_bias", "cmp_bias_kept", "cmp_hidden", "cmp_silu", "cmp_out", "cmp_kept"))
        p_h, p_he, p_w, p_we = (sem(n) for n in ("pcmp_hidden", "pcmp_silu", "pcmp_out", "pcmp_kept"))
        g_s, g_d, g_l, g_p = sem("gates_done"), sem("gates_stored"), sem("gates_rows"), sem("gates_prompt")
        o_p, o_e = [sem(f"out_done{i}") for i in L2], [sem(f"out_added{i}") for i in L2]
        u_p, u_g, u_u, u_a, u_e = ([sem(f"{n}{i}") for i in L2] for n in ("gu_done", "g_scaled", "u_scaled", "silu_done", "act_kept"))
        c_a = sem("pe_times_w1")
        d_p, d_e = [sem(f"down_done{i}") for i in L2], [sem(f"down_added{i}") for i in L2]
        ch, pch = sem("vector_chain"), sem("pool_chain")

        nin = [[min(512, n - c) for c in range(0, n, 512)] for n in (N0, N1)]
        IN_ORDER = ([1, 3, 0, 2, 4, 5], [0, 1, 2, 3, 5, 4])
        ROPED = ([(1, 512, 8, 0), (3, 1536, 8, 1)],
                 [(0, 0, 8, 2), (1, 512, 8, 2), (2, NQ1, 4, 3), (3, NQ1 + 2 * KVW, 4, 4), (4, NQ1 + 4 * KVW, 4, 5)])

        def full_chunks(l, pos):
            return sum(nin[l][n] == 512 for n in IN_ORDER[l][:pos + 1])

        w_in = [w_in0[0].rearrange("(k p) n -> p k n", p=P), w_in1[0].rearrange("(k p) n -> p k n", p=P)]
        w_out = [w_out0[0].rearrange("(k p) n -> p k n", p=P), w_out1[0].rearrange("(k p) n -> p k n", p=P)]
        w1_h = cmp_w1[0].rearrange("k (i p) n -> p k i n", p=P)

        plan = []

        for i, n in enumerate(IN_ORDER[0]):
            plan.append((("in", 0, n), in_p[0], 3 * (i + 1)))
        plan.insert(1, (("late",), None, 0))
        for cc in range(16):
            plan.append((("k0", cc // 2, cc % 2), k_p[0], 8 * (cc + 1)))
            if cc in (2, 3):
                plan.append((("w1r", cc - 2), None, 0))

        steps, nc_steps = [], 0
        for b in range(NB):
            if b % 4 == 0:
                steps.append(("turn", b // 4))
            for half in range(2):
                steps.append(("v", b, half))
                if b >= 1:
                    for _ in range(4):
                        steps.append(("c", nc_steps))
                        nc_steps += 1
            if b % 2 == 1:
                steps.append(("pick", b // 2))
                if b >= 3:
                    steps.append(("back", b // 2 - 1))
        steps += [("c", n) for n in range(nc_steps, 8 * (NB + 1))]
        steps.append(("back", 3))
        for step in steps:
            if step[0] == "v":
                plan.append((("v0", step[1], step[2]), v_c[0], 2 * step[1] + step[2] + 1))
            elif step[0] == "c" and step[1] % 8 == 0 and step[1] // 8 < NB:
                plan.append((("cmp", step[1] // 8), k_p[1], step[1] + 8))

        def ffn_plan(l):
            for n in range(2):
                plan.append((("out", l, n), o_p[l], 4 * (n + 1)))
            for n in range(FT // 2):
                plan.append((("gu", l, n), u_p[l], 2 * (n + 1)))
            for n in range(8):
                plan.append((("down", l, n), d_p[l], n + 1))

        ffn_plan(0)
        for i, n in enumerate(IN_ORDER[1]):
            plan.append((("in", 1, n), in_p[1], 3 * (i + 1)))
        for k in range(2):
            plan.append((("w1", k), p_h, 2 * (k + 1)))
        order = [("k1", 0), ("k1", 1)]
        for g in range(4):
            order += [("k1", 2 * g + 2)] if g < 3 else []
            order += [("v1", 2 * g - 2), ("v1", 2 * g - 1)] if g >= 1 else []
            order += [("k1", 2 * g + 3)] if g < 3 else []
        order += [("v1", 6), ("v1", 7)]
        for kind, b in order:
            plan.append(((kind, b),) + ((k_p[2], 6 * (b + 1)) if kind == "k1" else (v_c[1], 2 * (b // 2) + 2)))
        ffn_plan(1)

        place, landed, fill = {}, {}, [0] * SLOTS
        landed_half, fill_half = {}, [0] * SLOTS
        ringed = [e for e in plan if e[2]]

        def n_dmas(name):
            return {"k0": 4, "v0": 4, "gu": 2, "cmp": NPG, "k1": NPG // 2 + 1, "v1": NPG // 2 + 1}.get(name[0], 1)

        for i, e in enumerate(ringed):
            s = i % SLOTS
            fill[s] += 16 * n_dmas(e[0])
            place[e[0]], landed[e[0]] = s, fill[s]
            if e[0][0] in ("k1", "v1"):
                fill_half[s] += 16 * (NPG // 2)
                landed_half[e[0]] = fill_half[s]

        def take(eng, *name):
            s = place[name]
            eng.wait_ge(s_slot[s], landed[name])
            if name in landed_half:
                eng.wait_ge(s_half[s], landed_half[name])
            return ring[:, s, :]

        def page(eng, b, pg):
            return bass.ds(eng.value_load(pages[0:1, b * NPG + pg:b * NPG + pg + 1], min_val=0,
                                          max_val=cache_kv0.shape[1] - 1), 1)

        def page_jobs1(slot, kind, b):
            c = cache_kv1[0].rearrange("g s kv h d -> g s kv (h d)")
            return [(slot[:, r * KVW:(r + 1) * KVW], (c, b, r, 2 + (kind == "v1"))) for r in range(NPG)]

        def kept_k1(eng, b, i):
            if b % 2 == 0 and i % 2 == 1:
                eng.wait_ge(k_d[2], 3 * (b // 2) + i // 2 + 1)
            else:
                eng.wait_ge(k_a[2], 9 * (b // 2) + (3 + i + 1 if b % 2 else i // 2 + 1))

        block = ctx.enter_context(nc.Block())

        @block.sync
        def _(sp):
            n_first = off["group"][0]
            sp.dma_start(ct[:, 0:n_first], consts[:, 0:n_first]).then_inc(s_first, 16)
            for t in range(2):
                sp.dma_start(proj[:, t, 0:D], x_prompt[0, t * P:(t + 1) * P, :]).then_inc(s_x, 16)
            sp.dma_start(proj[0:TS, 2, 0:D], x_sample.rearrange("b q d -> (b q) d")).then_inc(s_x, 16)
            sp.dma_start(gc[:], gcol).then_inc(s_first, 16)
            sp.dma_start(pages[:], page_table.rearrange("b n -> (b n)").unsqueeze(0)).then_inc(s_page, 16)

            def late_constants():
                sp.dma_start(ct[:, n_first:], consts[:, n_first:]).then_inc(s_const, 16)
                sp.dma_start(gr[:], grow).then_inc(s_const, 16)
                sp.dma_start(pec[:], pecol).then_inc(s_const, 16)
                sp.dma_start(w2[:, :, :, :], cmp_w2[0].rearrange("k (h p) n -> p k h n", p=P)).then_inc(s_const, 16)
            sp.wait_ge(s_page, 16)

            i = 0
            for name, _, _ in plan:
                kind = name[0]
                if kind == "gu" and SLOTS <= name[2] < SLOTS + SP_ITS * SLOTS:
                    l, n = name[1:]
                    if n == SLOTS:
                        w = w_gu[l].rearrange("(k p) n -> p k n", p=P)
                        with sp.Fori(0, SP_ITS) as it:
                            for m in range(SLOTS):
                                s = (i + m) % SLOTS
                                sp.wait_ge(u_p[l], 2 * SLOTS * it + 2 * (m + 1))
                                d = ring[:, s, :].rearrange("p (k n) -> p k n", k=8)
                                for j in range(2):
                                    sp.dma_start(d[:, :, j * 256:(j + 1) * 256],
                                                 w[:, :, bass.ds(SLOTS * 256 * it + (j * DFF + (SLOTS + m) * 256), 256)]
                                                 ).then_inc(s_slot[s], 16)
                    i += 1
                    continue
                if kind == "late":
                    late_constants()
                    continue
                if kind == "w1r":
                    if name[1] == 0:
                        sp.wait_ge(t_p[0], 12)
                        sp.wait_ge(s_kv, 48)
                        for t in range(3):
                            sp.dma_start(proj[:, t, 0:8 * CH].rearrange("p (i n) -> p i n", n=CH),
                                         w1_h[:, t // 2, 8 * (t % 2):8 * (t % 2) + 8, :]).then_inc(s_w1, 16)
                    else:
                        sp.wait_ge(a_pv[0], NH)
                        for t in range(2):
                            sp.dma_start(proj[:, t, 8 * CH:12 * CH].rearrange("p (i n) -> p i n", n=CH),
                                         w1_h[:, 1, 8 + 4 * t:12 + 4 * t, :]).then_inc(s_w1, 16)
                    continue
                if i >= SLOTS:
                    _, freed, value = ringed[i - SLOTS]
                    sp.wait_ge(freed, value)
                s = i % SLOTS
                slot = ring[:, s, :]
                i += 1
                if kind == "in":
                    l, n = name[1:]
                    w = nin[l][n]
                    jobs = [(slot[:, 0:8 * w].rearrange("p (k n) -> p k n", k=8), w_in[l][:, :, n * 512:n * 512 + w])]
                elif kind == "out":
                    l, n = name[1:]
                    jobs = [(slot.rearrange("p (k n) -> p k n", k=8), w_out[l][:, :, n * 512:(n + 1) * 512])]
                elif kind == "gu":
                    l, n = name[1:]
                    w = w_gu[l].rearrange("(k p) n -> p k n", p=P)
                    d = slot.rearrange("p (k n) -> p k n", k=8)
                    jobs = [(d[:, :, j * 256:(j + 1) * 256], w[:, :, j * DFF + n * 256:j * DFF + (n + 1) * 256])
                            for j in range(2)]
                elif kind == "down":
                    l, n = name[1:]
                    w = w_down[l].rearrange("(k p) n -> p k n", p=P)
                    jobs = [(slot[:, 0:11 * 256].rearrange("p (k n) -> p k n", k=11),
                             w[:, (n % 2) * 11:(n % 2 + 1) * 11, (n // 2) * 256:(n // 2 + 1) * 256])]
                elif kind in ("k0", "v0"):
                    b, half = name[1:]
                    c = cache_kv0[0].rearrange("g s two h d -> g s two (h d)")
                    jobs = [(slot[:, r * D:(r + 1) * D], (c, b, half * 4 + r, int(kind == "v0"))) for r in range(4)]
                elif kind == "cmp":
                    c = cache_kv1[0].rearrange("g s (two kv) h d -> g s two (kv h d)", two=2)
                    jobs = [(slot[:, r * 512:(r + 1) * 512], (c, name[1], r, 0)) for r in range(NPG)]
                elif kind in ("k1", "v1"):
                    b, v = name[1], int(kind == "v1")
                    jobs = page_jobs1(slot, kind, b)[:NPG // 2]
                    jobs.append((slot[:, NPG * KVW:(NPG + NWB) * KVW].rearrange("p (r n) -> p r n", r=NWB),
                                 state_win[0, b].rearrange("(r p) two h d -> p r two (h d)", p=P)[:, :, v, :]))
                else:
                    jobs = [(slot.rearrange("p (i n) -> p i n", i=16), w1_h[:, name[1]])]
                assert len(jobs) == n_dmas(name)
                for dst, src in jobs:
                    if isinstance(src, tuple):
                        c, b, pg, part = src
                        src = c[page(sp, b, pg), :, part, :].rearrange("g s n -> (g s) n")
                    sp.dma_start(dst, src).then_inc(s_slot[s], 16)

        @block.tensor
        def _(pe):
            mm = nc.tensor.matmul

            def turn(out, in_, rows=P):
                return nc.tensor.transpose(out, in_, C("ident", 0, rows, rows))

            pe.wait_ge(s_x, 48)
            pe.wait_ge(s_first, 32)
            for t in range(3):
                for j in range(2):
                    for i in range(4):
                        last = turn(ps[2 * t + j][:, i * P:i * P + WT[t]],
                                    proj[0:WT[t], t, (4 * j + i) * P:(4 * j + i + 1) * P], WT[t])
                    last.then_inc(x_t, 1)

            def mean_rows(i):
                pe.wait_ge(n_sq[i], KD)
                for t in range(2):
                    for k in range(KD):
                        mm(ps[7][:, t:t + 1], sqT[:, k, t * P:(t + 1) * P], C("mean", 0, 1), start=k == 0, stop=k == KD - 1)
                for j in range(4):
                    for k in range(KD):
                        last = mm(ps[7][32 * j:32 * j + 32, 2:3], sqT[:, k, TP:T], C("mean", 0, 1), start=k == 0, stop=k == KD - 1)
                last.then_inc(n_ps[i], 1)

            def mean_cols(i):
                pe.wait_ge(n_sq[i], KD)
                for k in range(KD):
                    last = mm(ps[7][:, 0:T], C("mean"), sqT[:, k, :], start=k == 0, stop=k == KD - 1)
                last.then_inc(n_ps[i], 1)

            def project_in(l):
                for i, n in enumerate(IN_ORDER[l]):
                    w = nin[l][n]
                    src = take(pe, "in", l, n)[:, 0:8 * w].rearrange("p (k n) -> p k n", k=8)
                    if i >= 2:
                        pe.wait_ge(in_e[l], 3 * (i - 1))
                    b = (i % 2) * 3
                    for t in range(2):
                        for k in range(KD):
                            if i == 0 and t == 0:
                                pe.wait_ge(n_x[2 * l], k + 1)
                            last = mm(ps[b + t][:, 0:w], xT[:, k, t * P:(t + 1) * P], src[:, k, :], start=k == 0, stop=k == KD - 1)
                        last.then_inc(in_p[l], 1)
                    if w == 512:
                        for k in range(KD):
                            for j in range(4):
                                last = mm(ps[b + 2][32 * j:32 * j + 32, 0:P], xT[:, k, TP:T], src[:, k, j * P:(j + 1) * P],
                                          start=k == 0, stop=k == KD - 1)
                    else:
                        for k in range(KD):
                            last = mm(ps[b + 2][0:TS, 0:w], xT[:, k, TP:T], src[:, k, :], start=k == 0, stop=k == KD - 1)
                    last.then_inc(in_p[l], 1)
                    if i == 0:
                        mean_rows(2 * l)

            def turn_qk(l, lo, hi):
                if l == 0:
                    groups = [(t, c) for t in range(3) for c in (0, 512, 1024, 1536)]
                else:
                    groups = [(t, c) for t in range(3) for c in (0, 512)] + [(t, 1024) for t in range(2)] + \
                             [(t, None) for t in range(3)]
                for i in range(lo, hi):
                    t, c = groups[i]
                    if i >= 6:
                        pe.wait_ge(t_e[l], i - 5)
                    cols = [c + j * P for j in range(4)] if c is not None else [1536, 1664, 2048, 2176]
                    for j, a in enumerate(cols):
                        last = turn(ps[i % 6][:, j * P:j * P + WT[t]], proj[0:WT[t], t, a:a + P], WT[t])
                    last.then_inc(t_p[l], 1)
                if hi < 11 or l == 0:
                    pe.wait_ge(t_e[l], hi)

            def prompt0():
                def scores(h):
                    if h >= 10:
                        pe.wait_ge(a_m[0], h - 9)
                    elif h >= 2:
                        pe.wait_ge(a_g, h - 1)
                    hb = 64 * (h % 2)
                    q, k = qT[hb:hb + 64, h // 2, :], kT[hb:hb + 64, h // 2, :]
                    mm(ps[h % 2][:, 0:P], q[:, 0:P], k[:, 0:P], start=True, stop=True)
                    mm(ps[h % 2][:, P:3 * P], q[:, P:2 * P], k[:, 0:2 * P], start=True, stop=True).then_inc(a_s[0], 1)

                def turn_w(h):
                    pe.wait_ge(a_w[0], h + 1)
                    if h >= 2:
                        pe.wait_ge(a_te[0], h - 1)
                    for j in range(3):
                        last = turn(ps[2 + h % 2][:, j * P:(j + 1) * P], R[:, 3, (h % 2) * 384 + j * P:(h % 2) * 384 + (j + 1) * P])
                    last.then_inc(a_t[0], 1)

                def values(h):
                    pe.wait_ge(a_te[0], h + 1)
                    if h >= 4 and h % 2 == 0:
                        pe.wait_ge(a_oe[0], h // 2 - 1)
                    o = ps[4 + (h // 2) % 2][64 * (h % 2):64 * (h % 2) + 64, 0:TP]
                    v = 2 * D + h * HD
                    mm(o, proj[:, 0, v:v + HD], PTp[:, h % 2, 0:256], start=True, stop=False)
                    mm(o[:, P:2 * P], proj[:, 1, v:v + HD], PTp[:, h % 2, 256:384], start=False, stop=True).then_inc(a_pv[0], 1)

                scores(0)
                scores(1)
                for h in range(NH + 1):
                    if h + 2 < NH:
                        scores(h + 2)
                    if h >= 1:
                        values(h - 1)
                    if h < NH:
                        turn_w(h)

            def decode_k0():
                pe.wait_ge(qb_d[0], 1)
                for cc in range(17):
                    if cc < 16:
                        src = take(pe, "k0", cc // 2, cc % 2)
                    for p in range(8):
                        if cc < 16:
                            i = cc * 8 + p
                            if i >= 3:
                                pe.wait_ge((k_a, k_d)[(i - 3) % 2][0], (i - 3) // 2 + 1)
                            elif i == 0:
                                pe.wait_ge(a_oe[0], 8)
                            for r in range(4):
                                last = turn(ps[5 + i % 3][:, r * P:(r + 1) * P], src[:, r * D + p * P:r * D + (p + 1) * P])
                            last.then_inc(k_p[0], 1)
                        if cc >= 1:
                            c = cc - 1
                            b, half = c // 2, c % 2
                            bl = b % 4
                            i = c * 8 + p
                            pe.wait_ge((k_a, k_d)[i % 2][0], i // 2 + 1)
                            if c == 8 and p == 0:
                                pe.wait_ge(r_ps[0], 1)
                                pe.wait_ge(r_sg, 1)
                            mm(ps[(p // 4) * 2 + half][32 * bl:32 * bl + 32, :], qb0[:, b, p, :], KT[:, c % 2, p, :],
                               start=p % 4 == 0, stop=p % 4 == 3).then_inc(k_s[0], 1)
                    if cc >= 1 and (cc - 1) % 2 == 1:
                        b = (cc - 1) // 2
                        bl = b % 4
                        for p in range(8):
                            last = mm(ps[4][32 * bl:32 * bl + 32, (p // 4) * 32:(p // 4) * 32 + 32], qb0[:, b, p, :],
                                      kT[:, p, TP:T], start=p % 4 == 0, stop=p % 4 == 3)
                        last.then_inc(k_n[0], 1)

            def turn_o(l, i):
                pe.wait_ge(v_x[l], i + 1)
                if i >= 1:
                    pe.wait_ge(v_e[l], i)
                if l == 1:
                    pe.wait_ge(i_r, min(i + 3, 4))
                turn(ps[4][0:64, P:2 * P], osm[:, i % 2, :]).then_inc(v_t[l], 1)

            def turn_weights0(g):
                pe.wait_ge(r_w[0], 2 * (g + 1))
                for i in range(6):
                    y, c0 = i // 3, 4 * (i % 3)
                    n = g * 6 + i
                    if n >= 1:
                        pe.wait_ge(r_te[0], n)
                    for c in range(c0, min(c0 + 4, 9)):
                        w = P if c < 8 else TS
                        last = turn(ps[7][0:w, (c - c0) * P:(c - c0 + 1) * P], R[:, 3 * y, c * P:c * P + w])
                    last.then_inc(r_t[0], 1)
                pe.wait_ge(r_te[0], 6 * (g + 1))

            def values0(b, half):
                bl = b % 4
                if b % 2 == 0 and half == 0 and b >= 2:
                    pe.wait_ge(v_x[0], b // 2)
                src = take(pe, "v0", b, half)
                for r in range(4):
                    c = half * 4 + r
                    for y in range(2):
                        lo = (bl % 2) * 64 + y * 32
                        last = mm(ps[5][lo:lo + 32, :], PT0[:, y, c, 32 * bl:32 * bl + 32],
                                  src[:, r * D + y * 512:r * D + (y + 1) * 512], start=c == 0, stop=False)
                if half == 1:
                    for y in range(2):
                        lo = (bl % 2) * 64 + y * 32
                        last = mm(ps[5][lo:lo + 32, :], PT0[0:TS, y, 8, 32 * bl:32 * bl + 32],
                                  proj[0:TS, 2, 2 * D + y * 512:2 * D + (y + 1) * 512], start=False, stop=True)
                last.then_inc(v_c[0], 1)

            def project_out(l):
                for n in range(2):
                    src = take(pe, "out", l, n).rearrange("p (k n) -> p k n", k=8)
                    for j in range(4):
                        i = n * 4 + j
                        if i >= 4:
                            pe.wait_ge(o_e[l], i - 3)
                        for k in range(KD):
                            last = mm(ps[4 + j][:, 0:T], src[:, k, j * P:(j + 1) * P], oT[:, k, :], start=k == 0, stop=k == KD - 1)
                        last.then_inc(o_p[l], 1)

            def ffn(l):
                def gate_up(n, it=0):
                    slot = place[("gu", l, n)]
                    pe.wait_ge(s_slot[slot], 32 * it + landed[("gu", l, n)])
                    src = ring[:, slot, :].rearrange("p (k n) -> p k n", k=8)
                    for j in range(2):
                        f = 2 * n + j
                        if f >= 3:
                            pe.wait_ge(u_u[l], 2 * GU_BODY * it + f - 2)
                        for y in range(2):
                            for k in range(KD):
                                if f == 0 and y == 0:
                                    pe.wait_ge(n_x[2 * l + 1], k + 1)
                                last = mm(ps[2 * (f % 3) + y][:, 0:T], src[:, k, y * 256 + j * P:y * 256 + (j + 1) * P],
                                          x2T[:, k, :], start=k == 0, stop=k == KD - 1)
                        last.then_inc(u_p[l], 1)
                        if f == 0:
                            mean_cols(2 * l + 1)

                for n in range(GU_FIRST):
                    gate_up(n)
                with pe.Fori(0, GU_ITS) as it:
                    for n in range(GU_FIRST, GU_FIRST + GU_BODY):
                        gate_up(n, it)
                pe.wait_ge(u_e[l], FT)
                for n in range(8):
                    cg, kh = n // 2, n % 2
                    src = take(pe, "down", l, n)[:, 0:11 * 256].rearrange("p (k n) -> p k n", k=11)
                    if cg >= 2 and kh == 0:
                        pe.wait_ge(d_e[l], 2 * (cg - 1))
                    for j in range(2):
                        for k in range(11):
                            last = mm(ps[(cg % 2) * 2 + j][:, 0:T], src[:, k, j * P:(j + 1) * P], actT[:, kh * 11 + k, :],
                                      start=kh == 0 and k == 0, stop=kh == 1 and k == 10)
                    last.then_inc(d_p[l], 1)

            def second_k(b):
                pe.wait_ge(c_he, 4 * b + 2)
                if b >= 1:
                    pe.wait_ge(c_we, 2 * b)
                for par in range(2):
                    for kp in range(2):
                        for hf in range(2):
                            h = 2 * kp + par
                            last = mm(ps[6][par * 64:par * 64 + 64, kp * NCS:(kp + 1) * NCS], w2[:, 0, hf, :],
                                      hid[:, hf, h * NCS:(h + 1) * NCS], start=hf == 0, stop=hf == 1)
                last.then_inc(c_w, 1)

            def second_v(b):
                pe.wait_ge(c_he, 4 * b + 4)
                pe.wait_ge(c_we, 2 * b + 1)
                for h in range(NKV):
                    for hf in range(2):
                        last = mm(ps[6][0:NCS, P + h * HD:P + (h + 1) * HD], hid[:, hf, h * NCS:(h + 1) * NCS], w2[:, 1, hf, :],
                                  start=hf == 0, stop=hf == 1)
                last.then_inc(c_w, 1)

            cmp_src = [None]

            def compress(n):
                bb, i = n // 8, n % 8
                if n == 0:
                    pe.wait_ge(r_ps[0], 2)
                    pe.wait_ge(r_sg, 2)
                    pe.wait_ge(c_a, 1)
                    for j in range(4):
                        last = mm(ps[0][:, j:j + 1], pew[:, j * P:(j + 1) * P], C("mean", 0, 1), start=True, stop=True)
                    last.then_inc(c_b, 1)
                    pe.wait_ge(c_be, 1)
                if bb < NB:
                    if i == 0:
                        cmp_src[0] = take(pe, "cmp", bb)
                    for e in range(2 if i < 4 else 0):
                        m = 8 * bb + 2 * i + e
                        if m >= 2:
                            pe.wait_ge((k_a, k_d)[e][1], m // 2)
                        for r in range(4):
                            a = (4 * e + r) * 512 + i * P
                            last = turn(ps[2 + e][:, r * P:(r + 1) * P], cmp_src[0][:, a:a + P])
                        last.then_inc(k_p[1], 1)
                if bb >= 1:
                    b, j = bb - 1, i // 2
                    if i == 0:
                        pe.wait_ge(k_a[1], 4 * bb)
                        pe.wait_ge(k_d[1], 4 * bb)
                        if b == 0:
                            pe.wait_ge(s_w1, 80)
                    if i % 2 == 0 and 4 * b + j >= 2:
                        pe.wait_ge(c_he, 4 * b + j - 1)
                    for o in range(8 * (i % 2), 8 * (i % 2) + 8):
                        last = mm(ps[j % 2][:, 0:NKV * NCS], w1r(j // 2, o)[:, (j % 2) * P:(j % 2 + 1) * P],
                                  KT[:, b % 2, (j // 2) * 4:(j // 2) * 4 + 4, o:o + 8 * (NCS - 1) + 1:8],
                                  start=o == 0, stop=o == 15)
                    if i % 2 == 1:
                        last.then_inc(c_h, 1)
                    if i == 4:
                        second_k(b)
                    if i == 0 and b >= 1:
                        second_v(b - 1)
                    if n == 8 * (NB + 1) - 1:
                        second_v(b)

            def compress_prompt():
                for k in range(2):
                    if k == 1:
                        pe.wait_ge(q_d[1], 15)
                        turn_qk(1, 8, 11)
                    src = take(pe, "w1", k).rearrange("p (i n) -> p i n", i=16)
                    for hf in range(2):
                        for o in range(16):
                            last = mm(ps[PCMP_BANKS[2 * k + hf]][:, 0:NKV * NCP], src[:, o, hf * P:(hf + 1) * P],
                                      XTp[:, k * 4:k * 4 + 4, o:o + 8 * (NCP - 1) + 1:8], start=o == 0, stop=o == 15)
                        last.then_inc(p_h, 1)
                pe.wait_ge(t_e[1], 11)
                pe.wait_ge(p_he, 4)
                hv = hidp.rearrange("p j (h n) -> p j h n", h=NKV)
                for dh in range(2):
                    for hf in range(2):
                        mm(ps[5][dh * 64:dh * 64 + 64, 0:NKV * NCP], w2[:, 0, hf, :], hidp[:, hf, :], start=hf == 0, stop=hf == 1)
                for h in range(NKV):
                    for hf in range(2):
                        last = mm(ps[4][0:NCP, h * HD:(h + 1) * HD], hv[:, 2 + hf, h, :], w2[:, 1, hf, :],
                                  start=hf == 0, stop=hf == 1)
                last.then_inc(p_w, 1)
                pe.wait_ge(p_we, 1)

            def prompt1():
                def scores(h):
                    if h >= 2:
                        pe.wait_ge(a_m[1], h - 1)
                    hb, kv = 64 * (h % 2), h // 4
                    q = qT[hb:hb + 64, h // 2, :]
                    A, B = ps[2 * (h % 2)], ps[2 * (h % 2) + 1]
                    for br, bank in ((0, A), (1, B)):
                        k = kT[hb:hb + 64, 4 * br + kv, :]
                        mm(bank[:, 0:P], q[:, 0:P], k[:, 0:P], start=True, stop=True)
                        mm(bank[:, P:3 * P], q[:, P:2 * P], k[:, 0:2 * P], start=True, stop=True)
                    for t in range(2):
                        last = mm(A[:, 384 + t * NCP:384 + (t + 1) * NCP], q[:, t * P:(t + 1) * P], kcp[hb:hb + 64, kv, :],
                                  start=True, stop=True)
                    last.then_inc(a_s[1], 1)

                def turn_w(h):
                    pe.wait_ge(a_w[1], h + 1)
                    if h >= 1:
                        pe.wait_ge(a_te[1], h)
                    W = R[:, h % 3, :]
                    for br in range(2):
                        for j in range(3):
                            turn(ps[4 + br][:, j * P:(j + 1) * P], W[:, br * 384 + j * P:br * 384 + (j + 1) * P])
                    for t in range(2):
                        last = turn(ps[6][0:NCP, t * P:(t + 1) * P], W[:, 768 + t * NCP:768 + (t + 1) * NCP])
                    last.then_inc(a_t[1], 1)

                def values(h):
                    pe.wait_ge(a_te[1], h + 1)
                    if h >= 2 and h % 2 == 0:
                        pe.wait_ge(a_oe[1], h // 2)
                    kv = h // 4
                    o = ps[7][64 * (h % 2):64 * (h % 2) + 64, 0:TP]
                    X = PTp[:, h % 2, :]
                    mm(o, vcp[0:NCP, kv * HD:(kv + 1) * HD], X[0:NCP, 768:1024], start=True, stop=False)
                    for br in range(2):
                        v = NQ1 + (3 + 2 * br) * KVW + kv * HD
                        mm(o, proj[:, 0, v:v + HD], X[:, br * 384:br * 384 + 256], start=False, stop=False)
                        last = mm(o[:, P:2 * P], proj[:, 1, v:v + HD], X[:, br * 384 + 256:br * 384 + 384], start=False, stop=br == 1)
                    last.then_inc(a_pv[1], 1)

                scores(0)
                scores(1)
                for h in range(NH + 1):
                    if h + 2 < NH:
                        scores(h + 2)
                    if h >= 1:
                        values(h - 1)
                    if h < NH:
                        turn_w(h)

            def compressed_and_new(g):
                if g >= 1:
                    pe.wait_ge(r_ps[1], g)
                for b2 in range(2):
                    b, lo = 2 * g + b2, 64 * b2
                    for kp in range(2):
                        mm(ps[3][lo:lo + 64, 0:NCS], qb1[:, b, kp, :], kc[:, b, kp, :], start=kp == 0, stop=kp == 1)
                    for br in range(2):
                        for kp in range(2):
                            last = mm(ps[3][lo:lo + 64, 64 + 32 * br:96 + 32 * br], qb1[:, b, kp, :],
                                      kT[:, 2 * br + kp, TP:T], start=kp == 0, stop=kp == 1)
                last.then_inc(k_n[1], 1)

            def turn_k1(src, b, i):
                if i >= 2:
                    kept_k1(pe, b, i - 2)
                elif b == 1 or (b >= 3 and b % 2 == 1):
                    kept_k1(pe, b - 1, i + 4)
                for r in range(4):
                    a = ((4 * (i % 2) + r) * KVW + (i // 2) * P) if i < 4 else (NPG + r) * KVW + (i - 4) * P
                    last = turn(ps[6 + i % 2][:, r * P:(r + 1) * P], src[:, a:a + P])
                last.then_inc(k_p[2], 1)

            def scores_k1(g, i):
                kept_k1(pe, 2 * g, i)
                kept_k1(pe, 2 * g + 1, i)
                kp, bank = (i // 2, i % 2) if i < 4 else (i - 4, 2)
                for b2 in range(2):
                    mm(ps[bank][64 * b2:64 * b2 + 64, :], qb1[:, 2 * g + b2, kp, :], KT[:, b2, i, :],
                       start=kp == 0, stop=kp == 1).then_inc(k_s[1], 1)

            def importance(g):
                pe.wait_ge(i_w, g + 1)
                if g >= 3:
                    pe.wait_ge(v_e[1], g - 2)
                mm(ps[4][:, 0:64], C("group"), R[:, 2, (g % 2) * 256:(g % 2) * 256 + 64], start=True, stop=True).then_inc(i_p, 1)

            def turn_weights1(g):
                if g < 3:
                    kept_k1(pe, 2 * g + 3, 5)
                pe.wait_ge(r_w[1], g + 1)
                for i in range(4):
                    if i >= 2:
                        pe.wait_ge(r_te[1], 4 * g + i - 1)
                    bank = ps[6 + i % 2]
                    if i < 3:
                        for c in range(4):
                            j = 4 * i + c
                            src = R[:, 0, j * P:(j + 1) * P] if j < 8 else R[:, 1, (j - 8) * P:(j - 7) * P]
                            last = turn(bank[:, c * P:(c + 1) * P], src)
                    else:
                        turn(bank[0:TS, 0:P], R[:, 0, PAST:PAST + TS])
                        turn(bank[0:TS, P:2 * P], R[:, 1, WIN:WIN + TS])
                        a = (g % 2) * 256 + 128
                        last = turn(bank[0:NCS, 2 * P:3 * P], R[:, 2, a:a + NCS])
                    last.then_inc(r_t[1], 1)

            def values1(g):
                pe.wait_ge(r_te[1], 4 * (g + 1))
                if g >= 1:
                    pe.wait_ge(v_x[1], g)
                src = [take(pe, "v1", 2 * g + b2) for b2 in range(2)]
                o = [ps[5][64 * b2:64 * b2 + 64, 0:KVW] for b2 in range(2)]
                for j in range(12):
                    for b2 in range(2):
                        mm(o[b2], PT1[:, j, 64 * b2:64 * b2 + 64], src[b2][:, j * KVW:(j + 1) * KVW], start=j == 0, stop=False)
                for br in range(2):
                    v = NQ1 + (3 + 2 * br) * KVW
                    for b2 in range(2):
                        mm(o[b2], PT1[0:TS, 12 + br, 64 * b2:64 * b2 + 64], proj[0:TS, 2, v:v + KVW], start=False, stop=False)
                for b2 in range(2):
                    mm(o[b2], PT1[0:NCS, 14, 64 * b2:64 * b2 + 64], vc[0:NCS, 2 * g + b2, :],
                       start=False, stop=True).then_inc(v_c[1], 1)

            project_in(0)
            pe.wait_ge(in_e[0], 3 * len(nin[0]))
            pe.wait_ge(in_q[0], full_chunks(0, 5))
            pe.wait_ge(q_d[0], 6)
            turn_qk(0, 0, 12)
            prompt0()
            decode_k0()
            for step in steps:
                if step[0] == "turn":
                    turn_weights0(step[1])
                elif step[0] == "v":
                    values0(*step[1:])
                elif step[0] == "back":
                    turn_o(0, step[1])
                elif step[0] == "c":
                    compress(step[1])
            pe.wait_ge(a_oe[0], 8)
            pe.wait_ge(v_e[0], 4)
            pe.wait_ge(c_we, 2 * NB)
            project_out(0)
            ffn(0)
            pe.wait_ge(d_e[0], 5)
            project_in(1)
            pe.wait_ge(in_e[1], 3 * len(nin[1]))
            pe.wait_ge(q_d[1], 6)
            turn_qk(1, 0, 6)
            pe.wait_ge(q_d[1], 9)
            turn_qk(1, 6, 8)
            compress_prompt()
            prompt1()
            pe.wait_ge(a_oe[1], 8)
            pe.wait_ge(qb_d[1], 1)
            compressed_and_new(0)
            for b in range(2):
                src = take(pe, "k1", b)
                for i in range(6):
                    turn_k1(src, b, i)
            importance(0)
            for g in range(4):
                if g < 3:
                    src = take(pe, "k1", 2 * g + 2)
                for i in range(6):
                    scores_k1(g, i)
                    if g < 3:
                        if g >= 1 and i == 0:
                            pe.wait_ge(r_te[1], 4 * g)
                        turn_k1(src, 2 * g + 2, i)
                if g >= 1:
                    values1(g - 1)
                if g < 3:
                    compressed_and_new(g + 1)
                    src = take(pe, "k1", 2 * g + 3)
                    for i in range(6):
                        turn_k1(src, 2 * g + 3, i)
                turn_weights1(g)
                if g < 3:
                    importance(g + 1)
                if g >= 1:
                    turn_o(1, g - 1)
            values1(3)
            turn_o(1, 3)
            pe.wait_ge(v_e[1], 4)
            project_out(1)
            ffn(1)
            pe.wait_ge(d_e[1], KD)
            for t in range(3):
                for j in range(2):
                    for i in range(4):
                        last = turn(ps[2 * t + j][0:WT[t], i * P:(i + 1) * P], hT[:, 4 * j + i, t * P:t * P + WT[t]])
                    last.then_inc(y_t, 1)

        @block.scalar
        def _(act):
            f = nc.scalar.activation

            def copy(out, in_):
                return f(out, in_, ACT.Copy)

            for t in range(3):
                for j in range(2):
                    act.wait_ge(x_t, 2 * t + j + 1)
                    v = ps[2 * t + j][:, :].rearrange("p (i n) -> p i n", i=4)
                    copy(hT[:, 4 * j:4 * j + 4, t * P:t * P + WT[t]], v[:, :, 0:WT[t]]).then_inc(x_e, 1)

            def squares(i, ready):
                for k in range(KD):
                    act.wait_ge(ready, k + 1 if i else 6)
                    f(sqT[:, k, :], hT[:, k, :], ACT.Square).then_inc(n_sq[i], 1)

            def project_in(l):
                def roots(pos):
                    h0 = 0
                    for gi, (n, _, H, _) in enumerate(ROPED[l]):
                        if IN_ORDER[l].index(n) == pos:
                            act.wait_ge(q_rc[l], gi + 1)
                            f(ss[:, 0:2, h0:h0 + H], ss[:, 0:2, h0:h0 + H], ACT.Sqrt)
                            f(ss[0:TS, 2, h0:h0 + H], ss[0:TS, 2, h0:h0 + H], ACT.Sqrt).then_inc(q_rs[l], 1)
                        h0 += H

                act.wait_ge(n_rc[2 * l], 1)
                f(rt[:, :], rt[:, :], ACT.Sqrt).then_inc(n_rs[2 * l], 1)
                act.wait_ge(n_rs[2 * l], 1)
                for i, n in enumerate(IN_ORDER[l]):
                    w = nin[l][n]
                    b = (i % 2) * 3
                    for t in range(2):
                        act.wait_ge(in_p[l], 3 * i + t + 1)
                        f(proj[:, t, n * 512:n * 512 + w], ps[b + t][:, 0:w], ACT.Copy, scale=rt[:, t:t + 1]).then_inc(in_e[l], 1)
                    act.wait_ge(in_p[l], 3 * i + 3)
                    if w == 512:
                        full = full_chunks(l, i)
                        if full > 2:
                            act.wait_ge(in_q[l], full - 2)
                        f(smp[:, full % 2, :], ps[b + 2][:, 0:P], ACT.Copy, scale=rt[:, 2:3]).then_inc(in_e[l], 1)
                    else:
                        f(proj[0:TS, 2, n * 512:n * 512 + w], ps[b + 2][0:TS, 0:w], ACT.Copy, scale=rt[0:TS, 2:3]).then_inc(in_e[l], 1)
                    if i >= 1:
                        roots(i - 1)
                if l == 1:
                    keep_qk(1, 0, 8)
                roots(len(nin[l]) - 1)

            def keep_qk(l, lo, hi):
                if l == 0:
                    i = 0
                    for t in range(3):
                        for dst, j in ((qT, 0), (qT, 4), (kT, 0), (kT, 4)):
                            act.wait_ge(t_p[0], i + 1)
                            v = ps[i % 6][:, :].rearrange("p (j n) -> p j n", j=4)
                            copy(dst[:, j:j + 4, t * P:t * P + WT[t]], v[:, :, 0:WT[t]]).then_inc(t_e[0], 1)
                            i += 1
                    return
                for i in range(lo, hi):
                    act.wait_ge(t_p[1], i + 1)
                    v = ps[i % 6][:, :].rearrange("p (j n) -> p j n", j=4)
                    if i < 6:
                        t, j = i // 2, 4 * (i % 2)
                        last = copy(qT[:, j:j + 4, t * P:t * P + WT[t]], v[:, :, 0:WT[t]])
                    elif i < 8:
                        t = i - 6
                        xd = XTp[:, :, t * 64:(t + 1) * 64].rearrange("p (j e) n -> p j e n", e=2)
                        for e in range(2):
                            for par in range(2):
                                last = copy(xd[par * 64:par * 64 + 64, :, e, :], v[e * 64:e * 64 + 64, :, par::2])
                    elif i < 10:
                        t = i - 8
                        kd = kT[:, :, t * P:(t + 1) * P].rearrange("p (j e) n -> p j e n", e=2)
                        for e in range(2):
                            for dh in range(2):
                                last = copy(kd[dh * 64:dh * 64 + 64, :, e, :], v[e * 64:e * 64 + 64, :, :])
                    else:
                        last = copy(kT[:, 0:4, TP:T], v[:, :, 0:TS])
                    last.then_inc(t_e[1], 1)

            def prompt0():
                def probs(h):
                    b = h % 2
                    act.wait_ge(a_s[0], h + 1)
                    if h < 8:
                        if h >= 2:
                            act.wait_ge(a_w[0], h - 1)
                        f(R[:, 0, b * 384:b * 384 + 384], ps[b][:, 0:384], ACT.Sigmoid, scale=SC)
                        f(R[:, 1, b * 384:b * 384 + 384], ps[b][:, 0:384], ACT.Sigmoid, scale=-SC).then_inc(a_g, 1)
                    else:
                        act.wait_ge(a_m[0], h - 7)
                        for t, (lo, hi) in enumerate(((0, 128), (128, 384))):
                            last = f(R[:, 1, b * 384 + lo:b * 384 + hi], R[:, 0, b * 384 + lo:b * 384 + hi], ACT.Exp,
                                     scale=SC, bias=st[:, 8 * b + 2 + t:8 * b + 3 + t], accum_out=st[:, 8 * b + 4 + t:8 * b + 5 + t])
                        last.then_inc(a_e[0], 1)

                def keep(h):
                    act.wait_ge(a_t[0], h + 1)
                    if h >= 2:
                        act.wait_ge(a_pv[0], h - 1)
                    copy(PTp[:, h % 2, 0:384], ps[2 + h % 2][:, 0:384]).then_inc(a_te[0], 1)

                def keep_out(h):
                    if h % 2 == 1:
                        act.wait_ge(a_pv[0], h + 1)
                        copy(oT[:, h // 2, 0:TP], ps[4 + (h // 2) % 2][:, 0:TP]).then_inc(a_oe[0], 1)

                probs(0)
                for h in range(NH):
                    if h + 1 < NH:
                        probs(h + 1)
                    if h >= 1:
                        keep_out(h - 1)
                    keep(h)
                keep_out(NH - 1)

            def keep_k0(g):
                for cc in range(9 * g, (9, 16)[g]):
                    for p in range(0, 8, 2):
                        i = cc * 8 + p
                        act.wait_ge(k_p[0], i + 1)
                        if cc >= 2:
                            act.wait_ge(k_s[0], 8 * (cc - 2) + p + 1)
                        copy(KT[:, cc % 2, p, :], ps[5 + i % 3][:, :]).then_inc(k_a[0], 1)

            def rows0(g):
                act.wait_ge(k_s[0], 64 * (g + 1))
                act.wait_ge(k_n[0], 4 * (g + 1))
                if g:
                    act.wait_ge(r_t[0], 6 * g)
                for row, s in ((0, SC), (1, -SC)):
                    for j in range(2):
                        f(R[:, row, j * 512:(j + 1) * 512], ps[j][:, :], ACT.Sigmoid, scale=s)
                    last = f(R[:, row, PAST:PAST + TS], ps[4][:, 0:32], ACT.Sigmoid, scale=s)
                last.then_inc(r_sg, 1)
                act.wait_ge(r_m[0], g + 1)
                f(R[:, 3, 0:PAST + TS], R[:, 3, 0:PAST + TS], ACT.Exp, scale=SC, bias=st[:, 40:41],
                  accum_out=st[:, 41:42]).then_inc(r_e[0], 1)

            def keep_o(l, i):
                act.wait_ge(v_t[l], i + 1)
                for b2 in range(2):
                    v = ps[4][0:64, P + 64 * b2:P + 64 * b2 + 64].rearrange("p (i e q) -> p i e q", e=2, q=NQ)
                    c = TP + (2 * i + b2) * NQ
                    for e in range(2):
                        last = copy(oT[e * 64:e * 64 + 64, :, c:c + NQ], v[:, :, e, :])
                last.then_inc(v_e[l], 1)

            def keep_p0(g):
                for i in range(6):
                    y, c0 = i // 3, 4 * (i % 3)
                    act.wait_ge(r_t[0], g * 6 + i + 1)
                    v = ps[7][:, :].rearrange("p (c n) -> p c n", c=4)
                    if i % 3 < 2:
                        last = copy(PT0[:, y, c0:c0 + 4, :], v)
                    else:
                        last = copy(PT0[0:TS, y, 8, :], v[0:TS, 0, :])
                    last.then_inc(r_te[0], 1)

            def ffn(l):
                act.wait_ge(n_rc[2 * l + 1], 1)
                f(rst, R[:, 3, T:2 * T], ACT.Sqrt).then_inc(n_rs[2 * l + 1], 1)

                def silu(j, it=0):
                    a = (j % 2) * T
                    act.wait_ge(u_g[l], 2 * it + j + 1)
                    if j >= 2:
                        act.wait_ge(u_e[l], 2 * it + j - 1)
                    f(R[:, 1, a:a + T], R[:, 0, a:a + T], ACT.Silu).then_inc(u_a[l], 1)

                silu(0)
                silu(1)
                with act.Fori(0, FT // 2 - 1) as it:
                    silu(2, it)
                    silu(3, it)

            def compress(n):
                bb, i = n // 8, n % 8
                if bb < NB and i < 4:
                    act.wait_ge(k_p[1], 8 * bb + 2 * i + 1)
                    if bb >= 2:
                        act.wait_ge(c_h, 4 * (bb - 1))
                    for e in range(2):
                        for par in range(2):
                            last = copy(KT[par * 64:par * 64 + 64, bb % 2, 2 * i + e, 0:256], ps[2][e * 64:e * 64 + 64, par::2])
                    last.then_inc(k_a[1], 1)
                if bb >= 1 and i % 2 == 1:
                    b, j = bb - 1, i // 2
                    act.wait_ge(c_be, 1)
                    act.wait_ge(c_h, 4 * b + j + 1)
                    if j >= 2 or b >= 1:
                        act.wait_ge(c_w, 2 * b + j // 2)
                    f(hid[:, j % 2, :], ps[j % 2][:, 0:NKV * NCS], ACT.Silu, bias=cb[:, j:j + 1]).then_inc(c_he, 1)

            def prompt1():
                def probs(h):
                    act.wait_ge(a_m[1], h + 1)
                    W, b = R[:, h % 3, :], 24 * (h % 3)
                    for j, (lo, hi) in enumerate(((0, 128), (128, 384), (384, 512), (512, 768), (768, 783), (783, 798))):
                        last = f(W[:, lo:hi], W[:, lo:hi], ACT.Exp, scale=SC, bias=st[:, b + 6 + j:b + 7 + j],
                                 accum_out=st[:, b + 12 + j:b + 13 + j])
                    last.then_inc(a_e[1], 1)

                def keep(h):
                    act.wait_ge(a_t[1], h + 1)
                    if h >= 2:
                        act.wait_ge(a_pv[1], h - 1)
                    X = PTp[:, h % 2, :]
                    copy(X[:, 0:384], ps[4][:, 0:384])
                    copy(X[:, 384:768], ps[5][:, 0:384])
                    copy(X[0:NCP, 768:1024], ps[6][0:NCP, 0:256]).then_inc(a_te[1], 1)

                def keep_out(h):
                    if h % 2 == 1:
                        act.wait_ge(a_pv[1], h + 1)
                        copy(oT[:, h // 2, 0:TP], ps[7][:, 0:TP]).then_inc(a_oe[1], 1)

                probs(0)
                for h in range(NH):
                    if h + 1 < NH:
                        probs(h + 1)
                    if h >= 1:
                        keep_out(h - 1)
                    keep(h)
                keep_out(NH - 1)

            def exp_compressed(g):
                a = (g % 2) * 256
                act.wait_ge(i_m, g + 1)
                f(R[:, 2, a + 1:a + 1 + NCS], ps[3][:, 0:NCS], ACT.Exp, scale=SC, bias=st[:, 52:53],
                  accum_out=st[:, 53:54]).then_inc(i_e, 1)

            def exp_rows1(g):
                act.wait_ge(r_m[1], g + 1)
                f(R[:, 0, 0:PAST + TS], R[:, 0, 0:PAST + TS], ACT.Exp, scale=SC, bias=st[:, 56:57], accum_out=st[:, 58:59])
                f(R[:, 1, 0:WIN + TS], R[:, 1, 0:WIN + TS], ACT.Exp, scale=SC, bias=st[:, 57:58],
                  accum_out=st[:, 59:60]).then_inc(r_e[1], 1)

            def keep_k1(b):
                for i in range(0, 6, 2 - b % 2):
                    act.wait_ge(k_p[2], 6 * b + i + 1)
                    if b >= 2:
                        act.wait_ge(k_s[1], 12 * (b // 2 - 1) + 2 * i + 1 + b % 2)
                    copy(KT[:, b % 2, i, :], ps[6 + i % 2][:, :]).then_inc(k_a[2], 1)

            def keep_p1(g):
                for i in range(4):
                    act.wait_ge(r_t[1], 4 * g + i + 1)
                    v = ps[6 + i % 2][:, :].rearrange("p (c n) -> p c n", c=4)
                    if i < 3:
                        last = copy(PT1[:, 4 * i:4 * i + 4, :], v)
                    else:
                        copy(PT1[0:TS, 12:14, :], v[0:TS, 0:2, :])
                        last = copy(PT1[0:NCS, 14, :], v[0:NCS, 2, :])
                    last.then_inc(r_te[1], 1)

            squares(0, x_e)
            project_in(0)
            keep_qk(0, 0, 12)
            prompt0()
            keep_k0(0)
            rows0(0)
            keep_k0(1)
            for step in steps:
                if step[0] == "turn":
                    keep_p0(step[1])
                    if step[1] == 0:
                        rows0(1)
                elif step[0] == "back":
                    keep_o(0, step[1])
                elif step[0] == "c":
                    compress(step[1])
            squares(1, o_e[0])
            ffn(0)
            squares(2, d_e[0])
            project_in(1)
            for t in range(3):
                last = f(gates[0:WT[t], t, :], proj[0:WT[t], t, N1 - 48:N1], ACT.Sigmoid)
            last.then_inc(g_s, 1)
            for j in range(4):
                if j == 2:
                    keep_qk(1, 8, 11)
                act.wait_ge(p_h, j + 1)
                f(hidp[:, j, :], ps[PCMP_BANKS[j]][:, 0:NKV * NCP], ACT.Silu, bias=cb[:, j:j + 1]).then_inc(p_he, 1)
            prompt1()
            keep_k1(0)
            keep_k1(1)
            exp_compressed(0)
            for g in range(4):
                if g < 3:
                    keep_k1(2 * g + 2)
                exp_rows1(g)
                if g < 3:
                    keep_k1(2 * g + 3)
                    exp_compressed(g + 1)
                keep_p1(g)
                if g >= 1:
                    keep_o(1, g - 1)
            keep_o(1, 3)
            squares(3, o_e[1])
            ffn(1)
            for t in range(3):
                for j in range(2):
                    act.wait_ge(y_t, 2 * t + j + 1)
                    if t == 0 and j == 0:
                        act.wait_ge(s_kv, 48 + 16 * 5 + 16 * NB)
                    copy(proj[0:WT[t], t, j * 512:(j + 1) * 512], ps[2 * t + j][0:WT[t], :]).then_inc(y_e, 1)

        @block.vector
        def _(dve):
            v = nc.vector
            chained = [0]

            def link(ins):
                chained[0] += 1
                ins.then_inc(ch, 1)
                dve.wait_ge(ch, chained[0])

            tt, ts = v.tensor_tensor, v.tensor_scalar

            def norm_rows(i):
                dve.wait_ge(n_ps[i], 1)
                link(ts(rt[:, :], ps[7][:, 0:3], EPS, None, ALU.add))
                v.reciprocal(rt[:, :], rt[:, :]).then_inc(n_rc[i], 1)

            def norm_cols(i):
                dve.wait_ge(n_ps[i], 1)
                link(ts(R[:, 3, T:2 * T], ps[7][:, 0:T], EPS, None, ALU.add))
                v.reciprocal(R[:, 3, T:2 * T], R[:, 3, T:2 * T]).then_inc(n_rc[i], 1)
                dve.wait_ge(n_rs[i], 1)

            def norm_rope(l):
                A, B = R[:, 0, 0:512], R[:, 1, 0:512]
                h0 = 0
                for gi, (n, c, H, g) in enumerate(ROPED[l]):
                    pos = IN_ORDER[l].index(n)
                    dve.wait_ge(in_e[l], 3 * (pos + 1))
                    dve.wait_ge(in_q[l], full_chunks(l, pos))
                    for t in range(3):
                        w = WT[t]
                        X = proj[0:w, t, c:c + H * HD]
                        link(tt(A[0:w, 0:H * HD], X, X, ALU.mult))
                        link(v.reduce_sum(ss[0:w, t, h0:h0 + H], A[0:w, 0:H * HD].rearrange("p (h d) -> p h d", h=H), AX))
                    two = ((ss[:, 0:2, h0:h0 + H]), (ss[0:TS, 2, h0:h0 + H]))
                    for x in two:
                        last = ts(x, x, 1.0 / HD, EPS, ALU.mult, ALU.add)
                    link(last)
                    for x in two:
                        last = v.reciprocal(x, x)
                    last.then_inc(q_rc[l], 1)
                    dve.wait_ge(q_rs[l], gi + 1)
                    for t in range(3):
                        w = WT[t]
                        X = proj[0:w, t, c:c + H * HD].rearrange("p (h d) -> p h d", h=H)
                        a = A[0:w, 0:H * HD].rearrange("p (h d) -> p h d", h=H)
                        b = B[0:w, 0:H * HD].rearrange("p (h d) -> p h d", h=H)
                        co, si = C("cos", t * HD, (t + 1) * HD, w), C("sin", t * HD, (t + 1) * HD, w)
                        link(tt(X, X, rep(ss[0:w, t, h0:h0 + H], 2, HD), ALU.mult))
                        link(tt(X, X, rep(gr[0:w, g * HD:(g + 1) * HD], 1, H), ALU.mult))
                        tt(a, X, rep(co, 1, H), ALU.mult)
                        tt(b[:, :, 0:32], X[:, :, 32:64], rep(si[:, 0:32], 1, H), ALU.mult)
                        link(tt(b[:, :, 32:64], X[:, :, 0:32], rep(si[:, 32:64], 1, H), ALU.mult))
                        tt(X, a, b, ALU.add).then_inc(q_d[l], 1)
                        dve.wait_ge(q_d[l], 3 * gi + t + 1)
                    h0 += H

            def prompt0():
                for b in range(2):
                    E = R[:, 2, b * 400:b * 400 + 386]
                    v.memset(E[:, 128:129], 1.0)
                    link(v.memset(E[:, 385:386], 1.0))

                def views(h):
                    b = h % 2
                    return (b,) + tuple(R[:, r, b * 384:b * 384 + 384] for r in (0, 1, 3)) + (R[:, 2, b * 400:b * 400 + 386],)

                def first(h):
                    b, S, K, W, E = views(h)
                    dve.wait_ge(a_s[0], h + 1)
                    dve.wait_ge(a_w[0], h - 1)
                    mx = st[:, 8 * b:8 * b + 2]
                    link(tt(S, ps[b][:, 0:384], C("causal"), ALU.add))
                    v.reduce_max(mx[:, 0:1], S[:, 0:128], AX)
                    link(v.reduce_max(mx[:, 1:2], S[:, 128:384], AX))
                    ts(st[:, 8 * b + 2:8 * b + 4], mx, -SC, None, ALU.mult).then_inc(a_m[0], 1)

                def second(h):
                    b, S, K, W, E = views(h)
                    if h < 8:
                        dve.wait_ge(a_g, h + 1)
                        if h >= 2:
                            dve.wait_ge(a_w[0], h - 1)
                        v.tensor_tensor_scan(E[:, 0:128][:, ::-1], K[:, 0:128][:, ::-1], C("notpast")[:, ::-1], 1.0, ALU.mult, ALU.max)
                        link(v.tensor_tensor_scan(E[:, 257:385][:, ::-1], K[:, 256:384][:, ::-1], C("notpast")[:, ::-1], 1.0,
                                                  ALU.mult, ALU.max))
                        v.tensor_tensor_scan(E[:, 129:257][:, ::-1], K[:, 128:256][:, ::-1], zero.broadcast_to([P, 128]),
                                             E[:, 257:258], ALU.mult, ALU.max)
                        tt(S[:, 0:128], S[:, 0:128], C("strict"), ALU.mult)
                        link(tt(S[:, 256:384], S[:, 256:384], C("strict"), ALU.mult))
                        if h >= 2:
                            dve.wait_ge(a_t[0], h - 1)
                        tt(W[:, 0:128], S[:, 0:128], E[:, 1:129], ALU.mult)
                        tt(W[:, 128:384], S[:, 128:384], E[:, 130:386], ALU.mult).then_inc(a_w[0], 1)
                    else:
                        dve.wait_ge(a_e[0], h - 7)
                        link(v.reciprocal(st[:, 8 * b + 6:8 * b + 8], st[:, 8 * b + 4:8 * b + 6]))
                        dve.wait_ge(a_t[0], h - 1)
                        ts(W[:, 0:128], K[:, 0:128], st[:, 8 * b + 6:8 * b + 7], None, ALU.mult)
                        ts(W[:, 128:384], K[:, 128:384], st[:, 8 * b + 7:8 * b + 8], None, ALU.mult).then_inc(a_w[0], 1)

                for h in range(NH):
                    if 8 <= h + 1 < NH:
                        first(h + 1)
                    second(h)

            def keep_k0(g):
                for cc in range(9 * g, (9, 16)[g]):
                    for p in range(1, 8, 2):
                        i = cc * 8 + p
                        dve.wait_ge(k_p[0], i + 1)
                        if cc >= 2:
                            dve.wait_ge(k_s[0], 8 * (cc - 2) + p + 1)
                        v.tensor_copy(KT[:, cc % 2, p, :], ps[5 + i % 3][:, :]).then_inc(k_d[0], 1)

            def drop_least(vals, n, neg):
                link(v.tensor_reduce(st[:, 42:43], vals, AX, ALU.min))
                link(v.scalar_tensor_tensor(st[:, 60:60 + n], vals, st[:, 42:43], C("rank", 0, n), ALU.is_le, ALU.mult))
                link(v.reduce_max(st[:, 43:44], st[:, 60:60 + n], AX))
                link(ts(neg, st[:, 60:60 + n], st[:, 43:44], NEG, ALU.is_ge, ALU.mult))

            def rows0(g):
                dve.wait_ge(k_s[0], 64 * (g + 1))
                dve.wait_ge(k_n[0], 4 * (g + 1))
                S, E = R[:, 3, :], R[:, 2, :]
                for j in range(2):
                    last = v.reduce_sum(st[:, 48 + 2 * j:50 + 2 * j], ps[2 + j][:, :].rearrange("p (n k) -> p n k", n=2), AX)
                link(last)
                drop_least(st[:, 48:52], 4, st[:, 76:80])
                if g:
                    dve.wait_ge(r_t[0], 6 * g)
                for j in range(4):
                    ts(S[:, j * 256:(j + 1) * 256], ps[2 + j // 2][:, (j % 2) * 256:(j % 2 + 1) * 256], st[:, 76 + j:77 + j],
                       None, ALU.add)
                dve.wait_ge(r_sg, g + 1)
                tt(S[:, PAST:PAST + TS], ps[4][:, 32:64], C("newneg0", g * TS, (g + 1) * TS), ALU.add).then_inc(r_ps[0], 1)
                dve.wait_ge(r_ps[0], g + 1)
                link(v.reduce_max(st[:, 44:45], S[:, 0:PAST + TS], AX))
                ts(st[:, 40:41], st[:, 44:45], -SC, None, ALU.mult).then_inc(r_m[0], 1)
                G, K = R[:, 0, :], R[:, 1, :]
                n = PAST + TS
                v.memset(E[:, n:n + 1], 1.0)
                link(tt(K[:, PAST:n], K[:, PAST:n], C("newnot", g * TS, (g + 1) * TS), ALU.max))
                v.tensor_tensor_scan(E[:, 0:n][:, ::-1], K[:, 0:n][:, ::-1], zero.broadcast_to([P, n]), 1.0, ALU.mult, ALU.max)
                link(tt(G[:, PAST:n], G[:, PAST:n], C("newpast", g * TS, (g + 1) * TS), ALU.mult))
                tt(G[:, 0:n], G[:, 0:n], E[:, 1:n + 1], ALU.mult).then_inc(r_w[0], 1)
                dve.wait_ge(r_e[0], g + 1)
                link(v.reciprocal(st[:, 45:46], st[:, 41:42]))
                ts(S[:, 0:n], S[:, 0:n], st[:, 45:46], None, ALU.mult).then_inc(r_w[0], 1)

            def pick(l, i):
                H = (8, NKV)[l]
                dve.wait_ge(v_c[l], (4 * (i + 1), 2 * (i + 1))[l])
                if i >= 2:
                    dve.wait_ge(v_t[l], i - 1)
                A = R[:, 2, 512:512 + H * HD]
                link(tt(A.rearrange("p (h d) -> p h d", h=H), ps[5][:, 0:H * HD].rearrange("p (h d) -> p h d", h=H),
                        rep(C(f"head{l}"), 2, HD), ALU.mult))
                v.reduce_sum(osm[:, i % 2, :], A.rearrange("p (h d) -> p d h", h=H), AX).then_inc(v_x[l], 1)

            def project_out(l):
                for i in range(KD):
                    dve.wait_ge(o_p[l], i + 1)
                    tt(hT[:, i, :], hT[:, i, :], ps[4 + i % 4][:, 0:T], ALU.add).then_inc(o_e[l], 1)

            def ffn(l):
                norm_cols(2 * l + 1)

                def scale(j, it=0):
                    a, more = (j % 2) * T, 2 * GU_BODY * it
                    dve.wait_ge(u_p[l], more + j + 1)
                    if j >= 2:
                        dve.wait_ge(u_a[l], more + j - 1)
                        dve.wait_ge(u_e[l], more + j - 1)
                    tt(R[:, 0, a:a + T], ps[2 * (j % 3)][:, 0:T], rst, ALU.mult).then_inc(u_g[l], 1)
                    tt(R[:, 2, a:a + T], ps[2 * (j % 3) + 1][:, 0:T], rst, ALU.mult).then_inc(u_u[l], 1)

                for j in range(2 * GU_FIRST):
                    scale(j)
                with dve.Fori(0, GU_ITS) as it:
                    for j in range(2 * GU_FIRST, 2 * (GU_FIRST + GU_BODY)):
                        scale(j, it)
                for i in range(KD):
                    cg, j = i // 2, i % 2
                    dve.wait_ge(d_p[l], 2 * (cg + 1))
                    tt(hT[:, i, :], hT[:, i, :], ps[(cg % 2) * 2 + j][:, 0:T], ALU.add).then_inc(d_e[l], 1)

            def compress(n):
                bb, i = n // 8, n % 8
                if n == 0:
                    dve.wait_ge(c_b, 1)
                    ts(cb[:, :], ps[0][:, 0:4], float(D), None, ALU.mult).then_inc(c_be, 1)
                if bb < NB and i < 4:
                    dve.wait_ge(k_p[1], 8 * bb + 2 * i + 2)
                    if bb >= 2:
                        dve.wait_ge(c_h, 4 * (bb - 1))
                    for e in range(2):
                        for par in range(2):
                            last = v.tensor_copy(KT[par * 64:par * 64 + 64, bb % 2, 2 * i + e, 256:512],
                                                 ps[3][e * 64:e * 64 + 64, par::2])
                    last.then_inc(k_d[1], 1)
                if i == 5 and bb >= 1:
                    dve.wait_ge(c_w, 2 * (bb - 1) + 1)
                    v.tensor_copy(kc[:, bb - 1, :, :], ps[6][:, 0:2 * NCS].rearrange("p (i n) -> p i n", i=2)).then_inc(c_we, 1)
                last_step = n == 8 * (NB + 1) - 1
                if (i == 1 and bb >= 2) or last_step:
                    b = bb - 1 if last_step else bb - 2
                    dve.wait_ge(c_w, 2 * b + 2)
                    v.tensor_copy(vc[0:NCS, b, :], ps[6][0:NCS, P:P + KVW]).then_inc(c_we, 1)

            def prompt1():
                dve.wait_ge(p_w, 1)
                v.tensor_copy(kcp[:, :, :], ps[5][:, 0:NKV * NCP].rearrange("p (h n) -> p h n", h=NKV))
                v.tensor_copy(vcp[0:NCP, :], ps[4][0:NCP, 0:KVW]).then_inc(p_we, 1)
                dve.wait_ge(g_s, 1)
                for t in range(2):
                    gv = gates[:, t, :].rearrange("p (h r) -> p h r", r=3)
                    for j, br in enumerate(GATE_ORDER):
                        if br:
                            last = v.tensor_copy(gp[:, :, 2 * j + t], gv[:, :, br])
                        else:
                            last = ts(gp[:, :, 2 * j + t], gv[:, :, br], C("cmpany", t, t + 1), None, ALU.mult)
                link(last)

                def views(h):
                    W, b = R[:, h % 3, :], 24 * (h % 3)
                    two = W[:, 0:768].rearrange("p (r n) -> p r n", r=2)
                    cm = W[:, 768:798].rearrange("p (t n) -> p t n", t=2)
                    return W, b, ((two[:, :, 0:128], 0, 4, 2), (two[:, :, 128:384], 1, 4, 2), (cm, 4, 6, 1))

                def first(h):
                    W, b, parts = views(h)
                    A, B = ps[2 * (h % 2)], ps[2 * (h % 2) + 1]
                    dve.wait_ge(a_s[1], h + 1)
                    if h >= 3:
                        dve.wait_ge(a_t[1], h - 2)
                    tt(W[:, 0:384], A[:, 0:384], C("causal"), ALU.add)
                    tt(W[:, 384:768], B[:, 0:384], C("causal"), ALU.add)
                    link(tt(W[:, 768:798], A[:, 384:414], C("cmpcausal"), ALU.add))
                    for x, lo, hi, step in parts:
                        last = v.reduce_max(st[:, b + lo:b + hi:step], x, AX)
                    link(last)
                    ts(st[:, b + 6:b + 12], st[:, b:b + 6], -SC, None, ALU.mult).then_inc(a_m[1], 1)

                def second(h):
                    W, b, parts = views(h)
                    dve.wait_ge(a_e[1], h + 1)
                    link(v.reciprocal(st[:, b + 18:b + 24], st[:, b + 12:b + 18]))
                    link(tt(st[:, b + 18:b + 24], st[:, b + 18:b + 24], gp[:, h, :], ALU.mult))
                    for x, lo, hi, step in parts:
                        last = tt(x, x, rep(st[:, b + 18 + lo:b + 18 + hi:step], 2, x.shape[2]), ALU.mult)
                    last.then_inc(a_w[1], 1)

                first(0)
                for h in range(NH):
                    if h + 1 < NH:
                        first(h + 1)
                    second(h)

            def keep_k1(b):
                for i in range(1, 6, 2):
                    dve.wait_ge(k_p[2], 6 * b + i + 1)
                    if b >= 2:
                        dve.wait_ge(k_s[1], 12 * (b // 2 - 1) + 2 * i + 1)
                    v.tensor_copy(KT[:, 0, i, :], ps[7][:, :]).then_inc(k_d[2], 1)

            def cmp_rows(g):
                a = (g % 2) * 256
                pc, pg = R[:, 2, a:a + 64], R[:, 2, a + 128:a + 128 + NCS]
                dve.wait_ge(k_n[1], g + 1)
                if g >= 1:
                    dve.wait_ge(r_w[1], g)
                if g >= 2:
                    dve.wait_ge(r_t[1], 4 * (g - 1))
                v.memset(pc[:, 0:1], 0.0)
                link(v.reduce_max(st[:, 48:49], ps[3][:, 0:NCS], AX))
                ts(st[:, 52:53], st[:, 48:49], -SC, None, ALU.mult).then_inc(i_m, 1)
                dve.wait_ge(i_e, g + 1)
                link(v.reciprocal(st[:, 54:55], st[:, 53:54]))
                ts(pc[:, 1:64], pc[:, 1:64], st[:, 54:55], None, ALU.mult).then_inc(i_w, 1)
                dve.wait_ge(i_w, g + 1)
                link(ts(pg, pc[:, 1:64], gs[:, g, 0:1], None, ALU.mult))

            def select(g):
                dve.wait_ge(i_p, g + 1)
                link(v.reduce_sum(st[:, 0:16], ps[4][:, 0:64].rearrange("p (j c) -> p j c", c=4), AX))
                link(tt(st[:, 16:30], st[:, 1:15], ps[4][:, 8:61:4], ALU.add))
                v.memset(st[:, 76:77], 0.0)
                v.memset(st[:, 91:92], 0.0).then_inc(i_r, 1)
                drop_least(st[:, 16:30], 14, st[:, 77:91])

            def rows1(g):
                dve.wait_ge(k_s[1], 12 * (g + 1))
                if g:
                    dve.wait_ge(r_t[1], 4 * g)
                S, W = R[:, 0, :], R[:, 1, :]
                for j in range(2):
                    tt(S[:, j * 512:(j + 1) * 512].rearrange("p (n k) -> p n k", n=8),
                       ps[j][:, :].rearrange("p (n k) -> p n k", n=8), rep(st[:, 76 + 8 * j:84 + 8 * j], 2, HD), ALU.add)
                new = C("newneg1", g * TS, (g + 1) * TS)
                tt(S[:, PAST:PAST + TS], ps[3][:, 64:96], new, ALU.add)
                tt(W[:, 0:NQ], ps[2][:, 0:NQ], C("winneg"), ALU.add)
                v.tensor_copy(W[:, NQ:WIN], ps[2][:, NQ:WIN])
                tt(W[:, WIN:WIN + TS], ps[3][:, 96:128], new, ALU.add).then_inc(r_ps[1], 1)
                dve.wait_ge(r_ps[1], g + 1)
                v.reduce_max(st[:, 48:49], S[:, 0:PAST + TS], AX)
                link(v.reduce_max(st[:, 49:50], W[:, 0:WIN + TS], AX))
                ts(st[:, 56:58], st[:, 48:50], -SC, None, ALU.mult).then_inc(r_m[1], 1)
                dve.wait_ge(r_e[1], g + 1)
                link(v.reciprocal(st[:, 48:50], st[:, 58:60]))
                link(tt(st[:, 48:50], st[:, 48:50], gs[:, g, 1:3], ALU.mult))
                ts(S[:, 0:PAST + TS], S[:, 0:PAST + TS], st[:, 48:49], None, ALU.mult)
                ts(W[:, 0:WIN + TS], W[:, 0:WIN + TS], st[:, 49:50], None, ALU.mult).then_inc(r_w[1], 1)

            dve.wait_ge(s_first, 32)
            dve.wait_ge(x_e, 6)
            for k in range(KD):
                ts(xT[:, k, :], hT[:, k, :], gc[:, k:k + 1], None, ALU.mult).then_inc(n_x[0], 1)
            norm_rows(0)
            dve.wait_ge(s_const, 64)
            norm_rope(0)
            prompt0()
            keep_k0(0)
            rows0(0)
            keep_k0(1)
            rows0(1)
            for step in steps:
                if step[0] == "pick":
                    pick(0, step[1])
                elif step[0] == "c":
                    compress(step[1])
            project_out(0)
            ffn(0)
            norm_rows(2)
            norm_rope(1)
            prompt1()
            dve.wait_ge(g_l, 64)
            keep_k1(0)
            cmp_rows(0)
            select(0)
            for g in range(4):
                if g < 3:
                    keep_k1(2 * g + 2)
                rows1(g)
                if g >= 1:
                    pick(1, g - 1)
                if g < 3:
                    cmp_rows(g + 1)
                    select(g + 1)
            pick(1, 3)
            project_out(1)
            ffn(1)

        @block.gpsimd
        def _(pool):
            flat_state = state_win[0].rearrange("b w two h d -> b w (two h d)")
            flat_win = win_sample[0].rearrange("b w two h d -> b w (two h d)")
            pool.memset(pq[:], 0.0).then_inc(qb_z[0], 1)

            def spread(l):
                for i, n in enumerate(IN_ORDER[l]):
                    if nin[l][n] == 512:
                        full = full_chunks(l, i)
                        pool.wait_ge(in_e[l], 3 * (i + 1))
                        for j in range(4):
                            last = nc.gpsimd.tensor_copy(proj[0:TS, 2, n * 512 + j * P:n * 512 + (j + 1) * P],
                                                         smp[32 * j:32 * j + 32, full % 2, :])
                        last.then_inc(in_q[l], 1)

            def scale_by_gain(i, dst, ready):
                for k in range(KD):
                    pool.wait_ge(ready, k + 1)
                    nc.gpsimd.tensor_scalar(dst[:, k, :], hT[:, k, :], gc[:, i * KD + k:i * KD + k + 1], None,
                                            ALU.mult).then_inc(n_x[i], 1)

            def gate_up(l):
                with pool.Fori(0, FT // 2) as it:
                    for j in range(2):
                        a = j * T
                        pool.wait_ge(u_a[l], 2 * it + j + 1)
                        pool.wait_ge(u_u[l], 2 * it + j + 1)
                        nc.gpsimd.tensor_tensor(big[:, bass.ds(2 * T * it + a, T)], R[:, 1, a:a + T], R[:, 2, a:a + T],
                                                ALU.mult).then_inc(u_e[l], 1)

            spread(0)
            pool.wait_ge(q_d[0], 6)
            pool.wait_ge(in_e[0], 3 * len(nin[0]))
            pool.wait_ge(in_q[0], full_chunks(0, 5))
            kv = kv0_prompt[0, 0].rearrange("(t p) two h d -> t p (two h d)", p=P)
            for t in range(2):
                pool.dma_start(kv[t], proj[:, t, D:N0]).then_inc(s_kv, 16)
            pool.dma_start(kv0_sample[0].rearrange("b q two h d -> (b q) (two h d)"), proj[0:TS, 2, D:N0]).then_inc(s_kv, 16)
            pool.wait_ge(t_e[0], 12)
            pool.wait_ge(qb_z[0], 1)
            for p in range(8):
                for e in range(2):
                    h = 2 * (p % 4) + e
                    last = nc.gpsimd.tensor_copy(qb0[e * 64:e * 64 + 64, :, p, h * NQ:(h + 1) * NQ],
                                                 qT[e * 64:e * 64 + 64, p, TP:T].rearrange("p (b q) -> p b q", q=NQ))
            last.then_inc(qb_d[0], 1)
            for b in range(NB):
                pool.dma_start(flat_win[b, 0:WIN - NQ, :], flat_state[b, NQ:WIN, :]).then_inc(s_out, 16)
            pool.wait_ge(s_const, 64)
            pool.wait_ge(s_w1, 80)
            n_ch = 0
            for i in range(16):
                for k in range(2):
                    acc, e = pew[:, k * CH:(k + 1) * CH], pec[:, k * 16 + i:k * 16 + i + 1]
                    if i == 0:
                        nc.gpsimd.tensor_scalar(acc, w1r(k, i), e, None, ALU.mult).then_inc(pch, 1)
                        n_ch += 1
                        continue
                    pool.wait_ge(pch, n_ch)
                    nc.gpsimd.tensor_scalar(smp_t[:, 0:CH], w1r(k, i), e, None, ALU.mult).then_inc(pch, 1)
                    pool.wait_ge(pch, n_ch + 1)
                    nc.gpsimd.tensor_tensor(acc, acc, smp_t[:, 0:CH], ALU.add).then_inc(c_a if (i, k) == (15, 1) else pch, 1)
                    n_ch += 2
            scale_by_gain(1, x2T, o_e[0])
            gate_up(0)
            scale_by_gain(2, xT, d_e[0])
            nc.gpsimd.memset(pq[:, 0:1024], 0.0).then_inc(qb_z[1], 1)
            spread(1)
            pool.wait_ge(q_d[1], 15)
            pool.wait_ge(in_e[1], 3 * len(nin[1]))
            pool.wait_ge(in_q[1], full_chunks(1, 5))
            for t in range(2):
                rows = slice(t * P, (t + 1) * P)
                pool.dma_start(kv1_prompt[0, 0, rows].rearrange("p k h d -> p (k h d)"), proj[:, t, NQ1:NQ1 + 4 * KVW]).then_inc(s_kv, 16)
                pool.dma_start(win_prompt[0, 0, rows].rearrange("p k h d -> p (k h d)"), proj[:, t, NQ1 + 4 * KVW:NQ1 + 6 * KVW]).then_inc(s_kv, 16)
            pool.dma_start(kv1_sample[0].rearrange("b q k h d -> (b q) (k h d)"), proj[0:TS, 2, NQ1:NQ1 + 4 * KVW]).then_inc(s_kv, 16)
            for b in range(NB):
                pool.dma_start(flat_win[b, WIN - NQ:WIN, :], proj[b * NQ:(b + 1) * NQ, 2, NQ1 + 4 * KVW:NQ1 + 6 * KVW]).then_inc(s_kv, 16)
            pool.wait_ge(g_s, 1)
            for b in range(NB):
                pool.dma_start(gate_scratch[b].rearrange("h q r -> q h r"),
                               gates[b * NQ:(b + 1) * NQ, 2, :].rearrange("q (h r) -> q h r", r=3)).then_inc(g_d, 16)
            pool.wait_ge(g_d, 16 * NB)
            rows = gate_scratch.rearrange("b h q r -> (b h q) r")
            for g in range(4):
                pool.dma_start(gs[:, g, :], rows[g * P:(g + 1) * P, :]).then_inc(g_l, 16)
            pool.wait_ge(t_e[1], 11)
            pool.wait_ge(qb_z[1], 1)
            for h in range(NH):
                kvh = h // 4
                kp, e, s = kvh // 2, kvh % 2, h % 2
                last = nc.gpsimd.tensor_copy(qb1[e * 64:e * 64 + 64, :, kp, h * NQ:(h + 1) * NQ],
                                             qT[s * 64:s * 64 + 64, h // 2, TP:T].rearrange("p (b q) -> p b q", q=NQ))
            last.then_inc(qb_d[1], 1)
            pool.wait_ge(s_page, 16)
            for i, (name, _, _) in enumerate(ringed):
                if name[0] not in ("k1", "v1"):
                    continue
                _, freed, value = ringed[i - SLOTS]
                pool.wait_ge(freed, value)
                for dst, (c, b, pg, part) in page_jobs1(ring[:, i % SLOTS, :], *name)[NPG // 2:]:
                    pool.dma_start(dst, c[page(pool, b, pg), :, part, :].rearrange("g s n -> (g s) n")).then_inc(s_half[i % SLOTS], 16)
            scale_by_gain(3, x2T, o_e[1])
            gate_up(1)
            yp = y_prompt[0].rearrange("(t p) d -> t p d", p=P)
            for t in range(2):
                pool.wait_ge(y_e, 2 * t + 2)
                pool.dma_start(yp[t], proj[:, t, 0:D]).then_inc(s_out, 16)
            pool.wait_ge(y_e, 6)
            pool.dma_start(y_sample.rearrange("b q d -> (b q) d"), proj[0:TS, 2, 0:D]).then_inc(s_out, 16)
            pool.wait_ge(s_out, 16 * (NB + 3))
            pool.wait_ge(s_kv, 48 + 16 * 5 + 16 * NB)


_OUTS = [(1, TP, D), (NB, NQ, D), (1, 1, TP, 2, NH, HD), (1, NB, NQ, 2, NH, HD), (1, 1, TP, 4, NKV, HD),
         (1, NB, NQ, 4, NKV, HD), (1, 1, TP, 2, NKV, HD), (1, NB, WIN, 2, NKV, HD)]
_INS = ["x_prompt", "x_sample", "cache_kv0", "cache_kv1", "state_win", "page_table", "w_in0", "w_out0", "w_in1",
        "w_out1", "cmp_w1", "cmp_w2", "w_gu", "w_down"]


def kernel(**inputs):
    import concourse.bacc as _bacc
    from concourse.bass_utils import run_bass_kernel_spmd as _run

    nc = _bacc.Bacc("TRN2", target_bir_lowering=False, num_devices=1)
    table, off = constants()
    arrays = {n: np.ascontiguousarray(inputs[n]) for n in _INS}
    arrays["consts"] = table
    g = [inputs["g_mix0"][0], inputs["g_ffn"][0], inputs["g_mix1"][0], inputs["g_ffn"][1]]
    arrays["gcol"] = np.ascontiguousarray(np.concatenate([np.asarray(a).reshape(KD, P).T for a in g], 1))
    r = [inputs["g_q0"][0], inputs["g_k0"][0], inputs["g_q1"][0]] + [inputs["g_k1"][0, i] for i in range(3)]
    arrays["grow"] = np.ascontiguousarray(np.broadcast_to(np.concatenate([np.asarray(a) for a in r])[None, :], (P, 6 * HD)))
    pe = np.asarray(inputs["cmp_pe"])[0].reshape(2, 16, P)
    arrays["pecol"] = np.ascontiguousarray(pe.transpose(2, 0, 1).reshape(P, 32))
    args = [nc.dram_tensor("in_" + n, a.shape, mybir.dt.from_np(a.dtype), kind="ExternalInput").ap() for n, a in arrays.items()]
    args += [nc.dram_tensor(f"out_{i}", s, F32, kind="ExternalOutput").ap() for i, s in enumerate(_OUTS)]
    args.append(nc.dram_tensor("gate_scratch", (NB, NH, NQ, 3), F32, kind="Internal").ap())
    trunk(nc, off, *args)
    res = _run(nc, [{"in_" + n: a for n, a in arrays.items()}], core_ids=[0])
    return tuple(res.results[0][f"out_{i}"] for i in range(len(_OUTS)))
```
